# Optimizing a Trainium2 kernel written in Bass

```python
import math
import jax, jax.numpy as jnp
from jax import lax
import numpy as np

D_MODEL = 1024
BATCH = 1
SEQ = 1024
DEPTH = 1
DEC_BATCH = 8
DEC_SEQ = 4
PAST_LEN = 2048
PAGE_SIZE = 128

RWKV_HEAD_DIM = 64
RWKV_HEADS = D_MODEL // RWKV_HEAD_DIM
RWKV_WIDTH = RWKV_HEADS * RWKV_HEAD_DIM
DECAY_LORA = 64
AAA_LORA = 64
GATE_LORA = 128
LNX_EPS = 64e-5
RWKV_COLS = 3 * RWKV_WIDTH + DECAY_LORA + AAA_LORA + GATE_LORA

ATTN_HEAD_DIM = 64
HEADS_PER_GROUP = 4
WINDOWS = (128, 512, 2048)
DILATIONS = (1, 4, 16)
N_GROUPS = len(WINDOWS)
ATTN_WIDTH = N_GROUPS * HEADS_PER_GROUP * ATTN_HEAD_DIM
ATTN_OUT_WIDTH = HEADS_PER_GROUP * ATTN_HEAD_DIM
ATTN_SCALE = ATTN_HEAD_DIM ** -0.5
BLOCK = 128
NEG = -1e30

D_FF = 4 * D_MODEL
PLE_DIM = 256
NORM_EPS = 1e-6
IN_COLS = RWKV_COLS + 3 * ATTN_WIDTH + 2 * D_MODEL

kernel_name = "rwkv7_dilated_swa_hybrid_step"

def rmsnorm(x, g):
    xf = x.astype(jnp.float32)
    xf = xf * lax.rsqrt(jnp.mean(xf * xf, axis=-1, keepdims=True) + NORM_EPS)
    return (xf * g.astype(jnp.float32)).astype(x.dtype)

def wkv_scan(r, w, k, v, a, b, s0):
    xs = tuple(jnp.moveaxis(t.astype(jnp.float32), 1, 0) for t in (r, w, k, v, a, b))

    def step(s, inp):
        r_t, w_t, k_t, v_t, a_t, b_t = inp
        sa = jnp.einsum('nhvk,nhk->nhv', s, a_t)
        s = s * w_t[:, :, None, :] + sa[..., None] * b_t[:, :, None, :] + v_t[..., None] * k_t[:, :, None, :]
        return s, jnp.einsum('nhvk,nhk->nhv', s, r_t)

    s_T, ys = lax.scan(step, s0.astype(jnp.float32), xs)
    return jnp.moveaxis(ys, 0, 1), s_T

def rwkv_branch(z, z_prev, wkv0, shift_mu, decay_w0, decay_w2, aaa_a0, aaa_a2, gate_g2,
                k_k, k_a, r_k, lnx_w, lnx_b):
    N, T, _ = z.shape
    prev = jnp.concatenate([z_prev[:, None].astype(z.dtype), z[:, :-1]], axis=1)
    zs = z + (prev - z) * shift_mu
    r, k, v, xw, xa, xg = jnp.split(
        zs, [RWKV_WIDTH, 2 * RWKV_WIDTH, 3 * RWKV_WIDTH,
             3 * RWKV_WIDTH + DECAY_LORA, 3 * RWKV_WIDTH + DECAY_LORA + AAA_LORA], axis=-1)
    logw = -jax.nn.softplus(-(decay_w0 + jnp.tanh(xw) @ decay_w2)) - 0.5
    decay = jnp.exp(-jnp.exp(logw.astype(jnp.float32)))
    a = jax.nn.sigmoid(aaa_a0 + xa @ aaa_a2)
    g = jax.nn.sigmoid(xg) @ gate_g2

    def heads(t):
        return t.reshape(N, T, RWKV_HEADS, RWKV_HEAD_DIM)

    kk = heads(k * k_k).astype(jnp.float32)
    kk = kk / jnp.maximum(jnp.sqrt(jnp.sum(kk * kk, axis=-1, keepdims=True)), 1e-12)
    k = k * (1 + (a - 1) * k_a)
    r_h, k_h, v_h, a_h, w_h = heads(r), heads(k), heads(v), heads(a), heads(decay)
    y, s_T = wkv_scan(r_h, w_h, k_h, v_h, -kk, kk * a_h.astype(jnp.float32), wkv0)
    mu = jnp.mean(y, axis=-1, keepdims=True)
    var = jnp.mean(jnp.square(y - mu), axis=-1, keepdims=True)
    y = ((y - mu) * lax.rsqrt(var + LNX_EPS)).reshape(N, T, RWKV_WIDTH)
    y = y * lnx_w.astype(jnp.float32) + lnx_b.astype(jnp.float32)
    bonus = jnp.sum((r_h * k_h * r_k).astype(jnp.float32), axis=-1, keepdims=True) * v_h.astype(jnp.float32)
    out = ((y + bonus.reshape(N, T, RWKV_WIDTH)) * g.astype(jnp.float32)).astype(z.dtype)
    return out, s_T.astype(z.dtype), z[:, -1]

def dilated_attn_prompt(q, k, v, dilation, n_back):
    N, T, H, Dh = q.shape
    span = dilation * BLOCK
    Tp = -(-T // span) * span
    S = Tp // dilation
    nb = S // BLOCK

    def to_blocks(t):
        t = jnp.pad(t, ((0, 0), (0, Tp - T), (0, 0), (0, 0)))
        t = t.reshape(N, S, dilation, H, Dh).transpose(0, 2, 1, 3, 4)
        return t.reshape(N, dilation, nb, BLOCK, H, Dh).astype(jnp.float32)

    def with_prev(t):
        prev = jnp.pad(t[:, :, :-1], ((0, 0), (0, 0), (1, 0), (0, 0), (0, 0), (0, 0)))
        return jnp.concatenate([prev, t], axis=3)

    qb = to_blocks(q)
    kb = with_prev(to_blocks(k))
    vb = with_prev(to_blocks(v))
    s = jnp.einsum('ndbqhe,ndbkhe->ndbhqk', qb, kb) * ATTN_SCALE
    qi = jnp.arange(BLOCK)[:, None]
    ki = jnp.arange(2 * BLOCK)[None, :]
    dist = qi + BLOCK - ki
    band = (dist >= 0) & (dist <= n_back)
    has_prev = (jnp.arange(nb)[:, None, None] > 0) | (ki >= BLOCK)[None]
    mask = band[None] & has_prev
    s = jnp.where(mask[None, None, :, None], s, NEG)
    m = jnp.max(s, axis=-1, keepdims=True)
    e = jnp.exp(s - m)
    den = jnp.sum(e, axis=-1, keepdims=True)
    o = jnp.einsum('ndbhqk,ndbkhe->ndbqhe', e / den, vb)
    lse = (m + jnp.log(den))[..., 0].transpose(0, 1, 2, 4, 3)

    def from_blocks(t):
        rest = t.shape[4:]
        t = t.reshape(N, dilation, S, *rest).swapaxes(1, 2)
        return t.reshape(N, Tp, *rest)[:, :T]

    return from_blocks(o), from_blocks(lse)

def dilated_attn_sample(q, k, v, kv_cache, dilation, n_back):
    N, T = q.shape[:2]
    L = kv_cache.shape[1]
    keys = jnp.concatenate([kv_cache[:, :, 0], k], axis=1)
    vals = jnp.concatenate([kv_cache[:, :, 1], v], axis=1)
    idx = L + jnp.arange(T)[:, None] - dilation * jnp.arange(n_back + 1)[None, :]
    valid = idx >= 0
    idx = jnp.maximum(idx, 0)
    kg = keys[:, idx].astype(jnp.float32)
    vg = vals[:, idx].astype(jnp.float32)
    s = jnp.einsum('nthe,ntjhe->nthj', q.astype(jnp.float32), kg) * ATTN_SCALE
    s = jnp.where(valid[None, :, None, :], s, NEG)
    m = jnp.max(s, axis=-1, keepdims=True)
    e = jnp.exp(s - m)
    den = jnp.sum(e, axis=-1, keepdims=True)
    o = jnp.einsum('nthj,ntjhe->nthe', e / den, vg)
    return o, (m + jnp.log(den))[..., 0]

def decoder_layer(x, p, wkv0, shift0, kv_caches, prm):
    (norm_mix, w_in, shift_mu, decay_w0, decay_w2, aaa_a0, aaa_a2, gate_g2, k_k, k_a, r_k,
     lnx_w, lnx_b, w_branch_rwkv, w_branch_attn, w_out, norm_mlp, w_ff1, w_ff2,
     norm_ple, w_ple, w_ple_gate) = prm
    N, T, _ = x.shape
    h = rmsnorm(x, norm_mix)
    z = h @ w_in
    z_rwkv, z_q, z_k, z_v, z_gate = jnp.split(
        z, [RWKV_COLS, RWKV_COLS + ATTN_WIDTH, RWKV_COLS + 2 * ATTN_WIDTH,
            RWKV_COLS + 3 * ATTN_WIDTH], axis=-1)

    rwkv_out, wkv_T, shift_T = rwkv_branch(z_rwkv, shift0, wkv0, shift_mu, decay_w0, decay_w2,
                                           aaa_a0, aaa_a2, gate_g2, k_k, k_a, r_k, lnx_w, lnx_b)

    gshape = (N, T, N_GROUPS, HEADS_PER_GROUP, ATTN_HEAD_DIM)
    q, k, v = z_q.reshape(gshape), z_k.reshape(gshape), z_v.reshape(gshape)
    outs, lses, new_kv = [], [], []
    for gi in range(N_GROUPS):
        d = DILATIONS[gi]
        n_back = WINDOWS[gi] // d
        qg, kg, vg = q[:, :, gi], k[:, :, gi], v[:, :, gi]
        if kv_caches is None:
            o, l = dilated_attn_prompt(qg, kg, vg, d, n_back)
            keep = min(WINDOWS[gi], T)
            new_kv.append(jnp.stack([kg[:, T - keep:], vg[:, T - keep:]], axis=2))
        else:
            o, l = dilated_attn_sample(qg, kg, vg, kv_caches[gi], d, n_back)
            new_kv.append(jnp.stack([kg, vg], axis=2))
        outs.append(o)
        lses.append(l)
    alpha = jax.nn.softmax(jnp.stack(lses, axis=2), axis=2)
    attn = jnp.einsum('ntgh,ntghe->nthe', alpha, jnp.stack(outs, axis=2))
    attn = attn.reshape(N, T, ATTN_OUT_WIDTH).astype(x.dtype)

    gates = jax.nn.sigmoid(z_gate)
    mixed = gates[..., :D_MODEL] * (rwkv_out @ w_branch_rwkv) + gates[..., D_MODEL:] * (attn @ w_branch_attn)
    x = x + mixed @ w_out

    h = rmsnorm(x, norm_mlp)
    x = x + jnp.square(jax.nn.relu(h @ w_ff1)) @ w_ff2

    h = rmsnorm(x, norm_ple)
    x = x + jax.nn.sigmoid(h @ w_ple_gate) * (p @ w_ple)
    return x, new_kv, wkv_T, shift_T

def setup_inputs(seed: int = 0) -> dict:
    key = jax.random.key(seed)
    ks = iter(jax.random.split(key, 48))
    f32 = jnp.float32

    def nrm(shape, scale=1.0):
        return jax.random.normal(next(ks), shape, f32) * scale

    def gain(shape):
        return 1.0 + 0.05 * jax.random.normal(next(ks), shape, f32)

    cl = [min(w, PAST_LEN) for w in WINDOWS]
    kvs = (HEADS_PER_GROUP, ATTN_HEAD_DIM)
    return {
        "x_prompt": nrm((BATCH, SEQ, D_MODEL)),
        "x_sample": nrm((DEC_BATCH, DEC_SEQ, D_MODEL)),
        "cache_kv_g0": nrm((DEPTH, DEC_BATCH, cl[0], 2) + kvs),
        "cache_kv_g1": nrm((DEPTH, DEC_BATCH, cl[1], 2) + kvs),
        "cache_kv_g2": nrm((DEPTH, DEC_BATCH, cl[2], 2) + kvs),
        "state_wkv": nrm((DEPTH, DEC_BATCH, RWKV_HEADS, RWKV_HEAD_DIM, RWKV_HEAD_DIM), 0.5),
        "state_shift": nrm((DEPTH, DEC_BATCH, RWKV_COLS)),
        "p_prompt": nrm((DEPTH, BATCH, SEQ, PLE_DIM)),
        "p_sample": nrm((DEPTH, DEC_BATCH, DEC_SEQ, PLE_DIM)),
        "norm_mix": gain((DEPTH, D_MODEL)),
        "w_in": nrm((DEPTH, D_MODEL, IN_COLS), D_MODEL ** -0.5),
        "shift_mu": jax.random.uniform(next(ks), (DEPTH, RWKV_COLS), f32),
        "decay_w0": jax.random.uniform(next(ks), (DEPTH, RWKV_WIDTH), f32, -6.0, -1.0),
        "decay_w2": nrm((DEPTH, DECAY_LORA, RWKV_WIDTH), 0.1),
        "aaa_a0": nrm((DEPTH, RWKV_WIDTH), 0.5),
        "aaa_a2": nrm((DEPTH, AAA_LORA, RWKV_WIDTH), 0.1),
        "gate_g2": nrm((DEPTH, GATE_LORA, RWKV_WIDTH), GATE_LORA ** -0.5),
        "k_k": 0.85 + 0.05 * jax.random.normal(next(ks), (DEPTH, RWKV_WIDTH), f32),
        "k_a": gain((DEPTH, RWKV_WIDTH)),
        "r_k": nrm((DEPTH, RWKV_HEADS, RWKV_HEAD_DIM), 0.1),
        "lnx_w": gain((DEPTH, RWKV_WIDTH)),
        "lnx_b": nrm((DEPTH, RWKV_WIDTH), 0.01),
        "w_branch_rwkv": nrm((DEPTH, RWKV_WIDTH, D_MODEL), RWKV_WIDTH ** -0.5),
        "w_branch_attn": nrm((DEPTH, ATTN_OUT_WIDTH, D_MODEL), ATTN_OUT_WIDTH ** -0.5),
        "w_out": nrm((DEPTH, D_MODEL, D_MODEL), D_MODEL ** -0.5),
        "norm_mlp": gain((DEPTH, D_MODEL)),
        "w_ff1": nrm((DEPTH, D_MODEL, D_FF), D_MODEL ** -0.5),
        "w_ff2": nrm((DEPTH, D_FF, D_MODEL), D_FF ** -0.5),
        "norm_ple": gain((DEPTH, D_MODEL)),
        "w_ple": nrm((DEPTH, PLE_DIM, D_MODEL), PLE_DIM ** -0.5),
        "w_ple_gate": nrm((DEPTH, D_MODEL, D_MODEL), D_MODEL ** -0.5),
        "norm_final": gain((D_MODEL,)),
    }

def reference(x_prompt, x_sample, cache_kv_g0, cache_kv_g1, cache_kv_g2, state_wkv, state_shift,
              p_prompt, p_sample, norm_mix, w_in, shift_mu, decay_w0, decay_w2, aaa_a0, aaa_a2,
              gate_g2, k_k, k_a, r_k, lnx_w, lnx_b, w_branch_rwkv, w_branch_attn, w_out,
              norm_mlp, w_ff1, w_ff2, norm_ple, w_ple, w_ple_gate, norm_final):
    yp, ys = x_prompt, x_sample
    nb_p = x_prompt.shape[0]
    kvp = [[], [], []]
    kvs = [[], [], []]
    wkv_p, sh_p, wkv_s, sh_s = [], [], [], []
    for i in range(DEPTH):
        prm = (norm_mix[i], w_in[i], shift_mu[i], decay_w0[i], decay_w2[i], aaa_a0[i], aaa_a2[i],
               gate_g2[i], k_k[i], k_a[i], r_k[i], lnx_w[i], lnx_b[i], w_branch_rwkv[i],
               w_branch_attn[i], w_out[i], norm_mlp[i], w_ff1[i], w_ff2[i], norm_ple[i],
               w_ple[i], w_ple_gate[i])
        wkv0 = jnp.zeros((nb_p, RWKV_HEADS, RWKV_HEAD_DIM, RWKV_HEAD_DIM), x_prompt.dtype)
        shift0 = jnp.zeros((nb_p, RWKV_COLS), x_prompt.dtype)
        yp, nkv_p, w_p, s_p = decoder_layer(yp, p_prompt[i], wkv0, shift0, None, prm)
        ys, nkv_s, w_s, s_s = decoder_layer(
            ys, p_sample[i], state_wkv[i], state_shift[i],
            (cache_kv_g0[i], cache_kv_g1[i], cache_kv_g2[i]), prm)
        for gi in range(N_GROUPS):
            kvp[gi].append(nkv_p[gi])
            kvs[gi].append(nkv_s[gi])
        wkv_p.append(w_p)
        sh_p.append(s_p)
        wkv_s.append(w_s)
        sh_s.append(s_s)
    y_prompt = rmsnorm(yp, norm_final)
    y_sample = rmsnorm(ys, norm_final)
    return (y_prompt, y_sample,
            jnp.stack(kvp[0]), jnp.stack(kvp[1]), jnp.stack(kvp[2]),
            jnp.stack(wkv_p), jnp.stack(sh_p),
            jnp.stack(kvs[0]), jnp.stack(kvs[1]), jnp.stack(kvs[2]),
            jnp.stack(wkv_s), jnp.stack(sh_s))


_drawn_inputs = setup_inputs


def setup_inputs(seed=0):
    import zlib

    import numpy as np

    out = dict(_drawn_inputs(seed))
    spreads = {}
    factors = {'lnx_w': 4.447,
     'lnx_b': 30.925,
     'norm_ple': 25.567,
     'cache_kv_g0': 3.169,
     'cache_kv_g1': 3.264,
     'cache_kv_g2': 3.233}
    for name, (base, spread) in spreads.items():
        noise = np.random.default_rng([zlib.crc32(name.encode()), seed]).standard_normal(out[name].shape)
        drawn = base * np.exp(spread * noise) if base else spread * noise
        out[name] = __import__('jax').numpy.asarray(drawn.astype(out[name].dtype))
    for name, factor in factors.items():
        out[name] = (out[name] * factor).astype(out[name].dtype)
    return out
```

```python
import concourse.bass as bass
from concourse import mybir
from contextlib import ExitStack

F32 = mybir.dt.float32
ACT = mybir.ActivationFunctionType
ALU = mybir.AluOpType
AXX = mybir.AxisListType.X

P = 128
D = 1024
KT = D // P
SEQ = 1024
DB, DS = 8, 4
NS = DB * DS
T = SEQ + NS
NT = 3
TT = T // NT
HD = 64
PAIRS = 8
RT = 26
GROUPS, HPG = 3, 4
DIL = (1, 4, 16)
STEP = (1, 4, 8)
AW = HPG * HD
BL = 128
NB = SEQ // BL
C = 64
QC = 4
QUADS = SEQ // (C * QC)
QT = QC * C
LEVELS = 6
SLEVELS = 2
FFQ = 4
EPS, LNX_EPS = 1e-6, 64e-5
DECAY = 0.6065306597126334
NEG = -1e30
NCACHE = 128
SK = NCACHE + DS
STG = AW + 2 * HPG

VEC = {}
_at = 0
for _n, _w in (("norm_mix", KT), ("norm_mlp", KT), ("norm_ple", KT), ("norm_final", KT), ("shift_mu", RT),
               ("decay_w0", KT), ("aaa_a0", KT), ("k_k", KT), ("k_a", KT), ("r_k", KT), ("lnx_w", KT), ("lnx_b", KT)):
    VEC[_n] = _at
    _at += _w
NVEC = _at

def _columns(widths):
    out, at = {}, 0
    for n, w in widths:
        out[n] = (at, at + w)
        at += w
    return out, at


CST, NCST = _columns([("ident", P), ("ident2", HD), ("ones", P), ("ones2", P), ("gram", P), ("gram_s", P), ("level", LEVELS * HD),
                      ("reset", T), ("tok8", DB)])
ATT, NATT = _columns([("band", 2 * BL), ("pairs", BL), ("place", 2 * NS * 32), ("fresh", GROUPS * SK), ("own8", DB)])
WPAIR = 3 * KT * P + 2 * P
WMIX = (3 * KT + 2) * P
WQK, WKV = 3 * KT * P, KT * P + KT * AW
WPLE = (KT + 2) * P


class Steps:

    def __init__(self, sem, names, ahead=1):
        self.sem, self.names, self.at, self.ahead = sem, list(names), 0, ahead
        assert len(set(self.names)) == len(self.names)

    def begin(self, eng):
        eng.sem_inc(self.sem, self.ahead * len(self.names))

    def done(self, name, ins):
        assert self.names[self.at % len(self.names)] == name, (name, self.names[self.at % len(self.names)])
        self.at += 1
        ins.then_inc(self.sem, 1)

    def wait(self, eng, name, turn):
        eng.wait_ge(self.sem, turn * len(self.names) + (self.ahead * len(self.names) + self.names.index(name) + 1))


def thirds(tile):
    return tile.rearrange("p (n c) -> p n c", n=NT)


def product(nc, acc, w, x, kt, width=None):
    for k in range(kt):
        for n in range(NT):
            last = nc.tensor.matmul(acc[:, n, 0:TT], w[:, k, :], x[:, k, n * TT:(n + 1) * TT], start=k == 0, stop=k == kt - 1)
    return last


def load_all(nc, sem, pairs):
    with nc.Block() as block:
        @block.sync
        def _(sp):
            for n, (dst, src) in enumerate(pairs):
                sp.dma_start(dst, src).then_inc(sem, 16)
            sp.wait_ge(sem, 16 * len(pairs))


def rms_norm(nc, name, x, gain, cst, out, psum, ctx_outer, store=None):
    ones = cst[:, CST["ones"][0]:CST["ones"][1]]
    with ExitStack() as ctx:
        sq = ctx.enter_context(nc.sbuf_tensor(f"{name}_sq", [P, 2, T], F32))
        rinv = ctx.enter_context(nc.sbuf_tensor(f"{name}_rinv", [P, T], F32))
        squared = ctx_outer.enter_context(nc.semaphore(f"{name}_squared"))
        summed = ctx_outer.enter_context(nc.semaphore(f"{name}_summed"))
        root_in = ctx_outer.enter_context(nc.semaphore(f"{name}_root_in"))
        root = ctx_outer.enter_context(nc.semaphore(f"{name}_root"))
        normed = ctx_outer.enter_context(nc.semaphore(f"{name}_normed"))
        stored = ctx_outer.enter_context(nc.semaphore(f"{name}_stored"))
        with nc.Block() as block:
            @block.scalar
            def _(act):
                for k in range(KT):
                    if k >= 2:
                        act.wait_ge(summed, k - 1)
                    nc.scalar.activation(sq[:, k % 2, :], x[:, k, :], ACT.Square).then_inc(squared, 1)
                act.wait_ge(root_in, 2)
                nc.scalar.activation(rinv[:, :], rinv[:, :], ACT.Sqrt).then_inc(root, 1)

            @block.tensor
            def _(pe):
                for k in range(KT):
                    pe.wait_ge(squared, k + 1)
                    for n in range(NT):
                        last = nc.tensor.matmul(psum[:, n, 0:TT], ones, sq[:, k % 2, n * TT:(n + 1) * TT], start=k == 0, stop=k == KT - 1)
                    last.then_inc(summed, 1)

            @block.vector
            def _(vec):
                vec.wait_ge(summed, KT)
                nc.vector.tensor_scalar(thirds(rinv[:, :]), psum[:, 0:NT, 0:TT], 1.0 / D, EPS, ALU.mult, ALU.add).then_inc(root_in, 1)
                vec.wait_ge(root_in, 1)
                nc.vector.reciprocal(rinv[:, :], rinv[:, :]).then_inc(root_in, 1)
                vec.wait_ge(root, 1)
                for k in range(KT):
                    nc.vector.scalar_tensor_tensor(out[:, k, :], x[:, k, :], gain[:, k:k + 1], rinv[:, :], ALU.mult, ALU.mult).then_inc(normed, 1)

            if store is not None:
                @block.sync
                def _(sp):
                    for k in range(KT):
                        sp.wait_ge(normed, k + 1)
                        sp.dma_start(store[:, k, :], out[:, k, :]).then_inc(stored, 16)
                    sp.wait_ge(stored, 16 * KT)


def dilated(tile, g, first, n, blocks=None):
    if g == 0:
        return tile[:, bass.ds(first * BL, n)]
    rows = tile.rearrange("p (i r) -> p r i", r=STEP[g])
    lo = blocks * BL if g == 1 else 0
    return rows[:, bass.ds(first, 1), lo:lo + n].rearrange("p a b -> p (a b)")


def attention_projection(nc, top, g, hT, w_qk, w_kv, psum, qT, kT, vtok, vnew, k_out, v_out):
    with ExitStack() as ctx:
        wa = ctx.enter_context(nc.sbuf_tensor(f"wa{g}", [P, WQK], F32))
        wb = ctx.enter_context(nc.sbuf_tensor(f"wb{g}", [P, WKV], F32))
        sem = lambda n: top.enter_context(nc.semaphore(f"{n}{g}"))
        wa_in, wb_in, full, evac, v_full, v_evac, stored = (sem(n) for n in ("wa_in", "wb_in", "qk_full", "qk_evac", "v_full", "v_evac", "kv_stored"))
        with nc.Block() as block:
            @block.sync
            def _(sp):
                sp.dma_start(wa[:, :], w_qk).then_inc(wa_in, 16)
                sp.dma_start(wb[:, :], w_kv).then_inc(wb_in, 16)
                sp.wait_ge(evac, 4)
                sp.dma_start(k_out, kT[:, :, :]).then_inc(stored, 16)
                sp.wait_ge(v_evac, NB + 1)
                sp.dma_start(v_out, vtok[:, :, :]).then_inc(stored, 16)
                sp.wait_ge(stored, 32)

            @block.tensor
            def _(pe):
                wk = wa[:, :].rearrange("p (k c) -> p k c", k=KT)
                wk1 = wb[:, 0:KT * P].rearrange("p (k c) -> p k c", k=KT)
                wv = wb[:, KT * P:].rearrange("p (k c) -> p k c", k=KT)
                pe.wait_ge(wa_in, 16)
                for i in range(4):
                    if i >= 2:
                        pe.wait_ge(evac, i - 1)
                    if i == 3:
                        pe.wait_ge(wb_in, 16)
                    w = wk[:, :, i * P:(i + 1) * P] if i < 3 else wk1
                    product(nc, psum[:, 3 * (i % 2):3 * (i % 2) + 3, :], w, hT, KT).then_inc(full, 1)
                for b in range(NB + 1):
                    if b >= 2:
                        pe.wait_ge(v_evac, b - 1)
                    for k in range(KT):
                        if b == NB:
                            rows, toks = NS, hT[:, k, SEQ:T]
                        else:
                            rows = BL
                            toks = dilated(hT[:, k, 0:SEQ], g, (b, b // 2, b)[g], BL, b % 2)
                        last = nc.tensor.matmul(psum[0:rows, 6 + b % 2, 0:AW], toks, wv[:, k, :], start=k == 0, stop=k == KT - 1)
                    last.then_inc(v_full, 1)

            @block.scalar
            def _(act):
                for i in range(4):
                    act.wait_ge(full, i + 1)
                    dst = (qT if i < 2 else kT)[:, i % 2, :]
                    nc.scalar.activation(thirds(dst), psum[:, 3 * (i % 2):3 * (i % 2) + 3, 0:TT], ACT.Copy, scale=HD ** -0.5 if i < 2 else 1.0).then_inc(evac, 1)

            @block.vector
            def _(vec):
                for b in range(NB + 1):
                    vec.wait_ge(v_full, b + 1)
                    dst, rows = (vnew[:, g, :], NS) if b == NB else (vtok[:, b, :], BL)
                    nc.vector.tensor_copy(dst, psum[0:rows, 6 + b % 2, 0:AW]).then_inc(v_evac, 1)


def attention_prompt(nc, top, g, psum, qT, kT, vtok, att, ident, scratch):
    with ExitStack() as ctx:
        sb = lambda n, *s: ctx.enter_context(nc.sbuf_tensor(f"{n}{g}", [P, *s], F32))
        qz = sb("qz", 2, 2, BL)
        sc, ex, pt = sb("sc", HPG, 2 * BL), sb("ex", HPG, 2 * BL), sb("pt", HPG, 2, BL)
        stage = sb("stage", STG)
        S = psum[:, 0:2, :].rearrange("p n (h k) -> p (n h) k", h=2)
        PT = psum[:, 2:4, :].rearrange("p n (h b k) -> p (n h) b k", h=2, b=2)
        O = psum[:, 4, 0:AW]
        st = lambda n, names: Steps(top.enter_context(nc.semaphore(f"{n}{g}")), names)
        zero = top.enter_context(nc.semaphore(f"att_zero{g}"))
        stored = top.enter_context(nc.semaphore(f"att_stored{g}"))
        pool_s = st("att_pool", ["q0", "q1"])
        pe_s = st("att_pe", ["scores", "pt", "pv"])
        vec_s = st("att_vec", ["mask", "max", "o"])
        act_s = st("att_act", ["e0", "e1", "e2", "e3", "pt"])

        def turns(eng, unit):
            if g == 0:
                unit(0, 0, False)
                with eng.Fori(1, NB) as b:
                    unit(b, b, True)
            elif g == 1:
                with eng.Fori(0, DIL[1]) as r:
                    unit(2 * r, r, False)
                    unit(2 * r + 1, r, True)
            else:
                with eng.Fori(0, NB) as b:
                    unit(b, b, False)

        with nc.Block() as block:
            @block.gpsimd
            def _(pool):
                pool_s.begin(pool)
                pool.wait_ge(zero, 1)

                def unit(t, f, both):
                    pe_s.wait(pool, "scores", t - 1)
                    for h in range(2):
                        rows = slice(h * HD, (h + 1) * HD)
                        src = qT[rows, :, 0:SEQ]
                        if g == 0:
                            src = src[:, :, bass.ds(f * BL, BL)]
                            dst = qz[rows, :, h, :]
                        elif g == 1:
                            src = src.rearrange("p a (i r) -> p a r i", r=STEP[1])[:, :, bass.ds(f, 1), (BL if both else 0):(2 * BL if both else BL)].rearrange("p a o i -> p a (o i)")
                            dst = qz[rows, :, h, :]
                        else:
                            src = src.rearrange("p a (i r) -> p a r i", r=STEP[2])[:, :, bass.ds(f, 1), :].rearrange("p a o i -> p a (o i)")
                            dst = qz[rows, :, h, :]
                        pool_s.done(f"q{h}", nc.gpsimd.tensor_copy(dst, src))
                turns(pool, unit)

            @block.tensor
            def _(pe):
                pe_s.begin(pe)

                def unit(t, f, both):
                    nk = 2 * BL if both else BL
                    pool_s.wait(pe, "q1", t)
                    vec_s.wait(pe, "mask", t - 1)
                    for h in range(HPG):
                        if g == 0:
                            keys = dilated(kT[:, h // 2, 0:SEQ], 0, f - 1 if both else f, nk)
                        elif g == 1:
                            keys = dilated(kT[:, h // 2, 0:SEQ], 1, f, nk, 0)
                        else:
                            keys = dilated(kT[:, h // 2, 0:SEQ], 2, f, nk)
                        last = nc.tensor.matmul(S[:, h, 0:nk], qz[:, h // 2, h % 2, :], keys, start=True, stop=True)
                    pe_s.done("scores", last)
                    act_s.wait(pe, "e3", t)
                    for h in range(HPG):
                        for b in range(nk // BL):
                            last = nc.tensor.transpose(PT[:, h, b, :], ex[:, h, b * BL:(b + 1) * BL], ident)
                    pe_s.done("pt", last)
                    act_s.wait(pe, "pt", t)
                    vec_s.wait(pe, "o", t - 1)
                    for h in range(HPG):
                        for b in range(nk // BL):
                            blk = (t - 1 + b) if both else t
                            v = vtok[:, bass.ds(blk, 1), h * HD:(h + 1) * HD].rearrange("p o c -> p (o c)")
                            last = nc.tensor.matmul(O[:, h * HD:(h + 1) * HD], pt[:, h, b, :], v, start=b == 0, stop=b == nk // BL - 1)
                    pe_s.done("pv", last)
                turns(pe, unit)

            @block.vector
            def _(vec):
                vec_s.begin(vec)
                nc.vector.memset(qz[:, :, :, :], 0.0).then_inc(zero, 1)

                def unit(t, f, both):
                    nk = 2 * BL if both else BL
                    m = att("pairs") if g == 2 else att("band")[:, 2 * BL - nk:]
                    pe_s.wait(vec, "scores", t)
                    act_s.wait(vec, "e3", t - 1)
                    vec_s.done("mask", nc.vector.tensor_tensor(sc[:, :, 0:nk], S[:, :, 0:nk], m[:, None, :].to_broadcast([P, HPG, nk]), ALU.add))
                    vec_s.wait(vec, "mask", t)
                    vec.wait_ge(stored, 16 * t)
                    vec_s.done("max", nc.vector.tensor_reduce(stage[:, AW:AW + HPG], sc[:, :, 0:nk], AXX, ALU.max, negate=True))
                    pe_s.wait(vec, "pv", t)
                    vec_s.done("o", nc.vector.tensor_copy(stage[:, 0:AW], O))
                turns(vec, unit)

            @block.scalar
            def _(act):
                act_s.begin(act)

                def unit(t, f, both):
                    nk = 2 * BL if both else BL
                    vec_s.wait(act, "max", t)
                    pe_s.wait(act, "pt", t - 1)
                    for h in range(HPG):
                        act_s.done(f"e{h}", nc.scalar.activation(ex[:, h, 0:nk], sc[:, h, 0:nk], ACT.Exp, bias=stage[:, AW + h:AW + h + 1], accum_out=stage[:, AW + HPG + h:AW + HPG + h + 1]))
                    pe_s.wait(act, "pt", t)
                    act_s.done("pt", nc.scalar.activation(pt[:, :, 0:nk // BL, :], PT[:, :, 0:nk // BL, :], ACT.Copy))
                turns(act, unit)

            @block.sync
            def _(sp):
                rows = scratch.rearrange("(i r) c -> r i c", r=STEP[g])

                def unit(t, f, both):
                    vec_s.wait(sp, "o", t)
                    act_s.wait(sp, "e3", t)
                    if g == 0:
                        dst = scratch[bass.ds(f * BL, BL), g * STG:(g + 1) * STG]
                    elif g == 1:
                        dst = rows[bass.ds(f, 1), (BL if both else 0):(2 * BL if both else BL), g * STG:(g + 1) * STG].rearrange("o i c -> (o i) c")
                    else:
                        dst = rows[bass.ds(f, 1), :, g * STG:(g + 1) * STG].rearrange("o i c -> (o i) c")
                    sp.dma_start(dst, stage[:, :]).then_inc(stored, 16)
                turns(sp, unit)
                sp.wait_ge(stored, 16 * NB)


def sample_scores(nc, top, g, psum, qT, kT, att, kc, scores):
    tt = 1 if g == 0 else DS
    with ExitStack() as ctx:
        K = ctx.enter_context(nc.sbuf_tensor(f"sk{g}", [P, 2, DB, tt, SK], F32))
        Q = ctx.enter_context(nc.sbuf_tensor(f"sq{g}", [P, 2, NS, 32], F32))
        sem = lambda n: top.enter_context(nc.semaphore(f"samp_{n}{g}"))
        k_in, k_new, q_up, full, done = (sem(n) for n in ("k_in", "k_new", "q_up", "full", "done"))
        with nc.Block() as block:
            @block.sync
            def _(sp):
                for hp in range(2):
                    sp.dma_start(K[:, hp, :, :, 0:NCACHE], kc[:, hp, :, :, :]).then_inc(k_in, 16)

            @block.gpsimd
            def _(pool):
                for hp in range(2):
                    src = kT[:, hp, SEQ:T].rearrange("p (b t) -> p b t", b=DB)[:, :, None, :].to_broadcast([P, DB, tt, DS])
                    nc.gpsimd.tensor_copy(K[:, hp, :, :, NCACHE:SK], src).then_inc(k_new, 1)

            @block.vector
            def _(vec):
                place = att("place").rearrange("p (a t c) -> p a t c", a=2, t=NS)
                for hp in range(2):
                    nc.vector.tensor_tensor(Q[:, hp, :, :], qT[:, hp, SEQ:T][:, :, None].to_broadcast([P, NS, 32]), place[:, hp, :, :], ALU.mult).then_inc(q_up, 1)
                vec.wait_ge(full, 1)
                nc.vector.tensor_tensor(scores[:, g, :], psum[:, 0, 0:SK], att("fresh")[:, g * SK:(g + 1) * SK], ALU.add).then_inc(done, 1)

            @block.tensor
            def _(pe):
                pe.wait_ge(k_in, 32)
                pe.wait_ge(k_new, 2)
                pe.wait_ge(q_up, 2)
                for b in range(DB):
                    for t in range(DS):
                        for hp in range(2):
                            last = nc.tensor.matmul(psum[32 * (b // 2):32 * (b // 2) + 32, 0, 0:SK], Q[:, hp, DS * b + t, :], K[:, hp, b, t % tt, :],
                                                    start=b % 2 == 0 and t == 0 and hp == 0, stop=b % 2 == 1 and t == DS - 1 and hp == 1)
                last.then_inc(full, 1)


def sample_attention(nc, top, psum, att, ident, scores, vnew, vc, attn):
    with ExitStack() as ctx:
        sb = lambda n, s: ctx.enter_context(nc.sbuf_tensor(n, s, F32))
        V = [sb(f"sv{g}", [P, DB, 1 if g == 0 else DS, AW]) for g in range(GROUPS)]
        stat = sb("sa_stat", [P, 4])
        pn = sb("sa_new", [P, GROUPS, DB, DS])
        pct = sb("sa_pct", [P, GROUPS, P])
        pnt = sb("sa_pnt", [NS, GROUPS, P])
        sem = lambda n: top.enter_context(nc.semaphore(f"sa_{n}"))
        v_in, chain, exped, turned, copied, summed, placed = (sem(n) for n in ("v_in", "chain", "exped", "turned", "copied", "summed", "placed"))
        flat = scores[:, :, :].rearrange("p g k -> p (g k)")
        with nc.Block() as block:
            @block.sync
            def _(sp):
                for g in range(GROUPS):
                    sp.dma_start(V[g][:, :, :, :], vc[g]).then_inc(v_in, 16)

            @block.vector
            def _(vec):
                nc.vector.tensor_reduce(stat[:, 0:1], flat, AXX, ALU.max, negate=True).then_inc(chain, 1)
                vec.wait_ge(exped, 1)
                nc.vector.reciprocal(stat[:, 2:3], stat[:, 1:2]).then_inc(chain, 1)
                vec.wait_ge(chain, 2)
                nc.vector.tensor_scalar(flat, flat, stat[:, 2:3], None, ALU.mult).then_inc(chain, 1)
                vec.wait_ge(chain, 3)
                for g in range(GROUPS):
                    nc.vector.tensor_tensor(pn[:, g, :, :], scores[:, g, NCACHE:SK][:, None, :].to_broadcast([P, DB, DS]), att("own8")[:, :, None].to_broadcast([P, DB, DS]), ALU.mult).then_inc(chain, 1)
                vec.wait_ge(turned, 1)
                nc.vector.tensor_copy(pct[:, :, :], psum[:, 0, 0:GROUPS * P].rearrange("p (g r) -> p g r", g=GROUPS)).then_inc(copied, 1)
                nc.vector.tensor_copy(pnt[:, :, :], psum[0:NS, 1, 0:GROUPS * P].rearrange("p (g r) -> p g r", g=GROUPS)).then_inc(copied, 1)

            @block.scalar
            def _(act):
                act.wait_ge(chain, 1)
                nc.scalar.activation(flat, flat, ACT.Exp, bias=stat[:, 0:1], accum_out=stat[:, 1:2]).then_inc(exped, 1)
                act.wait_ge(summed, 1)
                for hp in range(2):
                    for h in range(2):
                        rows = slice(h * HD, (h + 1) * HD)
                        src = psum[rows, 2 + hp, 0:P].rearrange("p (n h) -> p h n", h=HPG)[:, 2 * hp + h, :]
                        nc.scalar.activation(attn[rows, hp, SEQ:T], src, ACT.Copy).then_inc(placed, 1)

            @block.tensor
            def _(pe):
                pe.wait_ge(chain, 6)
                for g in range(GROUPS):
                    nc.tensor.transpose(psum[:, 0, g * P:(g + 1) * P], scores[:, g, 0:NCACHE], ident)
                    last = nc.tensor.transpose(psum[0:NS, 1, g * P:(g + 1) * P], pn[:, g, :, :], ident)
                last.then_inc(turned, 1)
                pe.wait_ge(copied, 2)
                pe.wait_ge(v_in, 16 * GROUPS)
                for hp in range(2):
                    for g in range(GROUPS):
                        nc.tensor.matmul(psum[:, 2 + hp, 0:P], vnew[:, g, hp * P:(hp + 1) * P], pnt[:, g, :], start=g == 0, stop=False)
                    for b in range(DB):
                        rows = psum[:, 2 + hp, 16 * b:16 * b + 16].rearrange("p (t h) -> p t h", h=HPG)[:, :, 2 * hp:2 * hp + 2]
                        probs = pct[:, 0, 16 * b:16 * b + 16].rearrange("p (t h) -> p t h", h=HPG)[:, :, 2 * hp:2 * hp + 2]
                        nc.tensor.matmul(rows, V[0][:, b, 0, hp * P:(hp + 1) * P], probs, start=False, stop=False)
                        for g in (1, 2):
                            for t in range(DS):
                                r0 = HPG * (DS * b + t) + 2 * hp
                                last = nc.tensor.matmul(psum[:, 2 + hp, r0:r0 + 2], V[g][:, b, t, hp * P:(hp + 1) * P], pct[:, g, r0:r0 + 2],
                                                        start=False, stop=b == DB - 1 and g == 2 and t == DS - 1)
                last.then_inc(summed, 1)


def combine_groups(nc, top, psum, ident, scratch, attn):
    with ExitStack() as ctx:
        sb = lambda n, *s: ctx.enter_context(nc.sbuf_tensor(n, [P, *s], F32))
        rows = sb("cg_rows", GROUPS, STG)
        w, nmin, den, out = sb("cg_w", GROUPS, HPG), sb("cg_min", HPG), sb("cg_den", HPG), sb("cg_out", AW)
        wd = sb("cg_wd", GROUPS, HPG)
        loaded = top.enter_context(nc.semaphore("cg_loaded"))
        vec_s = Steps(top.enter_context(nc.semaphore("cg_vec")), ["min0", "min1", "gap", "wd", "den", "rden", "wn", "mul", "sum"])
        act_s = Steps(top.enter_context(nc.semaphore("cg_act")), ["exp", "out"])
        pe_s = Steps(top.enter_context(nc.semaphore("cg_pe")), ["turn"])
        with nc.Block() as block:
            @block.sync
            def _(sp):
                with sp.Fori(0, NB) as n:
                    vec_s.wait(sp, "sum", n - 1)
                    sp.dma_start(rows[:, :, :].rearrange("p g c -> p (g c)"), scratch[bass.ds(n * BL, BL), :]).then_inc(loaded, 16)

            @block.vector
            def _(vec):
                vec_s.begin(vec)
                nm = rows[:, :, AW:AW + HPG]
                with vec.Fori(0, NB) as n:
                    vec.wait_ge(loaded, 16 * n + 16)
                    vec_s.done("min0", nc.vector.tensor_tensor(nmin[:, :], nm[:, 0, :], nm[:, 1, :], ALU.min))
                    vec_s.wait(vec, "min0", n)
                    vec_s.done("min1", nc.vector.tensor_tensor(nmin[:, :], nmin[:, :], nm[:, 2, :], ALU.min))
                    vec_s.wait(vec, "min1", n)
                    vec_s.done("gap", nc.vector.tensor_tensor(w[:, :, :], nmin[:, None, :].to_broadcast([P, GROUPS, HPG]), nm, ALU.subtract))
                    act_s.wait(vec, "exp", n)
                    vec_s.done("wd", nc.vector.tensor_tensor(wd[:, :, :], w[:, :, :], rows[:, :, AW + HPG:STG], ALU.mult))
                    vec_s.wait(vec, "wd", n)
                    vec_s.done("den", nc.vector.tensor_reduce(den[:, :], wd[:, :, :].rearrange("p g h -> p h g"), AXX, ALU.add))
                    vec_s.wait(vec, "den", n)
                    vec_s.done("rden", nc.vector.reciprocal(den[:, :], den[:, :]))
                    vec_s.wait(vec, "rden", n)
                    vec_s.done("wn", nc.vector.tensor_tensor(w[:, :, :], w[:, :, :], den[:, None, :].to_broadcast([P, GROUPS, HPG]), ALU.mult))
                    vec_s.wait(vec, "wn", n)
                    for g in range(GROUPS):
                        vals = rows[:, g, 0:AW].rearrange("p (h e) -> p h e", h=HPG)
                        last = nc.vector.tensor_tensor(vals, vals, w[:, g, :][:, :, None].to_broadcast([P, HPG, HD]), ALU.mult)
                    vec_s.done("mul", last)
                    vec_s.wait(vec, "mul", n)
                    pe_s.wait(vec, "turn", n - 1)
                    vec_s.done("sum", nc.vector.tensor_reduce(out[:, :], rows[:, :, 0:AW].rearrange("p g c -> p c g"), AXX, ALU.add))

            @block.scalar
            def _(act):
                act_s.begin(act)
                with act.Fori(0, NB) as n:
                    vec_s.wait(act, "gap", n)
                    act_s.done("exp", nc.scalar.activation(w[:, :, :], w[:, :, :], ACT.Exp))
                    pe_s.wait(act, "turn", n)
                    act_s.done("out", nc.scalar.activation(attn[:, :, bass.ds(n * BL, BL)], psum[:, 0, 0:2 * BL].rearrange("p (a t) -> p a t", a=2), ACT.Copy))

            @block.tensor
            def _(pe):
                pe_s.begin(pe)
                with pe.Fori(0, NB) as n:
                    vec_s.wait(pe, "sum", n)
                    act_s.wait(pe, "out", n - 1)
                    for hp in range(2):
                        last = nc.tensor.transpose(psum[:, 0, hp * BL:(hp + 1) * BL], out[:, hp * P:(hp + 1) * P], ident)
                    pe_s.done("turn", last)


def rwkv_lora_inputs(nc, top, hT, w_lora, shift0, vec_sb, mu1, cst, psum, low, shift_sb):
    with ExitStack() as ctx:
        sb = lambda n, s: ctx.enter_context(nc.sbuf_tensor(n, s, F32))
        w = sb("lora_w", [P, KT, 2 * P])
        raw = sb("lora_raw", [P, 2, 1 + T])
        part = sb("lora_part", [P, 2, T])
        sem = lambda n: top.enter_context(nc.semaphore(n))
        loaded, full, evac, lerp, kept, zero, done = (sem(f"lora_{n}") for n in ("loaded", "full", "evac", "lerp", "kept", "zero", "done"))
        with nc.Block() as block:
            @block.sync
            def _(sp):
                sp.dma_start(w[:, :, :], w_lora).then_inc(loaded, 16)

            @block.tensor
            def _(pe):
                pe.wait_ge(loaded, 16)
                for i in range(2):
                    product(nc, psum[:, 3 * i:3 * i + 3, :], w[:, :, i * P:(i + 1) * P], hT, KT).then_inc(full, 1)

            @block.scalar
            def _(act):
                for i in range(2):
                    acc = psum[:, 3 * i:3 * i + 3, 0:TT]
                    act.wait_ge(full, i + 1)
                    nc.scalar.activation(thirds(raw[:, i, 1:1 + T]), acc, ACT.Copy).then_inc(evac, 1)
                    nc.scalar.activation(thirds(part[:, i, :]), acc, ACT.Copy, scale=mu1[:, 24 + i:25 + i]).then_inc(evac, 1)
                act.wait_ge(lerp, 2)
                nc.scalar.activation(low[0:HD, 0, :], low[0:HD, 0, :], ACT.Tanh).then_inc(done, 1)
                act.wait_ge(lerp, 4)
                nc.scalar.activation(low[:, 1, :], low[:, 1, :], ACT.Sigmoid).then_inc(done, 1)

            @block.gpsimd
            def _(pool):
                for i in range(2):
                    pool.wait_ge(evac, 2 * i + 1)
                    nc.gpsimd.tensor_copy(shift_sb[:, 24 + i, 0:1], raw[:, i, SEQ:SEQ + 1]).then_inc(kept, 1)
                    nc.gpsimd.tensor_copy(shift_sb[:, 24 + i, 1:9], raw[:, i, SEQ + DS:1 + T:DS]).then_inc(kept, 1)

            @block.vector
            def _(vec):
                nc.vector.memset(raw[:, :, 0:1], 0.0).then_inc(zero, 1)
                vec.wait_ge(zero, 1)
                for i in range(2):
                    mu = vec_sb[:, VEC["shift_mu"] + 24 + i:VEC["shift_mu"] + 25 + i]
                    vec.wait_ge(evac, 2 * i + 2)
                    nc.vector.scalar_tensor_tensor(low[:, i, :], raw[:, i, 0:T], mu, part[:, i, :], ALU.mult, ALU.add).then_inc(lerp, 1)
                    vec.wait_ge(lerp, 2 * i + 1)
                    nc.vector.scalar_tensor_tensor(low[:, i, SEQ:T:DS], shift0[:, 24 + i, :], mu, part[:, i, SEQ:T:DS], ALU.mult, ALU.add).then_inc(lerp, 1)


def rwkv_pairs(nc, top, hT, w_pair, shift0, s0T, vec_sb, mu1, ka1, cst, psum, low, shift_sb, out, wkv_p, wkv_s):
    with ExitStack() as ctx:
        sb = lambda n, *s: ctx.enter_context(nc.sbuf_tensor(n, [P, *s], F32))
        w = sb("pair_w", WPAIR)
        raw0, raw1, part0, part1 = sb("raw0", 1 + T), sb("raw1", 1 + T), sb("part0", T), sb("part1", T)
        zr, zk, zv, sg, cs, pp, pr, av, kkn = (sb(n, T) for n in ("zr", "zk", "zv", "sg", "cs", "pp", "pr", "av", "kkn"))
        H = [sb("H0", QC, P), sb("H1", QC, P)]
        BK = sb("BK", QC, 3, C)
        KB = sb("KB", QC, 2, C)
        LT = sb("LT", QC, P)
        RB = sb("RB", QC, 2, C)
        Gs, Gd, X, XT, XTd = sb("Gs", QC, C), sb("Gd", QC, P), sb("X", QC, C), sb("XT", QC, C), sb("XTd", QC, P)
        Vd, SV, UV = sb("Vd", QC, 2, C), sb("SV", QC, 2, C), sb("UV", QC, 2, C)
        rhs, SP, PC = sb("rhs", QC, C), sb("SP", C), sb("PC", QC)
        SVs, UVx, Rx = sb("SVs", 2, DB, HD), sb("UVx", 2, DB, HD), sb("Rx", DB, HD)
        ident, ident2 = cst("ident"), cst("ident2")
        ones2, gram, gram_s, reset = cst("ones2"), cst("gram"), cst("gram_s"), cst("reset")
        level = cst("level").rearrange("p (l c) -> p l c", l=LEVELS)
        tok8 = cst("tok8")
        half = (slice(0, HD), slice(HD, P))
        accA, accB = psum[:, 0:3, :], psum[:, 3:6, :]
        bank = lambda i: psum[:, i, :]
        G = [bank(0).rearrange("p (c t) -> p c t", c=QC), bank(1).rearrange("p (c t) -> p c t", c=QC)]
        TK = [bank(2).rearrange("p (c t) -> p c t", c=QC), bank(3).rearrange("p (c t) -> p c t", c=QC)]
        VT = bank(4).rearrange("p (c t) -> p c t", c=QC)
        inv = [bank(i)[:, 0:QT].rearrange("p (c t) -> p c t", c=QC) for i in (5, 6, 7)]
        Y = bank(4)[:, 0:QT].rearrange("p (c t) -> p c t", c=QC)
        RH, UU, SS = inv

        n_sem = [0]

        def steps(name, names):
            n_sem[0] += 1
            return Steps(top.enter_context(nc.semaphore(name)), names)

        zero = top.enter_context(nc.semaphore("rwkv_zero"))
        w_in = top.enter_context(nc.semaphore("pair_w_in"))
        s0_in = top.enter_context(nc.semaphore("s0_in"))
        s_out = top.enter_context(nc.semaphore("wkv_out"))
        pe_p = steps("pe_pair", ["r", "k", "v", "decay", "aaa", "ksum"])
        act_p = steps("act_pair", ["raw_r", "part_r", "raw_k", "part_k", "raw_v", "part_v", "sig_w", "sig_a", "ksq", "rn", "pr", "pp", "pi"])
        vec_p = steps("vec_pair", ["lerp_r", "fix_r", "lerp_k", "fix_k", "lerp_v", "fix_v", "s_zero0", "s_zero1", "cum", "before", "nmax", "nrec", "kkn", "t1", "bb", "kmod", "rkk"])
        pool_p = steps("pool_pair", ["keep_r", "keep_r8", "keep_k", "keep_k8", "keep_v", "keep_v8"])
        lv = range(LEVELS)
        inv_pe = lambda levels: [f"{m}{i}" for i in range(levels) for m in ("G", "W", "WT") if not (m == "W" and i == levels - 1)]
        pe_q = steps("pe_quad", ["gram0", "gram1", "tk", "vt", *inv_pe(LEVELS), *[f"{m}{c}" for c in range(QC) for m in ("rhs", "u", "s", "y")]])
        vec_q = steps("vec_quad", ["r0", "r1", "a0", "a1", "pc", "m0", "m1", "l0", "l1", "rb0", "rb1",
                                   *[x for i in lv for x in ([f"g{i}", f"x{i}", f"xt{i}"] if i < LEVELS - 1 else [f"g{i}", f"xt{i}"])],
                                   *[f"{m}{c}" for c in range(QC) for m in ("rhs", "u0", "s0", "s1")]])
        act_q = steps("act_quad", ["vd", "kb0", "kb1", "sv0", "sv1", "uv0", "uv1",
                                   *[x for i in lv for x in (f"gd0_{i}", f"gd1_{i}", f"xd0_{i}", f"xd1_{i}")],
                                   *[f"{m}{c}" for c in range(QC) for m in ("sp0", "sp1", "u1_")], "y"])
        pool_q = steps("pool_quad", ["b", "k"])
        pe_s = steps("pe_samp", ["gram0", "gram1", "tk", "vt", *inv_pe(SLEVELS), "rhs", "u", "s", "y"])
        vec_s = steps("vec_samp", ["r0", "r1", "a0", "a1", "m0", "m1", "l0", "l1", "rb0", "rb1",
                                   *[x for i in range(SLEVELS) for x in ([f"g{i}", f"x{i}", f"xt{i}"] if i < SLEVELS - 1 else [f"g{i}", f"xt{i}"])],
                                   "sel", "rhs", "u0", "ux0", "ux1", "s0", "s1", "dec"])
        act_s = steps("act_samp", ["vd", "kb0", "kb1", "sv0", "sv1", "uv0", "uv1",
                                   *[x for i in range(SLEVELS) for x in (f"gd0_{i}", f"gd1_{i}", f"xd0_{i}", f"xd1_{i}")],
                                   "u1", "y"])
        pool_s = steps("pool_samp", ["b", "k"])
        pe_o = steps("pe_post", ["bonus", "mean", "var", "gate"])
        vec_o = steps("vec_post", ["bon", "yc", "vv", "vr", "yn", "yl", "yb", "out"])
        act_o = steps("act_post", ["sq", "rs"])
        all_steps = {"pe": [pe_p, pe_q, pe_s, pe_o], "act": [act_p, act_q, act_s, act_o], "vec": [vec_p, vec_q, vec_s, vec_o], "pool": [pool_p, pool_q, pool_s]}

        def col(name, j):
            return vec_sb[:, bass.ds(VEC[name] + j, 1)]

        def quad_cols(tile, q):
            return tile[:, bass.ds(q * QT, QT)].rearrange("p (c t) -> p c t", c=QC)

        with nc.Block() as block:
            @block.sync
            def _(sp):
                with sp.Fori(0, PAIRS) as j:
                    pe_o.wait(sp, "gate", j - 1)
                    sp.dma_start(w[:, :], w_pair[bass.ds(j, 1), :, :].rearrange("o p c -> p (o c)")).then_inc(w_in, 16)
                    vec_s.wait(sp, "s1", j - 1)
                    pe_s.wait(sp, "y", j - 1)
                    for h in range(2):
                        sp.dma_start(SVs[half[h], h, :, :], s0T[bass.ds(j, 1), half[h], :, :].rearrange("o p b v -> p (o b) v")).then_inc(s0_in, 16)
                    vec_q.wait(sp, f"s1{QC - 1}", j * QUADS + (QUADS - 1))
                    for h in range(2):
                        sp.dma_start(wkv_p[bass.ds(j, 1), half[h], :].rearrange("o p v -> p (o v)"), SV[half[h], 0, h, :]).then_inc(s_out, 16)
                    vec_s.wait(sp, "dec", j)
                    sp.dma_start(wkv_s[bass.ds(j, 1), :, :, :].rearrange("o p b v -> p (o b) v"), Rx[:, :, :]).then_inc(s_out, 16)
                sp.wait_ge(s_out, 48 * PAIRS)

            @block.gpsimd
            def _(pool):
                for s in all_steps["pool"]:
                    s.begin(pool)
                with pool.Fori(0, PAIRS) as j:
                    for n, (z, raw) in enumerate((("r", raw0), ("k", raw1), ("v", raw0))):
                        act_p.wait(pool, f"raw_{z}", j)
                        pool_p.done(f"keep_{z}", nc.gpsimd.tensor_copy(shift_sb[:, bass.ds(j + n * KT, 1), 0:1].rearrange("p a b -> p (a b)"), raw[:, SEQ:SEQ + 1]))
                        pool_p.done(f"keep_{z}8", nc.gpsimd.tensor_copy(shift_sb[:, bass.ds(j + n * KT, 1), 1:9].rearrange("p a b -> p (a b)"), raw[:, SEQ + DS:1 + T:DS]))
                    with pool.Fori(0, QUADS) as q:
                        n = j * QUADS + q
                        act_p.wait(pool, "pi", j)
                        vec_p.wait(pool, "kmod", j)
                        pe_q.wait(pool, "tk", n - 1)
                        pe_s.wait(pool, "tk", j - 1)
                        pool_q.done("b", nc.gpsimd.tensor_tensor(BK[:, :, 0:3:2, :], quad_cols(av, q)[:, :, None, :].to_broadcast([P, QC, 2, C]), quad_cols(cs, q)[:, :, None, :].to_broadcast([P, QC, 2, C]), ALU.mult))
                        pool_q.done("k", nc.gpsimd.tensor_tensor(BK[:, :, 1, :], quad_cols(zk, q), quad_cols(cs, q), ALU.mult))
                    tail = slice(SEQ, T)
                    pe_q.wait(pool, "tk", j * QUADS + (QUADS - 1))
                    pool_s.done("b", nc.gpsimd.tensor_tensor(BK[:, 0, 0:3:2, 0:NS], av[:, None, tail].to_broadcast([P, 2, NS]), cs[:, None, tail].to_broadcast([P, 2, NS]), ALU.mult))
                    pool_s.done("k", nc.gpsimd.tensor_tensor(BK[:, 0, 1, 0:NS], zk[:, tail], cs[:, tail], ALU.mult))

            @block.scalar
            def _(act):
                for s in all_steps["act"]:
                    s.begin(act)
                with act.Fori(0, PAIRS) as j:
                    for n, (z, raw, part, acc) in enumerate((("r", raw0, part0, accA), ("k", raw1, part1, accB), ("v", raw0, part0, accA))):
                        pe_p.wait(act, z, j)
                        if z == "r":
                            vec_o.wait(act, "out", j - 1)
                        if z == "v":
                            vec_p.wait(act, "fix_r", j)
                            pool_p.wait(act, "keep_r8", j)
                        act_p.done(f"raw_{z}", nc.scalar.activation(thirds(raw[:, 1:1 + T]), acc[:, :, 0:TT], ACT.Copy))
                        act_p.done(f"part_{z}", nc.scalar.activation(thirds(part[:, :]), acc[:, :, 0:TT], ACT.Copy, scale=mu1[:, bass.ds(j + n * KT, 1)]))
                    pe_p.wait(act, "decay", j)
                    act_p.done("sig_w", nc.scalar.activation(thirds(sg[:, :]), accB[:, :, 0:TT], ACT.Sigmoid, bias=col("decay_w0", j)))
                    pe_p.wait(act, "aaa", j)
                    act_p.done("sig_a", nc.scalar.activation(thirds(av[:, :]), accA[:, :, 0:TT], ACT.Sigmoid, bias=col("aaa_a0", j)))
                    vec_p.wait(act, "fix_k", j)
                    pool_p.wait(act, "keep_k8", j)
                    act_p.done("ksq", nc.scalar.activation(raw1[:, 1:1 + T], zk[:, :], ACT.Square, scale=col("k_k", j)))
                    vec_p.wait(act, "nrec", j)
                    act_p.done("rn", nc.scalar.activation(part1[:, :], part1[:, :], ACT.Sqrt))
                    vec_p.wait(act, "before", j)
                    act_p.done("pr", nc.scalar.activation(pr[:, :], cs[:, :], ACT.Exp, scale=-DECAY))
                    act_p.done("pp", nc.scalar.activation(pp[:, :], pp[:, :], ACT.Exp, scale=-DECAY))
                    act_p.wait(act, "pr", j)
                    act_p.done("pi", nc.scalar.activation(cs[:, :], cs[:, :], ACT.Exp, scale=DECAY))

                    def sv_quad(h):
                        return SV[half[1 - h], :, h, :]

                    def sv_samp(h):
                        return SVs[half[1 - h], h, :, :]

                    def v_rows(h, c, sv):
                        v = VT[half[1 - h], c, h * HD:(h + 1) * HD]
                        return v if sv is sv_quad else v[:, None, :].to_broadcast([HD, DB, HD])

                    def evacs(st, pe_t, n, c, sv):
                        pe_t.wait(act, "tk", n)
                        st.done("kb0", nc.scalar.activation(KB[:, c, 0, :], TK[0][:, c, 0:HD], ACT.Copy))
                        st.done("kb1", nc.scalar.activation(KB[:, c, 1, :], TK[1][:, c, HD:P], ACT.Copy))
                        pe_t.wait(act, "vt", n)
                        st.done("sv0", nc.scalar.activation(sv(0), v_rows(0, c, sv), ACT.Copy))
                        st.done("sv1", nc.scalar.activation(sv(1), v_rows(1, c, sv), ACT.Copy))
                        st.done("uv0", nc.scalar.activation(UV[HD:P, c, 0, :], VT[HD:P, c, 0:HD], ACT.Copy))
                        st.done("uv1", nc.scalar.activation(UV[0:HD, c, 1, :], VT[0:HD, c, HD:P], ACT.Copy))

                    def diagonals(st, pe_t, vec_t, n, c, levels):
                        for i in range(levels):
                            vec_t.wait(act, f"g{i}", n)
                            for h in range(2):
                                st.done(f"gd{h}_{i}", nc.scalar.activation(Gd[half[h], c, h * C:(h + 1) * C], Gs[half[h], c, :], ACT.Copy))
                            vec_t.wait(act, f"xt{i}", n)
                            for h in range(2):
                                st.done(f"xd{h}_{i}", nc.scalar.activation(XTd[half[h], c, h * C:(h + 1) * C], XT[half[h], c, :], ACT.Copy))

                    with act.Fori(0, QUADS) as q:
                        n = j * QUADS + q
                        vec_p.wait(act, "fix_v", j)
                        pe_q.wait(act, "vt", n - 1)
                        pe_s.wait(act, "vt", j - 1)
                        act_q.done("vd", nc.scalar.activation(Vd[:, :, :, :], quad_cols(zv, q)[:, :, None, :].to_broadcast([P, QC, 2, C]), ACT.Copy))
                        pe_q.wait(act, f"y{QC - 1}", n - 1)
                        pe_s.wait(act, "y", j - 1)
                        evacs(act_q, pe_q, n, slice(0, QC), sv_quad)
                        diagonals(act_q, pe_q, vec_q, n, slice(0, QC), LEVELS)
                        for c in range(QC):
                            if c:
                                vec_q.wait(act, f"s1{c - 1}", n)
                            else:
                                vec_q.wait(act, f"s1{QC - 1}", n - 1)
                                vec_p.wait(act, "s_zero1", j)
                                vec_q.wait(act, "pc", n)
                            for h in range(2):
                                act_q.done(f"sp{h}{c}", nc.scalar.activation(SP[half[h], :], SV[half[h], c, h, :], ACT.Copy, scale=PC[half[h], c:c + 1]))
                            pe_q.wait(act, f"u{c}", n)
                            act_q.done(f"u1_{c}", nc.scalar.activation(UV[HD:P, c, 1, :], UU[HD:P, c, :], ACT.Copy))
                        pe_q.wait(act, f"y{QC - 1}", n)
                        act_q.done("y", nc.scalar.activation(raw0[:, bass.ds(q * QT + 1, QT)].rearrange("p (c t) -> p c t", c=QC), Y[:, :, :], ACT.Copy))
                    nq = j * QUADS + (QUADS - 1)
                    pe_q.wait(act, "vt", nq)
                    act_s.done("vd", nc.scalar.activation(Vd[:, 0, :, 0:NS], zv[:, None, SEQ:T].to_broadcast([P, 2, NS]), ACT.Copy))
                    pe_q.wait(act, f"y{QC - 1}", nq)
                    evacs(act_s, pe_s, j, 0, sv_samp)
                    diagonals(act_s, pe_s, vec_s, j, 0, SLEVELS)
                    pe_s.wait(act, "u", j)
                    act_s.done("u1", nc.scalar.activation(UV[HD:P, 0, 1, :], UU[HD:P, 0, :], ACT.Copy))
                    pe_s.wait(act, "y", j)
                    act_s.done("y", nc.scalar.activation(raw0[:, 1 + SEQ:1 + T], Y[:, 0, 0:NS], ACT.Copy))
                    vec_o.wait(act, "yc", j)
                    act_o.done("sq", nc.scalar.activation(part1[:, :], raw1[:, 1:1 + T], ACT.Square))
                    vec_o.wait(act, "vr", j)
                    act_o.done("rs", nc.scalar.activation(part1[:, :], part1[:, :], ACT.Sqrt))

            @block.vector
            def _(vec):
                for s in all_steps["vec"]:
                    s.begin(vec)
                for z in (RB[HD:P, :, 0, :], RB[0:HD, :, 1, :], LT[:, :, :], Gd[:, :, :], XTd[:, :, :], raw0[:, 0:1], raw1[:, 0:1]):
                    nc.vector.memset(z, 0.0).then_inc(zero, 1)
                vec.wait_ge(zero, 7)

                def masked(st, pe_t, n, c, m, bc):
                    for h in range(2):
                        o = half[1 - h]
                        pe_t.wait(vec, f"gram{h}", n)
                        st.done(f"m{h}", nc.vector.tensor_tensor(H[h][o, c, :], G[h][o, c, :], bc(m[o, :]), ALU.mult))
                    for h in range(2):
                        st.done(f"l{h}", nc.vector.tensor_tensor(LT[half[h], c, h * C:(h + 1) * C], G[h][half[h], c, 0:C], bc(m[half[h], 0:C]), ALU.mult))
                    for h in range(2):
                        st.done(f"rb{h}", nc.vector.tensor_tensor(RB[half[h], c, h, :], G[h][half[h], c, C:P], bc(m[half[h], C:P]), ALU.mult))

                def doubling(st, pe_t, act_t, n, c, levels, bc):
                    for i in range(levels):
                        pe_t.wait(vec, f"G{i}", n)
                        st.done(f"g{i}", nc.vector.tensor_tensor(Gs[:, c, :], inv[0][:, c, :], bc(level[:, i, :]), ALU.mult))
                        if i < levels - 1:
                            pe_t.wait(vec, f"W{i}", n)
                            st.done(f"x{i}", nc.vector.tensor_tensor(X[:, c, :], inv[1][:, c, :], bc(ident2) if i == 0 else X[:, c, :], ALU.add))
                        pe_t.wait(vec, f"WT{i}", n)
                        st.done(f"xt{i}", nc.vector.tensor_tensor(XT[:, c, :], inv[2][:, c, :], bc(ident2) if i == 0 else XT[:, c, :], ALU.add))

                with vec.Fori(0, PAIRS) as j:
                    for n, (z, raw, part, dst) in enumerate((("r", raw0, part0, zr), ("k", raw1, part1, zk), ("v", raw0, part0, zv))):
                        mu = vec_sb[:, bass.ds(VEC["shift_mu"] + j + n * KT, 1)]
                        act_p.wait(vec, f"part_{z}", j)
                        if z != "k":
                            pe_o.wait(vec, "bonus", j - 1)
                        vec_p.done(f"lerp_{z}", nc.vector.scalar_tensor_tensor(dst[:, :], raw[:, 0:T], mu, part[:, :], ALU.mult, ALU.add))
                        vec_p.wait(vec, f"lerp_{z}", j)
                        vec_p.done(f"fix_{z}", nc.vector.scalar_tensor_tensor(dst[:, SEQ:T:DS], shift0[:, bass.ds(j + n * KT, 1), :].rearrange("p a b -> p (a b)"), mu, part[:, SEQ:T:DS], ALU.mult, ALU.add))
                    vec.wait_ge(s_out, 48 * j)
                    pe_q.wait(vec, f"y{QC - 1}", j * QUADS - 1)
                    for h in range(2):
                        vec_p.done(f"s_zero{h}", nc.vector.memset(SV[half[h], 0, h, :], 0.0))
                    act_p.wait(vec, "sig_w", j)
                    vec_p.done("cum", nc.vector.tensor_tensor_scan(cs[:, :], reset, sg[:, :], 0.0, ALU.mult, ALU.add))
                    vec_p.wait(vec, "cum", j)
                    vec_p.done("before", nc.vector.tensor_tensor(pp[:, :], cs[:, :], sg[:, :], ALU.subtract))
                    pe_p.wait(vec, "ksum", j)
                    vec_p.done("nmax", nc.vector.tensor_scalar(thirds(part1[:, :]), accB[:, :, 0:TT], 1e-24, None, ALU.max))
                    vec_p.wait(vec, "nmax", j)
                    vec_p.done("nrec", nc.vector.reciprocal(part1[:, :], part1[:, :]))
                    act_p.wait(vec, "rn", j)
                    vec_p.done("kkn", nc.vector.scalar_tensor_tensor(kkn[:, :], zk[:, :], col("k_k", j), part1[:, :], ALU.mult, ALU.mult))
                    act_p.wait(vec, "sig_a", j)
                    vec_p.done("t1", nc.vector.tensor_scalar(part0[:, :], av[:, :], col("k_a", j), ka1[:, bass.ds(j, 1)], ALU.mult, ALU.add))
                    vec_p.wait(vec, "t1", j)
                    vec_p.done("bb", nc.vector.tensor_tensor(av[:, :], kkn[:, :], av[:, :], ALU.mult))
                    vec_p.done("kmod", nc.vector.tensor_tensor(zk[:, :], zk[:, :], part0[:, :], ALU.mult))
                    vec_p.wait(vec, "kmod", j)
                    vec_p.done("rkk", nc.vector.scalar_tensor_tensor(sg[:, :], zr[:, :], col("r_k", j), zk[:, :], ALU.mult, ALU.mult))

                    with vec.Fori(0, QUADS) as q:
                        n = j * QUADS + q
                        over = lambda m: m[:, None, :].to_broadcast([m.shape[0], QC, m.shape[1]])
                        every = slice(0, QC)
                        act_p.wait(vec, "pp", j)
                        pe_q.wait(vec, f"y{QC - 1}", n - 1)
                        pe_s.wait(vec, "y", j - 1)
                        for h in range(2):
                            vec_q.done(f"r{h}", nc.vector.tensor_tensor(H[h][half[h], :, C:P], quad_cols(zr[half[h], :], q), quad_cols(pr[half[h], :], q), ALU.mult))
                        for h in range(2):
                            vec_q.done(f"a{h}", nc.vector.scalar_tensor_tensor(H[h][half[h], :, 0:C], quad_cols(kkn[half[h], :], q), -1.0, quad_cols(pp[half[h], :], q), ALU.mult, ALU.mult))
                        act_q.wait(vec, f"sp1{QC - 1}", n - 1)
                        vec_q.wait(vec, f"s1{QC - 1}", n - 1)
                        vec_q.done("pc", nc.vector.tensor_copy(PC[:, :], quad_cols(pr, q)[:, :, C - 1]))
                        masked(vec_q, pe_q, n, every, gram, over)
                        doubling(vec_q, pe_q, act_q, n, every, LEVELS, over)
                        for c in range(QC):
                            pe_q.wait(vec, f"rhs{c}", n)
                            vec_q.done(f"rhs{c}", nc.vector.tensor_copy(rhs[:, c, :], RH[:, c, :]))
                            pe_q.wait(vec, f"u{c}", n)
                            vec_q.done(f"u0{c}", nc.vector.tensor_copy(UV[0:HD, c, 0, :], UU[0:HD, c, :]))
                            pe_q.wait(vec, f"s{c}", n)
                            act_q.wait(vec, f"sp1{c}", n)
                            for h in range(2):
                                vec_q.done(f"s{h}{c}", nc.vector.scalar_tensor_tensor(SV[half[h], (c + 1) % QC, h, :], SS[half[h], c, :], PC[half[h], c:c + 1], SP[half[h], :], ALU.mult, ALU.add))

                    tail = slice(SEQ, T)
                    pe_q.wait(vec, f"y{QC - 1}", j * QUADS + (QUADS - 1))
                    for h in range(2):
                        vec_s.done(f"r{h}", nc.vector.tensor_tensor(H[h][half[h], 0, C:C + NS], zr[half[h], tail], pr[half[h], tail], ALU.mult))
                    for h in range(2):
                        vec_s.done(f"a{h}", nc.vector.scalar_tensor_tensor(H[h][half[h], 0, 0:NS], kkn[half[h], tail], -1.0, pp[half[h], tail], ALU.mult, ALU.mult))
                    one = lambda m: m
                    masked(vec_s, pe_s, j, 0, gram_s, one)
                    doubling(vec_s, pe_s, act_s, j, 0, SLEVELS, one)
                    pe_s.wait(vec, "rhs", j)
                    vec.wait_ge(s_out, 48 * j)
                    big = psum[:, 0, :].rearrange("p (b v) -> p b v", b=DB)
                    vec_s.done("sel", nc.vector.tensor_tensor(Rx[:, :, :], big, tok8[:, :, None].to_broadcast([P, DB, HD]), ALU.mult))
                    vec_s.wait(vec, "sel", j)
                    vec_s.done("rhs", nc.vector.tensor_reduce(rhs[:, 0, :], Rx[:, :, :].rearrange("p b v -> p v b"), AXX, ALU.add))
                    pe_s.wait(vec, "u", j)
                    vec_s.done("u0", nc.vector.tensor_copy(UV[0:HD, 0, 0, :], UU[0:HD, 0, :]))
                    vec_s.wait(vec, "u0", j)
                    act_s.wait(vec, "u1", j)
                    for h in range(2):
                        vec_s.done(f"ux{h}", nc.vector.tensor_tensor(UVx[:, h, :, :], UV[:, 0, h, :][:, None, :].to_broadcast([P, DB, HD]), tok8[:, :, None].to_broadcast([P, DB, HD]), ALU.mult))
                    pe_s.wait(vec, "s", j)
                    big1 = psum[:, 1, :].rearrange("p (b v) -> p b v", b=DB)
                    for h in range(2):
                        vec_s.done(f"s{h}", nc.vector.tensor_tensor(Rx[half[h], :, :], big1[half[h], :, :], SVs[half[h], h, :, :], ALU.add))
                    vec_s.wait(vec, "s1", j)
                    vec_s.done("dec", nc.vector.tensor_tensor(Rx[:, :, :], Rx[:, :, :], pr[:, SEQ + DS - 1:T:DS][:, :, None].to_broadcast([P, DB, HD]), ALU.mult))

                    pe_o.wait(vec, "bonus", j)
                    vec_o.done("bon", nc.vector.tensor_tensor(thirds(part0[:, :]), accA[:, :, 0:TT], thirds(zv[:, :]), ALU.mult))
                    pe_o.wait(vec, "mean", j)
                    vec_o.done("yc", nc.vector.scalar_tensor_tensor(thirds(raw1[:, 1:1 + T]), accB[:, :, 0:TT], -1.0 / HD, thirds(raw0[:, 1:1 + T]), ALU.mult, ALU.add))
                    pe_o.wait(vec, "var", j)
                    vec_o.done("vv", nc.vector.tensor_scalar(thirds(part1[:, :]), accA[:, :, 0:TT], 1.0 / HD, LNX_EPS, ALU.mult, ALU.add))
                    vec_o.wait(vec, "vv", j)
                    vec_o.done("vr", nc.vector.reciprocal(part1[:, :], part1[:, :]))
                    act_o.wait(vec, "rs", j)
                    vec_o.done("yn", nc.vector.tensor_tensor(raw1[:, 1:1 + T], raw1[:, 1:1 + T], part1[:, :], ALU.mult))
                    vec_o.wait(vec, "yn", j)
                    vec_o.done("yl", nc.vector.tensor_scalar(raw1[:, 1:1 + T], raw1[:, 1:1 + T], col("lnx_w", j), col("lnx_b", j), ALU.mult, ALU.add))
                    vec_o.wait(vec, "yl", j)
                    vec_o.done("yb", nc.vector.tensor_tensor(part0[:, :], raw1[:, 1:1 + T], part0[:, :], ALU.add))
                    vec_o.wait(vec, "yb", j)
                    pe_o.wait(vec, "gate", j)
                    vec_o.done("out", nc.vector.tensor_tensor(out[:, bass.ds(j, 1), :].rearrange("p o (n c) -> p (o n) c", n=NT), accB[:, :, 0:TT], thirds(part0[:, :]), ALU.mult))

            @block.tensor
            def _(pe):
                for s in all_steps["pe"]:
                    s.begin(pe)
                pe.wait_ge(zero, 7)
                w3 = w[:, 0:3 * KT * P].rearrange("p (k c) -> p k c", k=KT)
                lora_w, gate_w = w[:, 3 * KT * P:3 * KT * P + P], w[:, 3 * KT * P + P:WPAIR]

                def grams(st, n, chunks, vec_t, pool_t, act_t):
                    vec_t.wait(pe, "a1", n)
                    pool_t.wait(pe, "k", n)
                    for h in range(2):
                        for c in chunks:
                            last = nc.tensor.matmul(G[h][:, c, :], BK[half[h], c, h:h + 2, :], H[h][half[h], c, :], start=True, stop=True)
                        st.done(f"gram{h}", last)
                    for c in chunks:
                        for h in range(2):
                            last = nc.tensor.transpose(TK[h][:, c, :], BK[:, c, h:h + 2, :], ident)
                    st.done("tk", last)
                    act_t.wait(pe, "vd", n)
                    for c in chunks:
                        last = nc.tensor.transpose(VT[:, c, :], Vd[:, c, :, :], ident)
                    st.done("vt", last)

                def inverse(st, n, chunks, vec_t, act_t, levels):
                    vec_t.wait(pe, "l1", n)
                    for i in range(levels):
                        if i:
                            vec_t.wait(pe, f"x{i - 1}", n)
                        for c in chunks:
                            last = nc.tensor.matmul(inv[0][:, c, :], LT[:, c, :], X[:, c, :] if i else ident2, start=True, stop=True)
                        st.done(f"G{i}", last)
                        vec_t.wait(pe, f"g{i}", n)
                        if i < levels - 1:
                            if i:
                                act_t.wait(pe, f"xd1_{i - 1}", n)
                            for c in chunks:
                                last = nc.tensor.matmul(inv[1][:, c, :], XTd[:, c, :] if i else ident, Gs[:, c, :], start=True, stop=True)
                            st.done(f"W{i}", last)
                        act_t.wait(pe, f"gd1_{i}", n)
                        if i:
                            vec_t.wait(pe, f"xt{i - 1}", n)
                        for c in chunks:
                            last = nc.tensor.matmul(inv[2][:, c, :], Gd[:, c, :], XT[:, c, :] if i else ident2, start=True, stop=True)
                        st.done(f"WT{i}", last)

                with pe.Fori(0, PAIRS) as j:
                    pe.wait_ge(w_in, 16 * j + 16)
                    for n, (z, acc) in enumerate((("r", accA), ("k", accB), ("v", accA))):
                        if z == "r":
                            vec_o.wait(pe, "vv", j - 1)
                            vec_o.wait(pe, "out", j - 1)
                        if z == "v":
                            act_p.wait(pe, "part_r", j)
                        pe_p.done(z, product(nc, acc, w3[:, :, n * P:(n + 1) * P], hT, KT))
                    for z, rows, acc, last in (("decay", half[0], accB, "part_k"), ("aaa", half[1], accA, "part_v")):
                        act_p.wait(pe, last, j)
                        for n in range(NT):
                            mm = nc.tensor.matmul(acc[:, n, 0:TT], lora_w[rows, :], low[rows, 0, n * TT:(n + 1) * TT], start=True, stop=True)
                        pe_p.done(z, mm)
                    act_p.wait(pe, "ksq", j)
                    act_p.wait(pe, "sig_w", j)
                    for n in range(NT):
                        mm = nc.tensor.matmul(accB[:, n, 0:TT], ones2, raw1[:, 1 + n * TT:1 + (n + 1) * TT], start=True, stop=True)
                    pe_p.done("ksum", mm)
                    with pe.Fori(0, QUADS) as q:
                        n = j * QUADS + q
                        vec_p.wait(pe, "nmax", j)
                        act_p.wait(pe, "sig_a", j)
                        act_q.wait(pe, "y", n - 1)
                        vec_q.wait(pe, f"s1{QC - 1}", n - 1)
                        grams(pe_q, n, range(QC), vec_q, pool_q, act_q)
                        inverse(pe_q, n, range(QC), vec_q, act_q, LEVELS)
                        act_q.wait(pe, "uv1", n)
                        vec_q.wait(pe, "rb1", n)
                        act_q.wait(pe, f"xd1_{LEVELS - 1}", n)
                        for c in range(QC):
                            if c:
                                vec_q.wait(pe, f"s1{c - 1}", n)
                            else:
                                vec_p.wait(pe, "s_zero1", j)
                            for h in range(2):
                                mm = nc.tensor.matmul(RH[half[h], c, :], H[h][:, c, 0:C], SV[:, c, h, :], start=True, stop=True)
                            pe_q.done(f"rhs{c}", mm)
                            vec_q.wait(pe, f"rhs{c}", n)
                            pe_q.done(f"u{c}", nc.tensor.matmul(UU[:, c, :], XTd[:, c, :], rhs[:, c, :], start=True, stop=True))
                            vec_q.wait(pe, f"u0{c}", n)
                            act_q.wait(pe, f"u1_{c}", n)
                            for h in range(2):
                                mm = nc.tensor.matmul(SS[half[h], c, :], KB[:, c, h, :], UV[:, c, h, :], start=True, stop=True)
                            pe_q.done(f"s{c}", mm)
                            for h in range(2):
                                nc.tensor.matmul(Y[half[h], c, :], SV[:, c, h, :], H[h][:, c, C:P], start=True, stop=False)
                                mm = nc.tensor.matmul(Y[half[h], c, :], UV[:, c, h, :], RB[:, c, h, :], start=False, stop=True)
                            pe_q.done(f"y{c}", mm)
                    nq = j * QUADS + (QUADS - 1)
                    act_q.wait(pe, "y", nq)
                    vec_q.wait(pe, f"s1{QC - 1}", nq)
                    grams(pe_s, j, range(1), vec_s, pool_s, act_s)
                    inverse(pe_s, j, range(1), vec_s, act_s, SLEVELS)
                    act_s.wait(pe, "uv1", j)
                    vec_s.wait(pe, "rb1", j)
                    act_s.wait(pe, f"xd1_{SLEVELS - 1}", j)
                    pe.wait_ge(s0_in, 32 * j + 32)
                    for h in range(2):
                        mm = nc.tensor.matmul(psum[half[h], 0, :], H[h][:, 0, 0:C], SVs[:, h, :, :], start=True, stop=True)
                    pe_s.done("rhs", mm)
                    vec_s.wait(pe, "rhs", j)
                    pe_s.done("u", nc.tensor.matmul(UU[:, 0, :], XTd[:, 0, :], rhs[:, 0, :], start=True, stop=True))
                    vec_s.wait(pe, "ux1", j)
                    for h in range(2):
                        mm = nc.tensor.matmul(psum[half[h], 1, :], KB[:, 0, h, :], UVx[:, h, :, :], start=True, stop=True)
                    pe_s.done("s", mm)
                    for h in range(2):
                        nc.tensor.matmul(Y[half[h], 0, 0:NS], UV[:, 0, h, :], RB[:, 0, h, 0:NS], start=True, stop=False)
                        for b in range(DB):
                            mm = nc.tensor.matmul(Y[half[h], 0, DS * b:DS * b + DS], SVs[:, h, b, :], H[h][:, 0, C + DS * b:C + DS * b + DS], start=False, stop=b == DB - 1)
                    pe_s.done("y", mm)

                    act_s.wait(pe, "y", j)
                    vec_s.wait(pe, "s1", j)
                    for n in range(NT):
                        mm = nc.tensor.matmul(accA[:, n, 0:TT], ones2, sg[:, n * TT:(n + 1) * TT], start=True, stop=True)
                    pe_o.done("bonus", mm)
                    for n in range(NT):
                        mm = nc.tensor.matmul(accB[:, n, 0:TT], ones2, raw0[:, 1 + n * TT:1 + (n + 1) * TT], start=True, stop=True)
                    pe_o.done("mean", mm)
                    vec_o.wait(pe, "bon", j)
                    act_o.wait(pe, "sq", j)
                    for n in range(NT):
                        mm = nc.tensor.matmul(accA[:, n, 0:TT], ones2, part1[:, n * TT:(n + 1) * TT], start=True, stop=True)
                    pe_o.done("var", mm)
                    for n in range(NT):
                        mm = nc.tensor.matmul(accB[:, n, 0:TT], gate_w, low[:, 1, n * TT:(n + 1) * TT], start=True, stop=True)
                    pe_o.done("gate", mm)


def gated_stage(nc, top, name, w_src, width, tiles, psum, x, out, add):
    nb = len(tiles)
    with ExitStack() as ctx:
        sb = lambda n, *s: ctx.enter_context(nc.sbuf_tensor(f"{name}_{n}", [P, *s], F32))
        w = sb("w", 2, width)
        gate, prod = sb("gate", 2, T), sb("prod", 2, T)
        acc = [psum[:, 0:3, :], psum[:, 3:6, :]]
        w_in = [top.enter_context(nc.semaphore(f"{name}_w_in{s}")) for s in range(2)]
        pe_s = Steps(top.enter_context(nc.semaphore(f"{name}_pe")), [f"{m}{i}" for i in range(nb) for m in ("gate", "branch")], ahead=2)
        act_s = Steps(top.enter_context(nc.semaphore(f"{name}_act")), [f"gate{i}" for i in range(nb)], ahead=2)
        vec_s = Steps(top.enter_context(nc.semaphore(f"{name}_vec")), [f"mul{i}" for i in range(nb)] + [f"add{i}" for i in range(nb - 1 + add)], ahead=2)

        def turns(eng, turn):
            with eng.Fori(0, KT // 2) as i:
                for s in range(2):
                    turn(2 * i + s, s, i)

        with nc.Block() as block:
            @block.sync
            def _(sp):
                def turn(t, s, i):
                    pe_s.wait(sp, f"branch{nb - 1}", t - 2)
                    sp.dma_start(w[:, s, :], w_src[bass.ds(t, 1), :, :].rearrange("o p c -> p (o c)")).then_inc(w_in[s], 16)
                turns(sp, turn)

            @block.tensor
            def _(pe):
                pe_s.begin(pe)

                def turn(t, s, i):
                    pe.wait_ge(w_in[s], 16 * i + 16)
                    at = 0
                    for b, (gk, gx, bk, bx) in enumerate(tiles):
                        for m, kt, src in (("gate", gk, gx), ("branch", bk, bx)):
                            if m == "gate":
                                act_s.wait(pe, f"gate{(b - 1) % nb}", t if b else t - 1)
                            else:
                                vec_s.wait(pe, f"mul{(b - 1) % nb}", t if b else t - 1)
                            wt = w[:, s, at:at + kt * P].rearrange("p (k c) -> p k c", k=kt)
                            at += kt * P
                            pe_s.done(f"{m}{b}", product(nc, acc[m == "branch"], wt, src, kt))
                turns(pe, turn)

            @block.scalar
            def _(act):
                act_s.begin(act)

                def turn(t, s, i):
                    for b in range(nb):
                        pe_s.wait(act, f"gate{b}", t)
                        vec_s.wait(act, f"mul{b}", t - 1 if nb == 2 else t - 2)
                        act_s.done(f"gate{b}", nc.scalar.activation(thirds(gate[:, b if nb == 2 else s, :]), acc[0][:, :, 0:TT], ACT.Sigmoid))
                turns(act, turn)

            @block.vector
            def _(vec):
                vec_s.begin(vec)

                def turn(t, s, i):
                    for b in range(nb):
                        act_s.wait(vec, f"gate{b}", t)
                        pe_s.wait(vec, f"branch{b}", t)
                        vec_s.wait(vec, vec_s.names[-1], t - 1)
                        vec_s.done(f"mul{b}", nc.vector.tensor_tensor(thirds(prod[:, b, :]), thirds(gate[:, b if nb == 2 else s, :]), acc[1][:, :, 0:TT], ALU.mult))
                    row = (x if add else out)[:, bass.ds(t, 1), :].rearrange("p o c -> p (o c)")
                    vec_s.wait(vec, f"mul{nb - 1}", t)
                    if add:
                        vec_s.done("add0", nc.vector.tensor_tensor(row, row, prod[:, 0, :], ALU.add))
                    else:
                        vec_s.done("add0", nc.vector.tensor_tensor(row, prod[:, 0, :], prod[:, 1, :], ALU.add))
                turns(vec, turn)


def residual_projection(nc, top, name, w_src, psum, src, x):
    with ExitStack() as ctx:
        w = ctx.enter_context(nc.sbuf_tensor(f"{name}_w", [P, 2, KT * P], F32))
        acc = [psum[:, 0:3, :], psum[:, 3:6, :]]
        w_in = [top.enter_context(nc.semaphore(f"{name}_w_in{s}")) for s in range(2)]
        pe_s = Steps(top.enter_context(nc.semaphore(f"{name}_pe")), ["full"], ahead=2)
        vec_s = Steps(top.enter_context(nc.semaphore(f"{name}_vec")), ["add"], ahead=2)
        with nc.Block() as block:
            @block.sync
            def _(sp):
                with sp.Fori(0, KT // 2) as i:
                    for s in range(2):
                        pe_s.wait(sp, "full", 2 * i + s - 2)
                        sp.dma_start(w[:, s, :], w_src[bass.ds(2 * i + s, 1), :, :].rearrange("o p c -> p (o c)")).then_inc(w_in[s], 16)

            @block.tensor
            def _(pe):
                pe_s.begin(pe)
                with pe.Fori(0, KT // 2) as i:
                    for s in range(2):
                        pe.wait_ge(w_in[s], 16 * i + 16)
                        vec_s.wait(pe, "add", 2 * i + s - 2)
                        pe_s.done("full", product(nc, acc[s], w[:, s, :].rearrange("p (k c) -> p k c", k=KT), src, KT))

            @block.vector
            def _(vec):
                vec_s.begin(vec)
                with vec.Fori(0, KT // 2) as i:
                    for s in range(2):
                        t = 2 * i + s
                        pe_s.wait(vec, "full", t)
                        row = x[:, bass.ds(t, 1), :].rearrange("p o (n c) -> p (o n) c", n=NT)
                        vec_s.done("add", nc.vector.tensor_tensor(row, row, acc[s][:, :, 0:TT], ALU.add))


def mlp(nc, top, w_src, psum, hT, ff, x):
    with ExitStack() as ctx:
        w = ctx.enter_context(nc.sbuf_tensor("ff_w", [P, 2, KT * P], F32))
        up = ctx.enter_context(nc.sbuf_tensor("ff_up", [P, 2, T], F32))
        acc = [psum[:, 0:3, :], psum[:, 3:6, :]]
        w_in = [top.enter_context(nc.semaphore(f"ff_w_in{s}")) for s in range(2)]
        pe_s = Steps(top.enter_context(nc.semaphore("ff_pe")), ["full"], ahead=2)
        act_s = Steps(top.enter_context(nc.semaphore("ff_act")), ["relu", "square"], ahead=2)
        vec_s = Steps(top.enter_context(nc.semaphore("ff_vec")), ["add"], ahead=2)
        H = KT // 2
        with nc.Block() as block:
            @block.sync
            def _(sp):
                with sp.Fori(0, FFQ * 2 * H) as i:
                    for s in range(2):
                        pe_s.wait(sp, "full", 2 * i + s - 2)
                        sp.dma_start(w[:, s, :], w_src[bass.ds(2 * i + s, 1), :, :].rearrange("o p c -> p (o c)")).then_inc(w_in[s], 16)

            @block.tensor
            def _(pe):
                pe_s.begin(pe)
                with pe.Fori(0, FFQ) as q:
                    with pe.Fori(0, H) as i:
                        for s in range(2):
                            pe.wait_ge(w_in[s], 16 * (2 * H * q + i) + 16)
                            act_s.wait(pe, "relu", KT * q + 2 * i + s - 2)
                            vec_s.wait(pe, "add", KT * q + s - 2)
                            pe_s.done("full", product(nc, acc[s], w[:, s, :].rearrange("p (k c) -> p k c", k=KT), hT, KT))
                    with pe.Fori(0, H) as i:
                        for s in range(2):
                            pe.wait_ge(w_in[s], 16 * (2 * H * q + H + i) + 16)
                            act_s.wait(pe, "square", KT * q + KT - 1)
                            vec_s.wait(pe, "add", KT * q + 2 * i + s - 2)
                            pe_s.done("full", product(nc, acc[s], w[:, s, :].rearrange("p (k c) -> p k c", k=KT), ff, KT))

            @block.scalar
            def _(act):
                act_s.begin(act)
                with act.Fori(0, FFQ) as q:
                    with act.Fori(0, H) as i:
                        for s in range(2):
                            t = KT * q + 2 * i + s
                            pe_s.wait(act, "full", 2 * KT * q + 2 * i + s)
                            act_s.wait(act, "square", t - 2)
                            act_s.done("relu", nc.scalar.activation(thirds(up[:, s, :]), acc[s][:, :, 0:TT], ACT.Relu))
                            act_s.wait(act, "relu", t)
                            act_s.done("square", nc.scalar.activation(ff[:, bass.ds(2 * i + s, 1), :].rearrange("p o c -> p (o c)"), up[:, s, :], ACT.Square))

            @block.vector
            def _(vec):
                vec_s.begin(vec)
                with vec.Fori(0, FFQ) as q:
                    with vec.Fori(0, H) as i:
                        for s in range(2):
                            pe_s.wait(vec, "full", 2 * KT * q + KT + 2 * i + s)
                            row = x[:, bass.ds(2 * i + s, 1), :].rearrange("p o (n c) -> p (o n) c", n=NT)
                            vec_s.done("add", nc.vector.tensor_tensor(row, row, acc[s][:, :, 0:TT], ALU.add))


def program(nc, ins, outs):
    with ExitStack() as ctx:
        sb = lambda n, s: ctx.enter_context(nc.sbuf_tensor(n, s, F32))
        hT = sb("hT", [P, KT, T])
        mixer = sb("rwkv_out", [P, KT, T])
        attn = sb("attn", [P, 2, T])
        vec_sb = sb("vec_sb", [P, NVEC])
        cst_sb = sb("cst_sb", [P, NCST])
        mu1 = sb("mu1", [P, RT])
        ka1 = sb("ka1", [P, KT])
        psum = ctx.enter_context(nc.psum_tensor("psum", [P, 8, 512], F32))
        scratch = nc.dram_tensor("attention_rows", (SEQ, GROUPS * STG), F32, kind="Internal").ap()
        sem = lambda n: ctx.enter_context(nc.semaphore(n))
        cst = lambda n: cst_sb[:, CST[n][0]:CST[n][1]]
        gain = lambda n: vec_sb[:, VEC[n]:VEC[n] + KT]

        with nc.sbuf_tensor("x_in", [P, KT, T], F32) as x_in:
            load_all(nc, sem("loaded"), [(x_in[:, :, :], ins["xT"]), (vec_sb[:, :], ins["vecs"]), (cst_sb[:, :], ins["consts"])])
            rms_norm(nc, "mix", x_in, gain("norm_mix"), cst_sb, hT, psum, ctx)
        derived = sem("derived")
        with nc.Block() as block:
            @block.vector
            def _(vec):
                nc.vector.tensor_scalar(mu1[:, :], vec_sb[:, VEC["shift_mu"]:VEC["shift_mu"] + RT], -1.0, 1.0, ALU.mult, ALU.add).then_inc(derived, 1)
                nc.vector.tensor_scalar(ka1[:, :], vec_sb[:, VEC["k_a"]:VEC["k_a"] + KT], -1.0, 1.0, ALU.mult, ALU.add).then_inc(derived, 1)

        with ExitStack() as c1:
            sb1 = lambda n, s: c1.enter_context(nc.sbuf_tensor(n, s, F32))
            att_sb = sb1("att_sb", [P, NATT])
            att = lambda n: att_sb[:, ATT[n][0]:ATT[n][1]]
            vnew = sb1("vnew", [NS, GROUPS, AW])
            scores = sb1("sample_scores", [P, GROUPS, SK])
            load_all(nc, sem("att_loaded"), [(att_sb[:, :], ins["att_consts"])])
            with ExitStack() as c2:
                sb2 = lambda n, s: c2.enter_context(nc.sbuf_tensor(n, s, F32))
                qT, kT, vtok = sb2("qT", [P, 2, T]), sb2("kT", [P, 2, T]), sb2("vtok", [P, NB, AW])
                for g in range(GROUPS):
                    attention_projection(nc, ctx, g, hT, ins["w_qk"][g], ins["w_kv"][g], psum, qT, kT, vtok, vnew, outs["k_all"][g], outs["v_all"][g])
                    attention_prompt(nc, ctx, g, psum, qT, kT, vtok, att, cst("ident"), scratch)
                    sample_scores(nc, ctx, g, psum, qT, kT, att, ins[f"kc{g}"], scores)
            load_all(nc, sem("vnew_stored"), [(outs["v_new"], vnew[:, :, :])])
            sample_attention(nc, ctx, psum, att, cst("ident"), scores, vnew, [ins[f"vc{g}"] for g in range(GROUPS)], attn)
            combine_groups(nc, ctx, psum, cst("ident"), scratch, attn)
        with ExitStack() as c2:
            low = c2.enter_context(nc.sbuf_tensor("low", [P, 2, T], F32))
            shift_sb = c2.enter_context(nc.sbuf_tensor("shift_sb", [P, RT, 1 + DB], F32))
            shift0 = c2.enter_context(nc.sbuf_tensor("shift0", [P, RT, DB], F32))
            load_all(nc, sem("shift_loaded"), [(shift0[:, :, :], ins["shift0"])])
            rwkv_lora_inputs(nc, ctx, hT, ins["w_lora"], shift0, vec_sb, mu1, cst, psum, low, shift_sb)
            rwkv_pairs(nc, ctx, hT, ins["w_pair"], shift0, ins["s0T"], vec_sb, mu1, ka1, cst, psum, low, shift_sb, mixer, outs["wkv_p"], outs["wkv_s"])
            load_all(nc, sem("shift_stored"), [(outs["shift"], shift_sb[:, :, :])])

        x = sb("x", [P, KT, T])
        with nc.sbuf_tensor("mixed", [P, KT, T], F32) as mixed:
            gated_stage(nc, ctx, "merge", ins["w_mix"], WMIX, [(KT, hT, KT, mixer), (KT, hT, 2, attn)], psum, None, mixed, False)
            load_all(nc, sem("x_again"), [(x[:, :, :], ins["xT"])])
            residual_projection(nc, ctx, "proj", ins["w_out"], psum, mixed, x)
        rms_norm(nc, "mlp", x, gain("norm_mlp"), cst_sb, hT, psum, ctx)
        mlp(nc, ctx, ins["w_ff"], psum, hT, mixer, x)
        rms_norm(nc, "ple", x, gain("norm_ple"), cst_sb, hT, psum, ctx)
        with nc.sbuf_tensor("pT", [P, 2, T], F32) as pT:
            load_all(nc, sem("p_loaded"), [(pT[:, :, :], ins["pT"])])
            gated_stage(nc, ctx, "ple", ins["w_ple"], WPLE, [(KT, hT, 2, pT)], psum, x, None, True)
        rms_norm(nc, "final", x, gain("norm_final"), cst_sb, hT, psum, ctx, store=outs["yT"])


def _constants(np):
    def two(m):
        return np.concatenate([m, m], 0)

    i, k = np.arange(P), np.arange(C)
    s, t = k[:, None], k[None, :]
    out = {
        "ident": np.eye(P),
        "ident2": two(np.eye(C)),
        "ones": np.ones((P, P)),
        "ones2": (i[:, None] // HD == i[None, :] // HD),
        "gram": two(np.concatenate([s < t, s <= t], 1)),
    }
    same = (s // DS == t // DS) & (s < NS) & (t < NS)
    out["gram_s"] = two(np.concatenate([same & (s < t), same & (s <= t)], 1))
    out["level"] = two(np.concatenate([(s // n % 2 == 1) & (t // n == s // n - 1) for n in (1 << np.arange(LEVELS))], 1))
    at = np.arange(T)
    out["reset"] = np.broadcast_to(np.where(at < SEQ, at % C != 0, (at - SEQ) % DS != 0), (P, T))
    q, key = i[:, None], np.arange(2 * BL)[None, :]
    dist = q + BL - key
    out["band"] = np.where((dist >= 0) & (dist <= BL), 0.0, NEG)
    kk = i[None, :]
    out["pairs"] = np.where((q % 2 == kk % 2) & (kk <= q), 0.0, NEG)
    hp, tok, c = np.arange(2)[:, None, None], np.arange(NS)[None, :, None], np.arange(32)[None, None, :]
    want = 16 * (tok // DS % 2) + 4 * (tok % DS) + 2 * hp
    out["place"] = np.stack([(c == want + h) for h in range(2)]).repeat(HD, 0).reshape(P, -1)
    row_t = (i // HPG % DS)[:, None]
    key = np.arange(SK)[None, :]
    new = key - NCACHE
    fresh = [np.where(np.where(new >= 0, new <= row_t, key >= row_t), 0.0, NEG)]
    fresh += [np.where((new < 0) | (new == row_t), 0.0, NEG)] * 2
    out["fresh"] = np.concatenate(fresh, 1)
    out["own8"] = i[:, None] // (HPG * DS) == np.arange(DB)[None, :]
    tk = np.concatenate([k, k])
    out["tok8"] = (tk[:, None] < NS) & (tk[:, None] // DS == np.arange(DB)[None, :])
    return [np.concatenate([np.asarray(out[n], np.float32) for n in names], 1) for names in (CST, ATT)]


def _tiles(np, w, cols):
    kk, m = w.shape
    return np.ascontiguousarray(w.reshape(kk // P, P, m // cols, cols).transpose(2, 1, 0, 3).reshape(m // cols, P, -1))


def _layout(np, a):
    a = {k: np.asarray(v) for k, v in a.items()}
    x = np.concatenate([a["x_prompt"][0], a["x_sample"].reshape(NS, D)], 0)
    p = np.concatenate([a["p_prompt"][0, 0], a["p_sample"][0].reshape(NS, -1)], 0)
    feat = lambda v: v.reshape(-1, P).T
    fm = lambda m: np.ascontiguousarray(m.T.reshape(-1, P, m.shape[0]).transpose(1, 0, 2))
    w_in = a["w_in"][0]
    rw = 3 * D + 256
    q0, k0, v0, g0 = rw, rw + 3 * AW, rw + 6 * AW, rw + 9 * AW
    heads = lambda c: [w_in[:, c + AW * g:c + AW * (g + 1)] for g in range(GROUPS)]
    d = {"xT": fm(x), "pT": fm(p)}
    d["vecs"] = np.concatenate([feat(a[n].reshape(-1)) for n in VEC], 1)
    d["consts"], d["att_consts"] = _constants(np)
    d["shift0"] = np.ascontiguousarray(a["state_shift"][0].T.reshape(RT, P, DB).transpose(1, 0, 2))
    d["w_lora"] = _tiles(np, w_in[:, 3 * D:rw], 256)[0].reshape(P, KT, 256)
    lora = np.concatenate([a["decay_w2"][0], a["aaa_a2"][0]], 0)
    rkv = w_in[:, :3 * D].reshape(KT, P, 3, PAIRS, P).transpose(3, 1, 0, 2, 4).reshape(PAIRS, P, -1)
    d["w_pair"] = np.concatenate([rkv, _tiles(np, lora, P), _tiles(np, a["gate_g2"][0], P)], 2)
    d["s0T"] = np.ascontiguousarray(a["state_wkv"][0].reshape(DB, PAIRS, 2, HD, HD).transpose(1, 2, 4, 0, 3).reshape(PAIRS, P, DB, HD))
    wq, wk, wv = heads(q0), heads(k0), heads(v0)
    d["w_qk"] = np.stack([_tiles(np, np.concatenate([wq[g], wk[g][:, :P]], 1), 3 * P)[0] for g in range(GROUPS)])
    d["w_kv"] = np.stack([np.concatenate([_tiles(np, wk[g][:, P:], P)[0], _tiles(np, wv[g], AW)[0]], 1) for g in range(GROUPS)])
    for g in range(GROUPS):
        cache = a[f"cache_kv_g{g}"][0]
        rows = cache.reshape(DB, NCACHE, DIL[g], 2, HPG, HD)[:, :, :DS]
        d[f"kc{g}"] = np.ascontiguousarray(rows[:, :, :, 0].reshape(DB, NCACHE, -1, 2, P).transpose(4, 3, 0, 2, 1))
        d[f"vc{g}"] = np.ascontiguousarray(rows[:, :, :, 1].reshape(DB, NCACHE, -1, AW).transpose(1, 0, 2, 3))
    g = _tiles(np, w_in[:, g0:], P)
    br = _tiles(np, a["w_branch_rwkv"][0], P)
    ba = _tiles(np, a["w_branch_attn"][0], P)
    d["w_mix"] = np.concatenate([g[:KT], br, g[KT:], ba], 2)
    d["w_out"] = _tiles(np, a["w_out"][0], P)
    w1 = _tiles(np, a["w_ff1"][0], P).reshape(FFQ, KT, P, -1)
    w2 = np.stack([_tiles(np, w, P) for w in a["w_ff2"][0].reshape(FFQ, D, D)])
    d["w_ff"] = np.concatenate([w1, w2], 1).reshape(FFQ * 2 * KT, P, -1)
    d["w_ple"] = np.concatenate([_tiles(np, a["w_ple_gate"][0], P), _tiles(np, a["w_ple"][0], P)], 2)
    return d


_OUT = {"yT": (P, KT, T), "k_all": (GROUPS, P, 2, T), "v_all": (GROUPS, P, NB, AW), "v_new": (NS, GROUPS, AW),
        "wkv_p": (PAIRS, P, HD), "wkv_s": (PAIRS, P, DB, HD), "shift": (P, RT, 1 + DB)}


def _results(np, r):
    y = r["yT"].transpose(2, 1, 0).reshape(T, D)
    kv_p, kv_s = [], []
    for g, keep in enumerate((128, 512, SEQ)):
        k = r["k_all"][g].transpose(2, 1, 0).reshape(T, HPG, HD)
        v = r["v_all"][g].transpose(1, 0, 2)
        if g == 1:
            v = v.reshape(STEP[1], SEQ // STEP[1], AW).transpose(1, 0, 2)
        elif g == 2:
            v = v.transpose(1, 0, 2)
        v = v.reshape(SEQ, HPG, HD)
        kv_p.append(np.stack([k[SEQ - keep:SEQ], v[SEQ - keep:]], 1)[None, None])
        vs = r["v_new"][:, g].reshape(DB, DS, HPG, HD)
        kv_s.append(np.stack([k[SEQ:].reshape(DB, DS, HPG, HD), vs], 2)[None])
    state = lambda w: w.reshape(PAIRS, 2, HD, -1, HD).transpose(3, 0, 1, 4, 2).reshape(-1, 2 * PAIRS, HD, HD)
    sh = r["shift"].transpose(2, 1, 0).reshape(1 + DB, RT * P)
    out = (y[None, :SEQ], y[SEQ:].reshape(DB, DS, D), *kv_p, state(r["wkv_p"][:, :, None, :])[None], sh[None, 0:1],
           *kv_s, state(r["wkv_s"])[None], sh[None, 1:])
    return tuple(np.ascontiguousarray(o) for o in out)


def kernel(**inputs):
    import numpy as np
    import concourse.bacc as bacc
    from concourse.bass_utils import run_bass_kernel_spmd

    nc = bacc.Bacc("TRN2", target_bir_lowering=False, num_devices=1)
    arrays = {f"in_{k}": np.ascontiguousarray(v) for k, v in _layout(np, inputs).items()}
    ins = {k[3:]: nc.dram_tensor(k, v.shape, F32, kind="ExternalInput").ap() for k, v in arrays.items()}
    outs = {k: nc.dram_tensor(f"out_{k}", s, F32, kind="ExternalOutput").ap() for k, s in _OUT.items()}
    program(nc, ins, outs)
    r = run_bass_kernel_spmd(nc, [arrays], core_ids=[0])
    got = r.results[0]
    return _results(np, {k: got[f"out_{k}"] for k in _OUT})
```

```python
import concourse.bass as bass
from concourse import mybir
from contextlib import ExitStack

F32 = mybir.dt.float32
F32R = mybir.dt.float32r
ACT = mybir.ActivationFunctionType
ALU = mybir.AluOpType
AXX = mybir.AxisListType.X

P = 128
D = 1024
KT = D // P
SEQ = 1024
DB, DS = 8, 4
NS = DB * DS
T = SEQ + NS
NT = 3
TT = T // NT
HD = 64
PAIRS = 8
RT = 26
GROUPS, HPG = 3, 4
DIL = (1, 4, 16)
STEP = (1, 4, 8)
AW = HPG * HD
BL = 128
NB = SEQ // BL
C = 64
QC = 4
QUADS = SEQ // (C * QC)
QT = QC * C
TQ = T // QUADS
FILL = {"start": 5, "masks": 2, "G1": 1, "G": 1, "inverse": 3, "rhs": 1, "u": 1}
LEVELS = 6
SLEVELS = 2
FFQ = 8
FFT = 4 * KT // FFQ
EPS, LNX_EPS = 1e-6, 64e-5
DECAY = 0.6065306597126334
NEG = -1e30
NCACHE = 128
SK = NCACHE + DS
STG = AW + 2 * HPG

VEC = {}
_at = 0
for _n, _w in (("norm_mix", KT), ("norm_mlp", KT), ("norm_ple", KT), ("norm_final", KT), ("shift_mu", RT),
               ("decay_w0", KT), ("aaa_a0", KT), ("k_k", KT), ("k_a", KT), ("r_k", KT), ("lnx_w", KT), ("lnx_b", KT)):
    VEC[_n] = _at
    _at += _w
NVEC = _at

def _columns(widths):
    out, at = {}, 0
    for n, w in widths:
        out[n] = (at, at + w)
        at += w
    return out, at


CST, NCST = _columns([("ident", P), ("ident2", HD), ("ones", P), ("ones2", P), ("gram", P), ("gram_s", P), ("level", LEVELS * HD),
                      ("reset", T), ("tok8", DB), ("level0_t", HD), ("eps", 1), ("lnx_eps", 1)])
ATT, NATT = _columns([("band", 2 * BL), ("pairs", BL), ("place", 2 * NS * 32), ("fresh", GROUPS * SK), ("own8", DB)])
WPAIR = 3 * KT * P + 2 * P
WMIX = (3 * KT + 2) * P
WQK, WKV = 3 * KT * P, KT * P + KT * AW
WPLE = (KT + 2) * P


class Steps:

    def __init__(self, sem, names, ahead=1):
        self.sem, self.names, self.at, self.ahead, self.first = sem, list(names), 0, ahead, 0
        assert len(set(self.names)) == len(self.names)

    def begin(self, eng):
        eng.sem_inc(self.sem, self.ahead * len(self.names))

    def done(self, name, ins):
        assert self.names[self.at % len(self.names)] == name, (name, self.names[self.at % len(self.names)])
        self.at += 1
        ins.then_inc(self.sem, 1)

    def wait(self, eng, name, turn):
        eng.wait_ge(self.sem, turn * len(self.names) + ((self.first + self.ahead) * len(self.names) + self.names.index(name) + 1))


def thirds(tile):
    return tile.rearrange("p (n c) -> p n c", n=NT)


def product(nc, acc, w, x, kt, width=None):
    for k in range(kt):
        for n in range(NT):
            last = nc.tensor.matmul(acc[:, n, 0:TT], w[:, k, :], x[:, k, n * TT:(n + 1) * TT], start=k == 0, stop=k == kt - 1)
    return last


def load_all(nc, sem, pairs):
    with nc.Block() as block:
        @block.sync
        def _(sp):
            for n, (dst, src) in enumerate(pairs):
                sp.dma_start(dst, src).then_inc(sem, 16)
            sp.wait_ge(sem, 16 * len(pairs))


def split_product(nc, acc, w, x, kt):
    (w_hi, w_lo), (x_hi, x_lo) = w, x
    for k in range(kt):
        for a, b in ((w_hi, x_hi), (w_hi, x_lo), (w_lo, x_hi)):
            for n in range(NT):
                last = nc.tensor.matmul(acc[:, n, 0:TT], a[:, k, :], b[:, k, n * TT:(n + 1) * TT], start=k == 0 and b is x_hi and a is w_hi, stop=k == kt - 1 and a is w_lo)
    return last


def start_loads(nc, loads):
    with nc.Block() as block:
        @block.sync
        def _(sp):
            for dst, src, sem in loads:
                sp.dma_start(dst, src).then_inc(sem, 16)


def rms_norm(nc, name, x, gain, cst, out, psum, ctx_outer, store=None, low=None):
    ones = cst[:, CST["ones"][0]:CST["ones"][1]]
    with ExitStack() as ctx:
        sq = ctx.enter_context(nc.sbuf_tensor(f"{name}_sq", [P, 2, T], F32))
        full = ctx.enter_context(nc.sbuf_tensor(f"{name}_full", [P, 2, T], F32)) if low is not None else None
        rinv = ctx.enter_context(nc.sbuf_tensor(f"{name}_rinv", [P, T], F32))
        squared = ctx_outer.enter_context(nc.semaphore(f"{name}_squared"))
        summed = ctx_outer.enter_context(nc.semaphore(f"{name}_summed"))
        root = ctx_outer.enter_context(nc.semaphore(f"{name}_root"))
        high_done, low_done = (ctx_outer.enter_context(nc.semaphore(f"{name}_{n}_done")) for n in ("high", "low"))
        normed = ctx_outer.enter_context(nc.semaphore(f"{name}_normed"))
        stored = ctx_outer.enter_context(nc.semaphore(f"{name}_stored"))
        with nc.Block() as block:
            @block.scalar
            def _(act):
                for k in range(KT):
                    if k >= 2:
                        act.wait_ge(summed, k - 1)
                    nc.scalar.activation(sq[:, k % 2, :], x[:, k, :], ACT.Square).then_inc(squared, 1)
                act.wait_ge(summed, KT)
                nc.scalar.activation(thirds(rinv[:, :]), psum[:, 0:NT, 0:TT], ACT.Ln, scale=1.0 / D, bias=cst[:, CST["eps"][0]:CST["eps"][1]]).then_inc(root, 1)
                act.wait_ge(root, 1)
                nc.scalar.activation(rinv[:, :], rinv[:, :], ACT.Exp, scale=-0.5).then_inc(root, 1)
                if low is not None:
                    for k in range(KT):
                        act.wait_ge(normed, k + 1)
                        nc.scalar.activation(out[:, k, :], full[:, k % 2, :], ACT.Copy).then_inc(high_done, 1)

            @block.tensor
            def _(pe):
                for k in range(KT):
                    pe.wait_ge(squared, k + 1)
                    for n in range(NT):
                        last = nc.tensor.matmul(psum[:, n, 0:TT], ones, sq[:, k % 2, n * TT:(n + 1) * TT], start=k == 0, stop=k == KT - 1)
                    last.then_inc(summed, 1)

            @block.vector
            def _(vec):
                vec.wait_ge(root, 2)
                for k in range(KT):
                    if low is None:
                        nc.vector.scalar_tensor_tensor(out[:, k, :], x[:, k, :], gain[:, k:k + 1], rinv[:, :], ALU.mult, ALU.mult).then_inc(normed, 1)
                        continue
                    if k >= 2:
                        vec.wait_ge(low_done, k - 1)
                    nc.vector.scalar_tensor_tensor(full[:, k % 2, :], x[:, k, :], gain[:, k:k + 1], rinv[:, :], ALU.mult, ALU.mult).then_inc(normed, 1)
                    for m in ([k - 1] if k else []) + ([k] if k == KT - 1 else []):
                        vec.wait_ge(high_done, m + 1)
                        nc.vector.tensor_tensor(low[:, m, :], full[:, m % 2, :], out[:, m, :].bitcast(F32), ALU.subtract).then_inc(low_done, 1)

            if store is not None:
                @block.sync
                def _(sp):
                    for k in range(KT):
                        sp.wait_ge(normed, k + 1)
                        sp.dma_start(store[:, k, :], out[:, k, :]).then_inc(stored, 16)
                    sp.wait_ge(stored, 16 * KT)


def dilated(tile, g, first, n, blocks=None):
    if g == 0:
        return tile[:, bass.ds(first * BL, n)]
    rows = tile.rearrange("p (i r) -> p r i", r=STEP[g])
    lo = blocks * BL if g == 1 else 0
    return rows[:, bass.ds(first, 1), lo:lo + n].rearrange("p a b -> p (a b)")


def attention_projection(nc, top, g, hT, wa, wb, wa_in, wb_in, tables_in, psum, qT, kT, vtok, vnew, k_out, v_out):
    with ExitStack() as ctx:
        sem = lambda n: top.enter_context(nc.semaphore(f"{n}{g}"))
        full, evac, v_full, v_evac, stored = (sem(n) for n in ("qk_full", "qk_evac", "v_full", "v_evac", "kv_stored"))
        with nc.Block() as block:
            @block.sync
            def _(sp):
                sp.wait_ge(tables_in, 16)
                sp.wait_ge(evac, 4)
                sp.dma_start(k_out, kT[:, :, :]).then_inc(stored, 16)
                sp.wait_ge(v_evac, NB + 1)
                sp.dma_start(v_out, vtok[:, :, :]).then_inc(stored, 16)
                sp.wait_ge(stored, 32)

            @block.tensor
            def _(pe):
                wk = wa[:, :].rearrange("p (k c) -> p k c", k=KT)
                wk1 = wb[:, 0:KT * P].rearrange("p (k c) -> p k c", k=KT)
                wv = wb[:, KT * P:].rearrange("p (k c) -> p k c", k=KT)
                pe.wait_ge(wa_in, 16 * g + 16)
                for i in range(4):
                    if i >= 2:
                        pe.wait_ge(evac, i - 1)
                    if i == 3:
                        pe.wait_ge(wb_in, 16 * g + 16)
                    w = wk[:, :, i * P:(i + 1) * P] if i < 3 else wk1
                    product(nc, psum[:, 3 * (i % 2):3 * (i % 2) + 3, :], w, hT, KT).then_inc(full, 1)
                for b in range(NB + 1):
                    if b >= 2:
                        pe.wait_ge(v_evac, b - 1)
                    for k in range(KT):
                        if b == NB:
                            rows, toks = NS, hT[:, k, SEQ:T]
                        else:
                            rows = BL
                            toks = dilated(hT[:, k, 0:SEQ], g, (b, b // 2, b)[g], BL, b % 2)
                        last = nc.tensor.matmul(psum[0:rows, 6 + b % 2, 0:AW], toks, wv[:, k, :], start=k == 0, stop=k == KT - 1)
                    last.then_inc(v_full, 1)

            @block.scalar
            def _(act):
                for i in range(4):
                    act.wait_ge(full, i + 1)
                    dst = (qT if i < 2 else kT)[:, i % 2, :]
                    nc.scalar.activation(thirds(dst), psum[:, 3 * (i % 2):3 * (i % 2) + 3, 0:TT], ACT.Copy, scale=HD ** -0.5 if i < 2 else 1.0).then_inc(evac, 1)

            @block.vector
            def _(vec):
                for b in range(NB + 1):
                    vec.wait_ge(v_full, b + 1)
                    dst, rows = (vnew[:, g, :], NS) if b == NB else (vtok[:, b, :], BL)
                    nc.vector.tensor_copy(dst, psum[0:rows, 6 + b % 2, 0:AW]).then_inc(v_evac, 1)


def prompt_counts(nc, top):
    sem = lambda n: top.enter_context(nc.semaphore(f"att_{n}"))
    names = {"pool": ["q0", "q1"], "score": ["scores"], "pe": ["pt", "pv"], "vec": ["mask", "max"], "out": ["o"], "act": ["e0", "e1", "e2", "e3", "pt"]}
    return [Steps(sem(n), names[n], ahead=2) for n in names], sem("zero"), [sem(f"stored{s}") for s in range(2)]


def attention_prompt(nc, top, g, counts, psum, qT, kT, vtok, att, ident, scratch, prefetch):
    with ExitStack() as ctx:
        sb = lambda n, *s: ctx.enter_context(nc.sbuf_tensor(f"{n}{g}", [P, *s], F32))
        qz, stage = sb("qz", 2, 2, 2, BL), sb("stage", 2, STG)
        sc, ex, pt = sb("sc", HPG, 2 * BL), sb("ex", HPG, 2 * BL), sb("pt", HPG, 2, BL)
        S = [psum[:, n:n + 2, :].rearrange("p n (h k) -> p (n h) k", h=2) for n in (0, 2)]
        PT = psum[:, 4:6, :].rearrange("p n (h b k) -> p (n h) b k", h=2, b=2)
        O = psum[:, 6, 0:AW]
        (pool_s, score_s, pe_s, vec_s, out_s, act_s), zero, stored = counts
        for each in counts[0]:
            each.first = g * NB

        def turns(eng, unit):
            def run(t, half_t, parity):
                first = half_t if g == 1 else t
                both = {0: not (isinstance(t, int) and t == 0), 1: parity == 1, 2: False}[g]
                unit(t, first, both, parity, half_t)

            if g == 0:
                run(0, 0, 0)
                with eng.Fori(0, NB // 2 - 1) as i:
                    run(2 * i + 1, i, 1)
                    run(2 * i + 2, i + 1, 0)
                run(NB - 1, NB // 2 - 1, 1)
            else:
                with eng.Fori(0, NB // 2) as i:
                    run(2 * i, i, 0)
                    run(2 * i + 1, i, 1)

        def turns_ahead(eng, first_part, rest):
            def run(part, t, half_t, parity):
                both = {0: not (isinstance(t, int) and t == 0), 1: parity == 1, 2: False}[g]
                part(t, half_t if g == 1 else t, both, parity, half_t)

            run(first_part, 0, 0, 0)
            if g == 0:
                run(first_part, 1, 0, 1)
                run(rest, 0, 0, 0)
                with eng.Fori(0, NB // 2 - 1) as i:
                    run(first_part, 2 * i + 2, i + 1, 0)
                    run(rest, 2 * i + 1, i, 1)
                    run(first_part, 2 * i + 3, i + 1, 1)
                    run(rest, 2 * i + 2, i + 1, 0)
            else:
                with eng.Fori(0, NB // 2 - 1) as i:
                    run(first_part, 2 * i + 1, i, 1)
                    run(rest, 2 * i, i, 0)
                    run(first_part, 2 * i + 2, i + 1, 0)
                    run(rest, 2 * i + 1, i, 1)
                run(first_part, NB - 1, NB // 2 - 1, 1)
                run(rest, NB - 2, NB // 2 - 1, 0)
            run(rest, NB - 1, NB // 2 - 1, 1)

        with nc.Block() as block:
            @block.gpsimd
            def _(pool):
                if g == 0:
                    pool_s.begin(pool)
                pool.wait_ge(zero, g + 1)

                def unit(t, f, both, s, k):
                    score_s.wait(pool, "scores", t - 2)
                    for h in range(2):
                        rows = slice(h * HD, (h + 1) * HD)
                        src = qT[rows, :, 0:SEQ]
                        if g == 0:
                            src = src[:, :, bass.ds(f * BL, BL)]
                            dst = qz[rows, s, :, h, :]
                        elif g == 1:
                            src = src.rearrange("p a (i r) -> p a r i", r=STEP[1])[:, :, bass.ds(f, 1), (BL if both else 0):(2 * BL if both else BL)].rearrange("p a o i -> p a (o i)")
                            dst = qz[rows, s, :, h, :]
                        else:
                            src = src.rearrange("p a (i r) -> p a r i", r=STEP[2])[:, :, bass.ds(f, 1), :].rearrange("p a o i -> p a (o i)")
                            dst = qz[rows, s, :, h, :]
                        pool_s.done(f"q{h}", nc.gpsimd.tensor_copy(dst, src))
                turns(pool, unit)

            @block.tensor
            def _(pe):
                if g == 0:
                    pe_s.begin(pe)
                if g == 0:
                    score_s.begin(pe)

                def scores(t, f, both, s, k):
                    nk = 2 * BL if both else BL
                    pool_s.wait(pe, "q1", t)
                    vec_s.wait(pe, "mask", t - 2)
                    for h in range(HPG):
                        if g == 0:
                            keys = dilated(kT[:, h // 2, 0:SEQ], 0, f - 1 if both else f, nk)
                        elif g == 1:
                            keys = dilated(kT[:, h // 2, 0:SEQ], 1, f, nk, 0)
                        else:
                            keys = dilated(kT[:, h // 2, 0:SEQ], 2, f, nk)
                        last = nc.tensor.matmul(S[s][:, h, 0:nk], qz[:, s, h // 2, h % 2, :], keys, start=True, stop=True)
                    score_s.done("scores", last)

                def rest(t, f, both, s, k):
                    nk = 2 * BL if both else BL
                    act_s.wait(pe, "e3", t)
                    act_s.wait(pe, "pt", t - 1)
                    for h in range(HPG):
                        for b in range(nk // BL):
                            last = nc.tensor.transpose(PT[:, h, b, :], ex[:, h, b * BL:(b + 1) * BL], ident)
                    pe_s.done("pt", last)
                    act_s.wait(pe, "pt", t)
                    out_s.wait(pe, "o", t - 1)
                    for h in range(HPG):
                        for b in range(nk // BL):
                            blk = (t - 1 + b) if both else t
                            v = vtok[:, bass.ds(blk, 1), h * HD:(h + 1) * HD].rearrange("p o c -> p (o c)")
                            last = nc.tensor.matmul(O[:, h * HD:(h + 1) * HD], pt[:, h, b, :], v, start=b == 0, stop=b == nk // BL - 1)
                    pe_s.done("pv", last)
                turns_ahead(pe, scores, rest)

            @block.vector
            def _(vec):
                if g == 0:
                    vec_s.begin(vec)
                if g == 0:
                    out_s.begin(vec)
                nc.vector.memset(qz[:, :, :, :, :], 0.0).then_inc(zero, 1)

                def maxima(t, f, both, s, k):
                    nk = 2 * BL if both else BL
                    m = att("pairs") if g == 2 else att("band")[:, 2 * BL - nk:]
                    score_s.wait(vec, "scores", t)
                    act_s.wait(vec, "e3", t - 1)
                    vec_s.done("mask", nc.vector.tensor_tensor(sc[:, :, 0:nk], S[s][:, :, 0:nk], m[:, None, :].to_broadcast([P, HPG, nk]), ALU.add))
                    vec_s.wait(vec, "mask", t)
                    vec.wait_ge(stored[s], (k + g * (NB // 2)) * 16)
                    vec_s.done("max", nc.vector.tensor_reduce(stage[:, s, AW:AW + HPG], sc[:, :, 0:nk], AXX, ALU.max, negate=True))

                def values(t, f, both, s, k):
                    pe_s.wait(vec, "pv", t)
                    out_s.done("o", nc.vector.tensor_copy(stage[:, s, 0:AW], O))
                turns_ahead(vec, maxima, values)

            @block.scalar
            def _(act):
                if g == 0:
                    act_s.begin(act)

                def unit(t, f, both, s, k):
                    nk = 2 * BL if both else BL
                    vec_s.wait(act, "max", t)
                    pe_s.wait(act, "pt", t - 1)
                    for h in range(HPG):
                        act_s.done(f"e{h}", nc.scalar.activation(ex[:, h, 0:nk], sc[:, h, 0:nk], ACT.Exp, bias=stage[:, s, AW + h:AW + h + 1], accum_out=stage[:, s, AW + HPG + h:AW + HPG + h + 1]))
                    pe_s.wait(act, "pt", t)
                    act_s.done("pt", nc.scalar.activation(pt[:, :, 0:nk // BL, :], PT[:, :, 0:nk // BL, :], ACT.Copy))
                turns(act, unit)

            @block.sync
            def _(sp):
                for dst, src, loaded in prefetch:
                    sp.dma_start(dst, src).then_inc(loaded, 16)
                rows = scratch.rearrange("(i r) c -> r i c", r=STEP[g])

                def unit(t, f, both, s, k):
                    out_s.wait(sp, "o", t)
                    act_s.wait(sp, "e3", t)
                    if g == 0:
                        dst = scratch[bass.ds(f * BL, BL), g * STG:(g + 1) * STG]
                    elif g == 1:
                        dst = rows[bass.ds(f, 1), (BL if both else 0):(2 * BL if both else BL), g * STG:(g + 1) * STG].rearrange("o i c -> (o i) c")
                    else:
                        dst = rows[bass.ds(f, 1), :, g * STG:(g + 1) * STG].rearrange("o i c -> (o i) c")
                    sp.dma_start(dst, stage[:, s, :]).then_inc(stored[s], 16)
                turns(sp, unit)
                for s in range(2):
                    sp.wait_ge(stored[s], 16 * (NB // 2) * (g + 1))


def sample_scores(nc, top, g, psum, qT, kT, att, K, k_in, scores):
    tt = 1 if g == 0 else DS
    with ExitStack() as ctx:
        Q = ctx.enter_context(nc.sbuf_tensor(f"sq{g}", [P, 2, NS, 32], F32))
        sem = lambda n: top.enter_context(nc.semaphore(f"samp_{n}{g}"))
        k_new, q_up, full, done = (sem(n) for n in ("k_new", "q_up", "full", "done"))
        with nc.Block() as block:
            @block.gpsimd
            def _(pool):
                for hp in range(2):
                    src = kT[:, hp, SEQ:T].rearrange("p (b t) -> p b t", b=DB)[:, :, None, :].to_broadcast([P, DB, tt, DS])
                    nc.gpsimd.tensor_copy(K[:, hp, :, :, NCACHE:SK], src).then_inc(k_new, 1)

            @block.vector
            def _(vec):
                place = att("place").rearrange("p (a t c) -> p a t c", a=2, t=NS)
                for hp in range(2):
                    nc.vector.tensor_tensor(Q[:, hp, :, :], qT[:, hp, SEQ:T][:, :, None].to_broadcast([P, NS, 32]), place[:, hp, :, :], ALU.mult).then_inc(q_up, 1)
                vec.wait_ge(full, 1)
                nc.vector.tensor_tensor(scores[:, g, :], psum[:, 0, 0:SK], att("fresh")[:, g * SK:(g + 1) * SK], ALU.add).then_inc(done, 1)

            @block.tensor
            def _(pe):
                pe.wait_ge(k_in, 32 * g + 32)
                pe.wait_ge(k_new, 2)
                pe.wait_ge(q_up, 2)
                for b in range(DB):
                    for t in range(DS):
                        for hp in range(2):
                            last = nc.tensor.matmul(psum[32 * (b // 2):32 * (b // 2) + 32, 0, 0:SK], Q[:, hp, DS * b + t, :], K[:, hp, b, t % tt, :],
                                                    start=b % 2 == 0 and t == 0 and hp == 0, stop=b % 2 == 1 and t == DS - 1 and hp == 1)
                last.then_inc(full, 1)


def sample_attention(nc, top, psum, att, ident, scores, vnew, V, v_in, attn):
    with ExitStack() as ctx:
        sb = lambda n, s: ctx.enter_context(nc.sbuf_tensor(n, s, F32))
        stat = sb("sa_stat", [P, 4])
        pn = sb("sa_new", [P, GROUPS, DB, DS])
        pct = sb("sa_pct", [P, GROUPS, P])
        pnt = sb("sa_pnt", [NS, GROUPS, P])
        sem = lambda n: top.enter_context(nc.semaphore(f"sa_{n}"))
        chain, exped, turned, copied, summed, placed = (sem(n) for n in ("chain", "exped", "turned", "copied", "summed", "placed"))
        flat = scores[:, :, :].rearrange("p g k -> p (g k)")
        with nc.Block() as block:
            @block.vector
            def _(vec):
                nc.vector.tensor_reduce(stat[:, 0:1], flat, AXX, ALU.max, negate=True).then_inc(chain, 1)
                vec.wait_ge(exped, 1)
                nc.vector.reciprocal(stat[:, 2:3], stat[:, 1:2]).then_inc(chain, 1)
                vec.wait_ge(chain, 2)
                nc.vector.tensor_scalar(flat, flat, stat[:, 2:3], None, ALU.mult).then_inc(chain, 1)
                vec.wait_ge(chain, 3)
                for g in range(GROUPS):
                    nc.vector.tensor_tensor(pn[:, g, :, :], scores[:, g, NCACHE:SK][:, None, :].to_broadcast([P, DB, DS]), att("own8")[:, :, None].to_broadcast([P, DB, DS]), ALU.mult).then_inc(chain, 1)
                vec.wait_ge(turned, 1)
                nc.vector.tensor_copy(pct[:, :, :], psum[:, 0, 0:GROUPS * P].rearrange("p (g r) -> p g r", g=GROUPS)).then_inc(copied, 1)
                nc.vector.tensor_copy(pnt[:, :, :], psum[0:NS, 1, 0:GROUPS * P].rearrange("p (g r) -> p g r", g=GROUPS)).then_inc(copied, 1)

            @block.scalar
            def _(act):
                act.wait_ge(chain, 1)
                nc.scalar.activation(flat, flat, ACT.Exp, bias=stat[:, 0:1], accum_out=stat[:, 1:2]).then_inc(exped, 1)
                act.wait_ge(summed, 1)
                for hp in range(2):
                    for h in range(2):
                        rows = slice(h * HD, (h + 1) * HD)
                        src = psum[rows, 2 + hp, 0:P].rearrange("p (n h) -> p h n", h=HPG)[:, 2 * hp + h, :]
                        nc.scalar.activation(attn[rows, hp, SEQ:T], src, ACT.Copy).then_inc(placed, 1)

            @block.tensor
            def _(pe):
                pe.wait_ge(chain, 6)
                for g in range(GROUPS):
                    nc.tensor.transpose(psum[:, 0, g * P:(g + 1) * P], scores[:, g, 0:NCACHE], ident)
                    last = nc.tensor.transpose(psum[0:NS, 1, g * P:(g + 1) * P], pn[:, g, :, :], ident)
                last.then_inc(turned, 1)
                pe.wait_ge(copied, 2)
                pe.wait_ge(v_in, 16 * GROUPS)
                for hp in range(2):
                    for g in range(GROUPS):
                        nc.tensor.matmul(psum[:, 2 + hp, 0:P], vnew[:, g, hp * P:(hp + 1) * P], pnt[:, g, :], start=g == 0, stop=False)
                    for b in range(DB):
                        rows = psum[:, 2 + hp, 16 * b:16 * b + 16].rearrange("p (t h) -> p t h", h=HPG)[:, :, 2 * hp:2 * hp + 2]
                        probs = pct[:, 0, 16 * b:16 * b + 16].rearrange("p (t h) -> p t h", h=HPG)[:, :, 2 * hp:2 * hp + 2]
                        nc.tensor.matmul(rows, V[0][:, b, 0, hp * P:(hp + 1) * P], probs, start=False, stop=False)
                        for g in (1, 2):
                            for t in range(DS):
                                r0 = HPG * (DS * b + t) + 2 * hp
                                last = nc.tensor.matmul(psum[:, 2 + hp, r0:r0 + 2], V[g][:, b, t, hp * P:(hp + 1) * P], pct[:, g, r0:r0 + 2],
                                                        start=False, stop=b == DB - 1 and g == 2 and t == DS - 1)
                last.then_inc(summed, 1)


def combine_groups(nc, top, psum, ident, scratch, attn, prefetch):
    with ExitStack() as ctx:
        sb = lambda n, *s: ctx.enter_context(nc.sbuf_tensor(n, [P, NB, *s], F32))
        rows = sb("cg_rows", GROUPS, STG)
        w, wd, nmin, den = sb("cg_w", GROUPS, HPG), sb("cg_wd", GROUPS, HPG), sb("cg_min", HPG), sb("cg_den", HPG)
        sem = lambda n: top.enter_context(nc.semaphore(f"cg_{n}"))
        loaded, chain, exped, summed, turned, placed = (sem(n) for n in ("loaded", "chain", "exped", "summed", "turned", "placed"))
        with nc.Block() as block:
            @block.sync
            def _(sp):
                sp.dma_start(rows[:, :, :, :].rearrange("p n g c -> p n (g c)"), scratch.rearrange("(n p) c -> p n c", p=P)).then_inc(loaded, 16)
                for dst, src, sem_in in prefetch:
                    sp.dma_start(dst, src).then_inc(sem_in, 16)

            @block.vector
            def _(vec):
                nm, dn = rows[:, :, :, AW:AW + HPG], rows[:, :, :, AW + HPG:STG]
                vec.wait_ge(loaded, 16)
                nc.vector.tensor_tensor(nmin[:, :, :], nm[:, :, 0, :], nm[:, :, 1, :], ALU.min).then_inc(chain, 1)
                vec.wait_ge(chain, 1)
                nc.vector.tensor_tensor(nmin[:, :, :], nmin[:, :, :], nm[:, :, 2, :], ALU.min).then_inc(chain, 1)
                vec.wait_ge(chain, 2)
                nc.vector.tensor_tensor(w[:, :, :, :], nmin[:, :, None, :].to_broadcast([P, NB, GROUPS, HPG]), nm, ALU.subtract).then_inc(chain, 1)
                vec.wait_ge(exped, 1)
                nc.vector.tensor_tensor(wd[:, :, :, :], w[:, :, :, :], dn, ALU.mult).then_inc(chain, 1)
                vec.wait_ge(chain, 4)
                nc.vector.tensor_reduce(den[:, :, :], wd[:, :, :, :].rearrange("p n g h -> p n h g"), AXX, ALU.add).then_inc(chain, 1)
                vec.wait_ge(chain, 5)
                nc.vector.reciprocal(den[:, :, :], den[:, :, :]).then_inc(chain, 1)
                vec.wait_ge(chain, 6)
                nc.vector.tensor_tensor(w[:, :, :, :], w[:, :, :, :], den[:, :, None, :].to_broadcast([P, NB, GROUPS, HPG]), ALU.mult).then_inc(chain, 1)
                vec.wait_ge(chain, 7)
                for n in range(NB):
                    vals = rows[:, n, :, 0:AW].rearrange("p g (h e) -> p g h e", h=HPG)
                    nc.vector.tensor_tensor(vals, vals, w[:, n, :, :][:, :, :, None].to_broadcast([P, GROUPS, HPG, HD]), ALU.mult).then_inc(chain, 1)
                    vec.wait_ge(chain, 8 + 2 * n)
                    nc.vector.tensor_tensor(rows[:, n, 0, 0:AW], rows[:, n, 0, 0:AW], rows[:, n, 1, 0:AW], ALU.add).then_inc(chain, 1)
                    vec.wait_ge(chain, 9 + 2 * n)
                    nc.vector.tensor_tensor(rows[:, n, 0, 0:AW], rows[:, n, 0, 0:AW], rows[:, n, 2, 0:AW], ALU.add).then_inc(summed, 1)

            @block.scalar
            def _(act):
                act.wait_ge(chain, 3)
                nc.scalar.activation(w[:, :, :, :], w[:, :, :, :], ACT.Exp).then_inc(exped, 1)
                for n in range(NB):
                    act.wait_ge(turned, n + 1)
                    nc.scalar.activation(attn[:, :, n * BL:(n + 1) * BL], psum[:, n % 2, 0:2 * BL].rearrange("p (a t) -> p a t", a=2), ACT.Copy).then_inc(placed, 1)

            @block.tensor
            def _(pe):
                for n in range(NB):
                    pe.wait_ge(summed, n + 1)
                    if n >= 2:
                        pe.wait_ge(placed, n - 1)
                    for hp in range(2):
                        last = nc.tensor.transpose(psum[:, n % 2, hp * BL:(hp + 1) * BL], rows[:, n, 0, hp * P:(hp + 1) * P], ident)
                    last.then_inc(turned, 1)




def rwkv_lora_inputs(nc, top, hT, w_lora, shift0, vec_sb, mu1, cst, psum, low, shift_sb):
    with ExitStack() as ctx:
        sb = lambda n, s: ctx.enter_context(nc.sbuf_tensor(n, s, F32))
        w = sb("lora_w", [P, KT, 2 * P])
        raw = sb("lora_raw", [P, 2, 1 + T])
        part = sb("lora_part", [P, 2, T])
        sem = lambda n: top.enter_context(nc.semaphore(n))
        loaded, full, evac, lerp, kept, zero, done = (sem(f"lora_{n}") for n in ("loaded", "full", "evac", "lerp", "kept", "zero", "done"))
        with nc.Block() as block:
            @block.sync
            def _(sp):
                sp.dma_start(w[:, :, :], w_lora).then_inc(loaded, 16)

            @block.tensor
            def _(pe):
                pe.wait_ge(loaded, 16)
                for i in range(2):
                    product(nc, psum[:, 3 * i:3 * i + 3, :], w[:, :, i * P:(i + 1) * P], hT, KT).then_inc(full, 1)

            @block.scalar
            def _(act):
                for i in range(2):
                    acc = psum[:, 3 * i:3 * i + 3, 0:TT]
                    act.wait_ge(full, i + 1)
                    nc.scalar.activation(thirds(raw[:, i, 1:1 + T]), acc, ACT.Copy).then_inc(evac, 1)
                    nc.scalar.activation(thirds(part[:, i, :]), acc, ACT.Copy, scale=mu1[:, 24 + i:25 + i]).then_inc(evac, 1)
                act.wait_ge(lerp, 2)
                nc.scalar.activation(low[0:HD, 0, :], low[0:HD, 0, :], ACT.Tanh).then_inc(done, 1)
                act.wait_ge(lerp, 4)
                nc.scalar.activation(low[:, 1, :], low[:, 1, :], ACT.Sigmoid).then_inc(done, 1)

            @block.gpsimd
            def _(pool):
                for i in range(2):
                    pool.wait_ge(evac, 2 * i + 1)
                    nc.gpsimd.tensor_copy(shift_sb[:, 24 + i, 0:1], raw[:, i, SEQ:SEQ + 1]).then_inc(kept, 1)
                    nc.gpsimd.tensor_copy(shift_sb[:, 24 + i, 1:9], raw[:, i, SEQ + DS:1 + T:DS]).then_inc(kept, 1)

            @block.vector
            def _(vec):
                nc.vector.memset(raw[:, :, 0:1], 0.0).then_inc(zero, 1)
                vec.wait_ge(zero, 1)
                for i in range(2):
                    mu = vec_sb[:, VEC["shift_mu"] + 24 + i:VEC["shift_mu"] + 25 + i]
                    vec.wait_ge(evac, 2 * i + 2)
                    nc.vector.scalar_tensor_tensor(low[:, i, :], raw[:, i, 0:T], mu, part[:, i, :], ALU.mult, ALU.add).then_inc(lerp, 1)
                    vec.wait_ge(lerp, 2 * i + 1)
                    nc.vector.scalar_tensor_tensor(low[:, i, SEQ:T:DS], shift0[:, 24 + i, :], mu, part[:, i, SEQ:T:DS], ALU.mult, ALU.add).then_inc(lerp, 1)


def rwkv_pairs(nc, top, hT, w_pair, shift0, s0T, vec_sb, mu1, ka1, cst, psum, low, shift_sb, out, wkv_p, wkv_s):
    with ExitStack() as ctx:
        sb = lambda n, *s: ctx.enter_context(nc.sbuf_tensor(n, [P, *s], F32))
        w3, lora_w, gate_w = sb("rkv_w", KT, 3 * P), sb("lora2_w", P), sb("gate_w", P)
        raws = [sb(f"raw_{z}", 1 + T) for z in "rkv"]
        bonus, rinv, norm, centred, bias = sb("bonus", T), sb("rinv", T), sb("norm", T), sb("centred", T), sb("bias", 2)
        zr, zk, zv, sg, cs, pp, pr, av, kkn = (sb(n, T) for n in ("zr", "zk", "zv", "sg", "cs", "pp", "pr", "av", "kkn"))
        mixed = (zr, zk, zv)
        H = [sb("H0", QC, P), sb("H1", QC, P)]
        BK = sb("BK", QC, 3, C)
        KB = sb("KB", QC, 2, C)
        LT = sb("LT", QC, P)
        RB = sb("RB", QC, 2, C)
        Gs, Gd, X, XT, XTd = sb("Gs", QC, C), sb("Gd", QC, P), sb("X", QC, C), sb("XT", QC, C), sb("XTd", QC, P)
        SU = sb("SU", QC, 2, 2, C)
        SV, UV = SU[:, :, 0, :, :], SU[:, :, 1, :, :]
        rhs, PC = sb("rhs", QC, C), sb("PC", QC)
        Vs, SP = rhs, Gs[:, 0, :]
        SVs, UVx, Rx = sb("SVs", 2, DB, HD), sb("UVx", 2, DB, HD), sb("Rx", DB, HD)
        ident, ident2 = cst("ident"), cst("ident2")
        ones2, gram, gram_s, reset = cst("ones2"), cst("gram"), cst("gram_s"), cst("reset")
        level = cst("level").rearrange("p (l c) -> p l c", l=LEVELS)
        tok8 = cst("tok8")
        half = (slice(0, HD), slice(HD, P))
        accA, accB = psum[:, 0:3, :], psum[:, 3:6, :]
        bank = lambda i: psum[:, i, :]
        G = [bank(0).rearrange("p (c t) -> p c t", c=QC), bank(1).rearrange("p (c t) -> p c t", c=QC)]
        TK = bank(2).rearrange("p (c h t) -> p c h t", c=QC, h=2)
        VT = bank(3)[:, QT:2 * QT].rearrange("p (c t) -> p c t", c=QC)
        Y = bank(3)[:, 0:QT].rearrange("p (c t) -> p c t", c=QC)
        inv = [m.rearrange("p (c t) -> p c t", c=QC) for m in (bank(4)[:, 0:QT], bank(4)[:, QT:2 * QT], bank(5)[:, 0:QT])]
        side = lambda i: bank(6 + i % 2)[:, 0:TT]
        ahead = [bank(6)[:, 0:TQ], bank(7)[:, 0:TQ], bank(6)[:, 0:TQ]]
        RH, UU, SS = inv

        n_sem = [0]

        def steps(name, names):
            n_sem[0] += 1
            return Steps(top.enter_context(nc.semaphore(name)), names)

        zero = top.enter_context(nc.semaphore("rwkv_zero"))
        w3_in, lw_in, gw_in = (top.enter_context(nc.semaphore(n)) for n in ("rkv_w_in", "lora2_w_in", "gate_w_in"))
        s0_in = top.enter_context(nc.semaphore("s0_in"))
        sp_out, ss_out = (top.enter_context(nc.semaphore(f"wkv_{n}_out")) for n in ("prompt", "sample"))
        pe_n = steps("pe_next", ["r", "k", "v"])
        act_n = steps("act_next", ["r", "k", "v"])
        tri = lambda n: [f"{n}{i}" for i in range(NT)]
        pe_p = steps("pe_pair", [*tri("decay"), *tri("aaa"), *tri("ksum")])
        act_p = steps("act_pair", ["bias_w", "bias_a", "part_k", "part_r", *tri("sig_w"), "part_v", *tri("sig_a"), "ksq", "t1", "ln", "rn", "pp", "pr", "pi"])
        vec_p = steps("vec_pair", ["lerp_k", "cum", "before", *tri("nmax"), "lerp_r", "lerp_v", "s_zero0", "s_zero1", "kkn", "bb", "kmod"])
        pool_p = steps("pool_pair", [f"{m}_{z}" for z in "krv" for m in ("keep", "keep8", "first")])
        inv_pe = lambda levels: ["G0", "tk"] + [m if m == "vt" else f"{m}{i}" for i in range(1, levels) for m in (("G", "vt", "W", "WT") if i == 1 else ("G", "W", "WT")) if not (m == "W" and i == levels - 1)]
        inv_vec = lambda levels: ["g0", "x0", "xa0", "xa1", "xt0"] + [f"{m}{i}" for i in range(1, levels) for m in ("g", "x", "xt") if not (m == "x" and i == levels - 1)]
        inv_act = lambda levels, v: ["xd0_0", "xd1_0", "kb"] + [f"{m}_{i}" for i in range(1, 2) for m in ("gd0", "gd1", "xd0", "xd1")] + v + [f"{m}_{i}" for i in range(2, levels) for m in ("gd0", "gd1", "xd0", "xd1")]
        pe_q = steps("pe_quad", ["gram0", "gram1", *inv_pe(LEVELS), *[f"{m}{c}" for c in range(QC) for m in ("rhs", "u", "s", "y")]])
        vec_q = steps("vec_quad", ["r0", "r1", "a0", "a1", "pc", "l0", "l1", "m0", "m1", "rb0", "rb1",
                                   *inv_vec(LEVELS),
                                   *[f"{m}{c}" for c in range(QC) for m in ("rhs", "u0", "s0", "s1")]])
        act_q = steps("act_quad", ["vs", *inv_act(LEVELS, ["v0", "v1"]),
                                   *[f"{m}{c}" for c in range(QC) for m in ("sp0", "sp1", "u1_")], "y"])
        pool_q = steps("pool_quad", ["b", "k"])
        pe_s = steps("pe_samp", ["gram0", "gram1", *inv_pe(SLEVELS), "rhs", "u", "s", "y"])
        vec_s = steps("vec_samp", ["r0", "r1", "a0", "a1", "l0", "l1", "m0", "m1", "rb0", "rb1",
                                   *inv_vec(SLEVELS),
                                   "sel", "rhs", "u0", "ux0", "ux1", "s0", "s1", "dec"])
        act_s = steps("act_samp", ["vs", *inv_act(SLEVELS, ["sv0", "sv1", "v0", "v1"]),
                                   "u1", "y"])
        pool_s = steps("pool_samp", ["b", "k"])
        pe_o = steps("pe_post", [*tri("bonus"), "mean", "var", "gate"])
        vec_o = steps("vec_post", ["rkk", *tri("bon"), "yc", "yn", "yb", "out"])
        act_o = steps("act_post", ["sq", "ln", "rs"])
        all_steps = {"pe": [pe_n, pe_p, pe_q, pe_s, pe_o], "act": [act_n, act_p, act_q, act_s, act_o], "vec": [vec_p, vec_q, vec_s, vec_o], "pool": [pool_p, pool_q, pool_s]}

        def col(name, j):
            return vec_sb[:, bass.ds(VEC[name] + j, 1)]

        def quad_cols(tile, q):
            return tile[:, bass.ds(q * QT, QT)].rearrange("p (c t) -> p c t", c=QC)

        def cols(n):
            return slice(n * TT, (n + 1) * TT)

        with nc.Block() as block:
            @block.sync
            def _(sp):
                def rkv(j):
                    sp.dma_start(w3[:, :, :].rearrange("p k c -> p (k c)"), w_pair[bass.ds(j, 1), :, 0:3 * KT * P].rearrange("o p c -> p (o c)")).then_inc(w3_in, 16)

                def lora(j):
                    sp.dma_start(lora_w[:, :], w_pair[bass.ds(j, 1), :, 3 * KT * P:3 * KT * P + P].rearrange("o p c -> p (o c)")).then_inc(lw_in, 16)

                def pair(j):
                    pe_o.wait(sp, "gate", j - 1)
                    sp.dma_start(gate_w[:, :], w_pair[bass.ds(j, 1), :, 3 * KT * P + P:WPAIR].rearrange("o p c -> p (o c)")).then_inc(gw_in, 16)
                    vec_s.wait(sp, "s1", j - 1)
                    pe_s.wait(sp, "y", j - 1)
                    for h in range(2):
                        sp.dma_start(SVs[half[h], h, :, :], s0T[bass.ds(j, 1), half[h], :, :].rearrange("o p b v -> p (o b) v")).then_inc(s0_in, 16)
                    if not isinstance(j, int) or j < PAIRS - 1:
                        pe_p.wait(sp, "aaa2", j)
                        lora(j + 1)
                    if not isinstance(j, int):
                        pe_n.wait(sp, "v", (j + 1) * QUADS + (QUADS - 1))
                        rkv(j + 2)
                    vec_q.wait(sp, f"s1{QC - 1}", j * QUADS + (QUADS - 1))
                    for h in range(2):
                        sp.dma_start(wkv_p[bass.ds(j, 1), half[h], :].rearrange("o p v -> p (o v)"), SV[half[h], 0, h, :]).then_inc(sp_out, 16)
                    vec_s.wait(sp, "dec", j)
                    sp.dma_start(wkv_s[bass.ds(j, 1), :, :, :].rearrange("o p b v -> p (o b) v"), Rx[:, :, :]).then_inc(ss_out, 16)

                rkv(0)
                lora(0)
                pe_n.wait(sp, "v", QUADS - 1)
                rkv(1)
                with sp.Fori(0, PAIRS - 2) as j:
                    pair(j)
                for j in (PAIRS - 2, PAIRS - 1):
                    pair(j)
                sp.wait_ge(sp_out, 32 * PAIRS)
                sp.wait_ge(ss_out, 16 * PAIRS)

            @block.gpsimd
            def _(pool):
                for s in all_steps["pool"]:
                    s.begin(pool)

                def ahead_of(j):
                    for n, z in ((1, "k"), (0, "r"), (2, "v")):
                        raw = raws[n]
                        act_n.wait(pool, "v", j * QUADS + (QUADS - 1))
                        pool_p.done(f"keep_{z}", nc.gpsimd.tensor_copy(shift_sb[:, bass.ds(j + n * KT, 1), 0:1].rearrange("p a b -> p (a b)"), raw[:, SEQ:SEQ + 1]))
                        pool_p.done(f"keep8_{z}", nc.gpsimd.tensor_copy(shift_sb[:, bass.ds(j + n * KT, 1), 1:9].rearrange("p a b -> p (a b)"), raw[:, SEQ + DS:1 + T:DS]))
                        act_p.wait(pool, f"part_{z}", j)
                        pool_p.wait(pool, f"keep8_{z}", j)
                        pool_p.done(f"first_{z}", nc.gpsimd.tensor_copy(raw[:, SEQ:T:DS], shift0[:, bass.ds(j + n * KT, 1), :].rearrange("p a b -> p (a b)")))

                def pair(j, more):
                    with pool.Fori(0, QUADS) as q:
                        n = j * QUADS + q
                        act_p.wait(pool, "pi", j)
                        vec_p.wait(pool, "kmod", j)
                        pe_q.wait(pool, "tk", n - 1)
                        pe_s.wait(pool, "tk", j - 1)
                        pool_q.done("b", nc.gpsimd.tensor_tensor(BK[:, :, 0:3:2, :], quad_cols(av, q)[:, :, None, :].to_broadcast([P, QC, 2, C]), quad_cols(cs, q)[:, :, None, :].to_broadcast([P, QC, 2, C]), ALU.mult))
                        pool_q.done("k", nc.gpsimd.tensor_tensor(BK[:, :, 1, :], quad_cols(zk, q), quad_cols(cs, q), ALU.mult))
                    tail = slice(SEQ, T)
                    pe_q.wait(pool, "tk", j * QUADS + (QUADS - 1))
                    pool_s.done("b", nc.gpsimd.tensor_tensor(BK[:, 0, 0:3:2, 0:NS], av[:, None, tail].to_broadcast([P, 2, NS]), cs[:, None, tail].to_broadcast([P, 2, NS]), ALU.mult))
                    pool_s.done("k", nc.gpsimd.tensor_tensor(BK[:, 0, 1, 0:NS], zk[:, tail], cs[:, tail], ALU.mult))

                    if more:
                        ahead_of(j + 1)

                ahead_of(0)
                with pool.Fori(0, PAIRS - 1) as j:
                    pair(j, True)
                pair(PAIRS - 1, False)

            @block.scalar
            def _(act):
                for s in all_steps["act"]:
                    s.begin(act)
                def evacuate(i, m, q):
                    pe_n.wait(act, "rkv"[i], m)
                    act_n.done("rkv"[i], nc.scalar.activation(raws[i][:, bass.ds(q * TQ + 1, TQ)], ahead[i], ACT.Copy))

                with act.Fori(0, QUADS) as q:
                    for i in range(3):
                        evacuate(i, q, q)

                def ahead_of(j):
                    def part(n, z):
                        act_p.done(f"part_{z}", nc.scalar.activation(mixed[n][:, :], raws[n][:, 1:1 + T], ACT.Copy, scale=mu1[:, bass.ds(j + n * KT, 1)]))

                    act_n.wait(act, "v", j * QUADS + (QUADS - 1))
                    pool_s.wait(act, "k", j - 1)
                    vec_s.wait(act, "a1", j - 1)
                    act_p.wait(act, "sig_a2", j - 1)
                    act_p.done("bias_w", nc.scalar.activation(bias[:, 0:1], col("decay_w0", j), ACT.Copy))
                    act_p.done("bias_a", nc.scalar.activation(bias[:, 1:2], col("aaa_a0", j), ACT.Copy))
                    part(1, "k")
                    part(0, "r")
                    act_p.wait(act, "bias_a", j)
                    pe_o.wait(act, "bonus2", j - 1)
                    for n in range(NT):
                        pe_p.wait(act, f"decay{n}", j)
                        act_p.done(f"sig_w{n}", nc.scalar.activation(sg[:, cols(n)], side(1 + n), ACT.Sigmoid, bias=bias[:, 0:1]))
                    yield
                    vec_o.wait(act, "bon2", j - 1)
                    part(2, "v")
                    for n in range(NT):
                        pe_p.wait(act, f"aaa{n}", j)
                        act_p.done(f"sig_a{n}", nc.scalar.activation(av[:, cols(n)], side(n), ACT.Sigmoid, bias=bias[:, 1:2]))
                    vec_p.wait(act, "lerp_k", j)
                    vec_p.wait(act, "kkn", j - 1)
                    act_p.done("ksq", nc.scalar.activation(norm[:, :], zk[:, :], ACT.Square, scale=col("k_k", j)))
                    yield
                    vec_p.wait(act, "before", j)
                    act_p.wait(act, "sig_a2", j)
                    act_p.done("t1", nc.scalar.activation(sg[:, :], av[:, :], ACT.Identity, scale=col("k_a", j), bias=ka1[:, bass.ds(j, 1)]))
                    vec_p.wait(act, "nmax2", j)
                    act_p.done("ln", nc.scalar.activation(norm[:, :], norm[:, :], ACT.Ln))
                    act_p.wait(act, "ln", j)
                    act_p.done("rn", nc.scalar.activation(norm[:, :], norm[:, :], ACT.Exp, scale=-0.5))
                    act_p.done("pp", nc.scalar.activation(pp[:, :], pp[:, :], ACT.Exp, scale=-DECAY))
                    yield
                    vec_s.wait(act, "dec", j - 1)
                    act_p.done("pr", nc.scalar.activation(pr[:, :], cs[:, :], ACT.Exp, scale=-DECAY))
                    act_p.wait(act, "pr", j)
                    act_p.done("pi", nc.scalar.activation(cs[:, :], cs[:, :], ACT.Exp, scale=DECAY))
                    yield

                def pair(j, more):
                    piece = ahead_of(j + 1) if more else iter(())

                    def keys(st, pe_t, n, c):
                        pe_t.wait(act, "tk", n)
                        st.done("kb", nc.scalar.activation(KB[:, c, :, :], TK[:, c, :, :], ACT.Copy))

                    def values(st, pe_t, n, c, samples):
                        pe_t.wait(act, "vt", n)
                        if samples:
                            for h in range(2):
                                o = half[1 - h]
                                st.done(f"sv{h}", nc.scalar.activation(SVs[o, h, :, :], VT[o, 0, :][:, None, :].to_broadcast([HD, DB, HD]), ACT.Copy))
                            for h in range(2):
                                st.done(f"v{h}", nc.scalar.activation(UV[half[1 - h], 0, h, :], VT[half[1 - h], 0, :], ACT.Copy))
                        else:
                            for h in range(2):
                                o = half[1 - h]
                                st.done(f"v{h}", nc.scalar.activation(SU[o, :, :, h, :], VT[o, :, None, :].to_broadcast([HD, QC, 2, HD]), ACT.Copy))

                    def diagonals(st, pe_t, vec_t, n, c, levels, samples, fill=lambda: None):
                        for i in range(levels):
                            if i:
                                vec_t.wait(act, f"g{i}", n)
                                for h in range(2):
                                    st.done(f"gd{h}_{i}", nc.scalar.activation(Gd[half[h], c, h * C:(h + 1) * C], Gs[half[h], c, :], ACT.Copy))
                            vec_t.wait(act, f"xt{i}", n)
                            for h in range(2):
                                st.done(f"xd{h}_{i}", nc.scalar.activation(XTd[half[h], c, h * C:(h + 1) * C], XT[half[h], c, :], ACT.Copy))
                            if i == 0:
                                keys(st, pe_t, n, c)
                                fill()
                            if i == 1:
                                values(st, pe_t, n, c, samples)

                    with act.Fori(0, QUADS) as q:
                        n = j * QUADS + q
                        vec_p.wait(act, "lerp_v", j)
                        pe_q.wait(act, f"y{QC - 1}", n - 1)
                        pe_s.wait(act, "y", j - 1)
                        act_q.done("vs", nc.scalar.activation(Vs[:, :, :], quad_cols(zv, q), ACT.Copy))
                        pe_q.wait(act, f"y{QC - 1}", n - 1)
                        pe_s.wait(act, "y", j - 1)
                        diagonals(act_q, pe_q, vec_q, n, slice(0, QC), LEVELS, False)
                        if more:
                            evacuate(0, (j + 1) * QUADS + q, q)
                        for c in range(QC):
                            if c:
                                vec_q.wait(act, f"s1{c - 1}", n)
                            else:
                                vec_q.wait(act, f"s1{QC - 1}", n - 1)
                                vec_p.wait(act, "s_zero1", j)
                                vec_q.wait(act, "pc", n)
                            for h in range(2):
                                act_q.done(f"sp{h}{c}", nc.scalar.activation(SP[half[h], :], SV[half[h], c, h, :], ACT.Copy, scale=PC[half[h], c:c + 1]))
                            pe_q.wait(act, f"u{c}", n)
                            act_q.done(f"u1_{c}", nc.scalar.activation(UV[HD:P, c, 1, :], UU[HD:P, c, :], ACT.Copy))
                            if more and c == 1:
                                evacuate(1, (j + 1) * QUADS + q, q)
                        pe_q.wait(act, f"y{QC - 1}", n)
                        act_q.done("y", nc.scalar.activation(quad_cols(kkn, q), Y[:, :, :], ACT.Copy))
                        if more:
                            evacuate(2, (j + 1) * QUADS + q, q)
                    nq = j * QUADS + (QUADS - 1)
                    pe_q.wait(act, f"y{QC - 1}", nq)
                    act_s.done("vs", nc.scalar.activation(Vs[:, 0, 0:NS], zv[:, SEQ:T], ACT.Copy))
                    pe_q.wait(act, f"y{QC - 1}", nq)
                    next(piece, None)
                    diagonals(act_s, pe_s, vec_s, j, 0, SLEVELS, True, lambda: next(piece, None))
                    next(piece, None)
                    pe_s.wait(act, "u", j)
                    act_s.done("u1", nc.scalar.activation(UV[HD:P, 0, 1, :], UU[HD:P, 0, :], ACT.Copy))
                    pe_s.wait(act, "y", j)
                    act_s.done("y", nc.scalar.activation(kkn[:, SEQ:T], Y[:, 0, 0:NS], ACT.Copy))
                    next(piece, None)
                    vec_o.wait(act, "yc", j)
                    act_o.done("sq", nc.scalar.activation(rinv[:, :], centred[:, :], ACT.Square))
                    pe_o.wait(act, "var", j)
                    act_o.done("ln", nc.scalar.activation(thirds(rinv[:, :]), accA[:, :, 0:TT], ACT.Ln, scale=1.0 / HD, bias=cst("lnx_eps")))
                    act_o.wait(act, "ln", j)
                    act_o.done("rs", nc.scalar.activation(rinv[:, :], rinv[:, :], ACT.Exp, scale=-0.5))

                for _ in ahead_of(0):
                    pass
                with act.Fori(0, PAIRS - 1) as j:
                    pair(j, True)
                pair(PAIRS - 1, False)

            @block.vector
            def _(vec):
                for s in all_steps["vec"]:
                    s.begin(vec)
                for z in (RB[HD:P, :, 0, :], RB[0:HD, :, 1, :], LT[:, :, :], Gd[:, :, :], XTd[:, :, :], *[raw[:, 0:1] for raw in raws]):
                    nc.vector.memset(z, 0.0).then_inc(zero, 1)
                vec.wait_ge(zero, 8)

                def masked(st, pe_t, n, c, m, bc):
                    for h in range(2):
                        pe_t.wait(vec, f"gram{h}", n)
                        st.done(f"l{h}", nc.vector.tensor_tensor(LT[half[h], c, h * C:(h + 1) * C], G[h][half[h], c, 0:C], bc(m[half[h], 0:C]), ALU.mult))
                    for h in range(2):
                        o = half[1 - h]
                        st.done(f"m{h}", nc.vector.tensor_tensor(H[h][o, c, :], G[h][o, c, :], bc(m[o, :]), ALU.mult))
                    for h in range(2):
                        st.done(f"rb{h}", nc.vector.tensor_tensor(RB[half[h], c, h, :], G[h][half[h], c, C:P], bc(m[half[h], C:P]), ALU.mult))

                def doubling(st, pe_t, act_t, n, c, levels, bc, fill=lambda: None):
                    pe_t.wait(vec, "G0", n)
                    st.done("g0", nc.vector.tensor_tensor(Gs[:, c, :], inv[0][:, c, :], bc(level[:, 0, :]), ALU.mult))
                    st.wait(vec, "g0", n)
                    st.done("x0", nc.vector.tensor_tensor(X[:, c, :], Gs[:, c, :], bc(ident2), ALU.add))
                    for h in range(2):
                        st.done(f"xa{h}", nc.vector.tensor_tensor(XT[half[h], c, :], G[h][half[h], c, 0:C], bc(cst("level0_t")[half[h], :]), ALU.mult))
                    st.wait(vec, "xa1", n)
                    st.done("xt0", nc.vector.tensor_tensor(XT[:, c, :], XT[:, c, :], bc(ident2), ALU.add))
                    fill()
                    for i in range(1, levels):
                        pe_t.wait(vec, f"G{i}", n)
                        st.done(f"g{i}", nc.vector.tensor_tensor(Gs[:, c, :], inv[0][:, c, :], bc(level[:, i, :]), ALU.mult))
                        if i < levels - 1:
                            pe_t.wait(vec, f"W{i}", n)
                            st.done(f"x{i}", nc.vector.tensor_tensor(X[:, c, :], inv[1][:, c, :], X[:, c, :], ALU.add))
                        pe_t.wait(vec, f"WT{i}", n)
                        st.done(f"xt{i}", nc.vector.tensor_tensor(XT[:, c, :], inv[2][:, c, :], XT[:, c, :], ALU.add))

                def ahead_of(j):
                    def lerp(n, z):
                        act_p.wait(vec, f"part_{z}", j)
                        pool_p.wait(vec, f"first_{z}", j)
                        mu = vec_sb[:, bass.ds(VEC["shift_mu"] + j + n * KT, 1)]
                        vec_p.done(f"lerp_{z}", nc.vector.scalar_tensor_tensor(mixed[n][:, :], raws[n][:, 0:T], mu, mixed[n][:, :], ALU.mult, ALU.add))

                    lerp(1, "k")
                    yield
                    act_p.wait(vec, "sig_w2", j)
                    pool_s.wait(vec, "k", j - 1)
                    vec_p.done("cum", nc.vector.tensor_tensor_scan(cs[:, :], reset, sg[:, :], 0.0, ALU.mult, ALU.add))
                    vec_p.wait(vec, "cum", j)
                    vec_p.done("before", nc.vector.tensor_tensor(pp[:, :], cs[:, :], sg[:, :], ALU.subtract))
                    for n in range(NT):
                        pe_p.wait(vec, f"ksum{n}", j)
                        vec_p.done(f"nmax{n}", nc.vector.tensor_scalar(norm[:, cols(n)], side(1 + n), 1e-24, None, ALU.max))
                    yield
                    lerp(0, "r")
                    yield
                    lerp(2, "v")
                    vec.wait_ge(sp_out, 32 * j)
                    pe_q.wait(vec, f"y{QC - 1}", j * QUADS - 1)
                    for h in range(2):
                        vec_p.done(f"s_zero{h}", nc.vector.memset(SV[half[h], 0, h, :], 0.0))
                    yield
                    vec_o.wait(vec, "yc", j - 1)
                    act_p.wait(vec, "rn", j)
                    vec_p.done("kkn", nc.vector.scalar_tensor_tensor(kkn[:, :], zk[:, :], col("k_k", j), norm[:, :], ALU.mult, ALU.mult))
                    act_p.wait(vec, "t1", j)
                    vec_p.wait(vec, "kkn", j)
                    vec_p.done("bb", nc.vector.tensor_tensor(av[:, :], kkn[:, :], av[:, :], ALU.mult))
                    vec_p.done("kmod", nc.vector.tensor_tensor(zk[:, :], zk[:, :], sg[:, :], ALU.mult))
                    yield

                def pair(j, more):
                    piece = ahead_of(j + 1) if more else iter(())
                    with vec.Fori(0, QUADS) as q:
                        n = j * QUADS + q
                        over = lambda m: m[:, None, :].to_broadcast([m.shape[0], QC, m.shape[1]])
                        every = slice(0, QC)
                        act_p.wait(vec, "pi", j)
                        pe_q.wait(vec, f"y{QC - 1}", n - 1)
                        pe_s.wait(vec, "y", j - 1)
                        for h in range(2):
                            vec_q.done(f"r{h}", nc.vector.tensor_tensor(H[h][half[h], :, C:P], quad_cols(zr[half[h], :], q), quad_cols(pr[half[h], :], q), ALU.mult))
                        for h in range(2):
                            vec_q.done(f"a{h}", nc.vector.scalar_tensor_tensor(H[h][half[h], :, 0:C], quad_cols(kkn[half[h], :], q), -1.0, quad_cols(pp[half[h], :], q), ALU.mult, ALU.mult))
                        act_q.wait(vec, f"sp1{QC - 1}", n - 1)
                        vec_q.wait(vec, f"s1{QC - 1}", n - 1)
                        vec_q.done("pc", nc.vector.tensor_copy(PC[:, :], quad_cols(pr, q)[:, :, C - 1]))
                        masked(vec_q, pe_q, n, every, gram, over)
                        doubling(vec_q, pe_q, act_q, n, every, LEVELS, over)
                        for c in range(QC):
                            pe_q.wait(vec, f"rhs{c}", n)
                            vec_q.done(f"rhs{c}", nc.vector.tensor_copy(rhs[:, c, :], RH[:, c, :]))
                            pe_q.wait(vec, f"u{c}", n)
                            vec_q.done(f"u0{c}", nc.vector.tensor_copy(UV[0:HD, c, 0, :], UU[0:HD, c, :]))
                            pe_q.wait(vec, f"s{c}", n)
                            act_q.wait(vec, f"sp1{c}", n)
                            for h in range(2):
                                vec_q.done(f"s{h}{c}", nc.vector.scalar_tensor_tensor(SV[half[h], (c + 1) % QC, h, :], SS[half[h], c, :], PC[half[h], c:c + 1], SP[half[h], :], ALU.mult, ALU.add))

                    vec_p.wait(vec, "kmod", j)
                    vec_o.done("rkk", nc.vector.scalar_tensor_tensor(sg[:, :], zr[:, :], col("r_k", j), zk[:, :], ALU.mult, ALU.mult))
                    tail = slice(SEQ, T)
                    pe_q.wait(vec, f"y{QC - 1}", j * QUADS + (QUADS - 1))
                    for h in range(2):
                        vec_s.done(f"r{h}", nc.vector.tensor_tensor(H[h][half[h], 0, C:C + NS], zr[half[h], tail], pr[half[h], tail], ALU.mult))
                    for h in range(2):
                        vec_s.done(f"a{h}", nc.vector.scalar_tensor_tensor(H[h][half[h], 0, 0:NS], kkn[half[h], tail], -1.0, pp[half[h], tail], ALU.mult, ALU.mult))
                    one = lambda m: m
                    for n in range(NT):
                        pe_o.wait(vec, f"bonus{n}", j)
                        vec_o.done(f"bon{n}", nc.vector.tensor_tensor(bonus[:, cols(n)], side(n), zv[:, cols(n)], ALU.mult))
                    masked(vec_s, pe_s, j, 0, gram_s, one)
                    doubling(vec_s, pe_s, act_s, j, 0, SLEVELS, one, lambda: next(piece, None))
                    next(piece, None)
                    pe_s.wait(vec, "rhs", j)
                    vec.wait_ge(ss_out, 16 * j)
                    big = psum[:, 0, :].rearrange("p (b v) -> p b v", b=DB)
                    vec_s.done("sel", nc.vector.tensor_tensor(Rx[:, :, :], big, tok8[:, :, None].to_broadcast([P, DB, HD]), ALU.mult))
                    vec_s.wait(vec, "sel", j)
                    vec_s.done("rhs", nc.vector.tensor_reduce(rhs[:, 0, :], Rx[:, :, :].rearrange("p b v -> p v b"), AXX, ALU.add))
                    next(piece, None)
                    pe_s.wait(vec, "u", j)
                    vec_s.done("u0", nc.vector.tensor_copy(UV[0:HD, 0, 0, :], UU[0:HD, 0, :]))
                    vec_s.wait(vec, "u0", j)
                    act_s.wait(vec, "u1", j)
                    for h in range(2):
                        vec_s.done(f"ux{h}", nc.vector.tensor_tensor(UVx[:, h, :, :], UV[:, 0, h, :][:, None, :].to_broadcast([P, DB, HD]), tok8[:, :, None].to_broadcast([P, DB, HD]), ALU.mult))
                    pe_s.wait(vec, "s", j)
                    big1 = psum[:, 1, :].rearrange("p (b v) -> p b v", b=DB)
                    for h in range(2):
                        vec_s.done(f"s{h}", nc.vector.tensor_tensor(Rx[half[h], :, :], big1[half[h], :, :], SVs[half[h], h, :, :], ALU.add))
                    vec_s.wait(vec, "s1", j)
                    vec_s.done("dec", nc.vector.tensor_tensor(Rx[:, :, :], Rx[:, :, :], pr[:, SEQ + DS - 1:T:DS][:, :, None].to_broadcast([P, DB, HD]), ALU.mult))

                    next(piece, None)
                    pe_o.wait(vec, "mean", j)
                    vec_o.done("yc", nc.vector.scalar_tensor_tensor(thirds(centred[:, :]), accA[:, :, 0:TT], -1.0 / HD, thirds(kkn[:, :]), ALU.mult, ALU.add))
                    next(piece, None)
                    act_o.wait(vec, "rs", j)
                    vec_o.done("yn", nc.vector.scalar_tensor_tensor(rinv[:, :], centred[:, :], col("lnx_w", j), rinv[:, :], ALU.mult, ALU.mult))
                    vec_o.wait(vec, "yn", j)
                    vec_o.done("yb", nc.vector.scalar_tensor_tensor(bonus[:, :], rinv[:, :], col("lnx_b", j), bonus[:, :], ALU.add, ALU.add))
                    vec_o.wait(vec, "yb", j)
                    pe_o.wait(vec, "gate", j)
                    vec_o.done("out", nc.vector.tensor_tensor(out[:, bass.ds(j, 1), :].rearrange("p o (n c) -> p (o n) c", n=NT), accB[:, :, 0:TT], thirds(bonus[:, :]), ALU.mult))

                for _ in ahead_of(0):
                    pass
                with vec.Fori(0, PAIRS - 1) as j:
                    pair(j, True)
                pair(PAIRS - 1, False)

            @block.tensor
            def _(pe):
                for s in all_steps["pe"]:
                    s.begin(pe)
                pe.wait_ge(zero, 8)

                def next_pair(m, q):
                    for z in range(3):
                        act_n.wait(pe, "vkr"[z], m - 1 if z < 2 else m)
                        for k in range(KT):
                            mm = nc.tensor.matmul(ahead[z], w3[:, k, z * P:(z + 1) * P], hT[:, k, bass.ds(q * TQ, TQ)], start=k == 0, stop=k == KT - 1)
                            if k == KT - 1:
                                pe_n.done("rkv"[z], mm)
                            yield

                def grams(st, n, chunks, vec_t, pool_t):
                    vec_t.wait(pe, "a1", n)
                    pool_t.wait(pe, "k", n)
                    for h in range(2):
                        for c in chunks:
                            last = nc.tensor.matmul(G[h][:, c, :], BK[half[h], c, h:h + 2, :], H[h][half[h], c, :], start=True, stop=True)
                        st.done(f"gram{h}", last)

                def token_major(st, n, chunks, act_t):
                    for c in chunks:
                        for h in range(2):
                            last = nc.tensor.matmul(TK[:, c, h, :], BK[:, c, h:h + 2, :], ident[:, half[h]], start=True, stop=True)
                    st.done("tk", last)
                    yield
                    act_t.wait(pe, "vs", n)
                    for c in chunks:
                        for h in range(2):
                            last = nc.tensor.matmul(VT[half[1 - h], c, :], Vs[:, c, :], ident[:, half[h]], start=True, stop=True)
                    st.done("vt", last)
                    yield

                def inverse(st, n, chunks, vec_t, act_t, levels, fill, after_first=lambda: None):
                    vec_t.wait(pe, "l1", n)
                    turned = token_major(st, n, chunks, act_t)
                    for i in range(levels):
                        if i:
                            vec_t.wait(pe, f"x{i - 1}", n)
                        for c in chunks:
                            last = nc.tensor.matmul(inv[0][:, c, :], LT[:, c, :], X[:, c, :] if i else ident2, start=True, stop=True)
                        st.done(f"G{i}", last)
                        if i < 2:
                            next(turned)
                        if i == 0:
                            after_first()
                            continue
                        fill(FILL["G1"] if i == 1 else FILL["G"])
                        vec_t.wait(pe, f"g{i}", n)
                        act_t.wait(pe, f"xd1_{i - 1}", n)
                        if i < levels - 1:
                            for c in chunks:
                                last = nc.tensor.matmul(inv[1][:, c, :], XTd[:, c, :], Gs[:, c, :], start=True, stop=True)
                            st.done(f"W{i}", last)
                        act_t.wait(pe, f"gd1_{i}", n)
                        for c in chunks:
                            last = nc.tensor.matmul(inv[2][:, c, :], Gd[:, c, :], XT[:, c, :], start=True, stop=True)
                        st.done(f"WT{i}", last)

                pe.wait_ge(w3_in, 16)
                with pe.Fori(0, QUADS) as q:
                    for _ in next_pair(q, q):
                        pass

                def ahead_of(j):
                    pe.wait_ge(lw_in, 16 * j + 16)
                    for n in range(NT):
                        if n < 2:
                            vec_o.wait(pe, f"bon{1 + n}", j - 1)
                            act_n.wait(pe, "v", j * QUADS + (QUADS - 1))
                        else:
                            act_p.wait(pe, "sig_w0", j)
                        pe_p.done(f"decay{n}", nc.tensor.matmul(side(1 + n), lora_w[half[0], :], low[half[0], 0, cols(n)], start=True, stop=True))
                    yield
                    for n, last in enumerate(("sig_w1", "sig_w2", "sig_a0")):
                        act_p.wait(pe, last, j)
                        pe_p.done(f"aaa{n}", nc.tensor.matmul(side(n), lora_w[half[1], :], low[half[1], 0, cols(n)], start=True, stop=True))
                    yield
                    act_p.wait(pe, "ksq", j)
                    for n, (t, last) in enumerate(((act_p, "sig_a1"), (act_p, "sig_a2"), (vec_p, "nmax0"))):
                        t.wait(pe, last, j)
                        pe_p.done(f"ksum{n}", nc.tensor.matmul(side(1 + n), ones2, norm[:, cols(n)], start=True, stop=True))
                    yield

                def pair(j, more):
                    piece = ahead_of(j + 1) if more else iter(())
                    with pe.Fori(0, QUADS) as q:
                        n = j * QUADS + q
                        product_ahead = next_pair((j + 1) * QUADS + q, q) if more else iter(())

                        def fill(count):
                            for _ in range(count):
                                next(product_ahead, None)

                        if more:
                            pe.wait_ge(w3_in, 16 * j + 32)
                        vec_p.wait(pe, "nmax2", j)
                        fill(FILL["start"])
                        vec_o.wait(pe, "out", j - 1)
                        act_q.wait(pe, "y", n - 1)
                        vec_q.wait(pe, f"s1{QC - 1}", n - 1)
                        grams(pe_q, n, range(QC), vec_q, pool_q)
                        fill(FILL["masks"])
                        inverse(pe_q, n, range(QC), vec_q, act_q, LEVELS, fill)
                        fill(FILL["inverse"])
                        act_q.wait(pe, "v1", n)
                        vec_q.wait(pe, "rb1", n)
                        act_q.wait(pe, f"xd1_{LEVELS - 1}", n)
                        for c in range(QC):
                            if c:
                                vec_q.wait(pe, f"s1{c - 1}", n)
                            else:
                                vec_p.wait(pe, "s_zero1", j)
                            for h in range(2):
                                mm = nc.tensor.matmul(RH[half[h], c, :], H[h][:, c, 0:C], SV[:, c, h, :], start=True, stop=True)
                            pe_q.done(f"rhs{c}", mm)
                            fill(FILL["rhs"])
                            vec_q.wait(pe, f"rhs{c}", n)
                            pe_q.done(f"u{c}", nc.tensor.matmul(UU[:, c, :], XTd[:, c, :], rhs[:, c, :], start=True, stop=True))
                            fill(FILL["u"])
                            vec_q.wait(pe, f"u0{c}", n)
                            act_q.wait(pe, f"u1_{c}", n)
                            for h in range(2):
                                mm = nc.tensor.matmul(SS[half[h], c, :], KB[:, c, h, :], UV[:, c, h, :], start=True, stop=True)
                            pe_q.done(f"s{c}", mm)
                            for h in range(2):
                                nc.tensor.matmul(Y[half[h], c, :], SV[:, c, h, :], H[h][:, c, C:P], start=True, stop=False)
                                mm = nc.tensor.matmul(Y[half[h], c, :], UV[:, c, h, :], RB[:, c, h, :], start=False, stop=True)
                            pe_q.done(f"y{c}", mm)
                        fill(3 * KT)
                    nq = j * QUADS + (QUADS - 1)
                    act_q.wait(pe, "y", nq)
                    vec_q.wait(pe, f"s1{QC - 1}", nq)
                    nothing = lambda count: None
                    vec_o.wait(pe, "rkk", j)
                    if more:
                        act_n.wait(pe, "v", (j + 1) * QUADS + (QUADS - 1))
                    else:
                        vec_p.wait(pe, "nmax2", j)
                    for n in range(NT):
                        if n == 2:
                            vec_o.wait(pe, "bon0", j)
                        pe_o.done(f"bonus{n}", nc.tensor.matmul(side(n), ones2, sg[:, cols(n)], start=True, stop=True))
                    grams(pe_s, j, range(1), vec_s, pool_s)
                    next(piece, None)
                    inverse(pe_s, j, range(1), vec_s, act_s, SLEVELS, nothing, lambda: next(piece, None))
                    act_s.wait(pe, "v1", j)
                    vec_s.wait(pe, "rb1", j)
                    act_s.wait(pe, f"xd1_{SLEVELS - 1}", j)
                    pe.wait_ge(s0_in, 32 * j + 32)
                    next(piece, None)
                    for h in range(2):
                        mm = nc.tensor.matmul(psum[half[h], 0, :], H[h][:, 0, 0:C], SVs[:, h, :, :], start=True, stop=True)
                    pe_s.done("rhs", mm)
                    vec_s.wait(pe, "rhs", j)
                    pe_s.done("u", nc.tensor.matmul(UU[:, 0, :], XTd[:, 0, :], rhs[:, 0, :], start=True, stop=True))
                    vec_s.wait(pe, "ux1", j)
                    for h in range(2):
                        mm = nc.tensor.matmul(psum[half[h], 1, :], KB[:, 0, h, :], UVx[:, h, :, :], start=True, stop=True)
                    pe_s.done("s", mm)
                    for h in range(2):
                        nc.tensor.matmul(Y[half[h], 0, 0:NS], UV[:, 0, h, :], RB[:, 0, h, 0:NS], start=True, stop=False)
                        for b in range(DB):
                            mm = nc.tensor.matmul(Y[half[h], 0, DS * b:DS * b + DS], SVs[:, h, b, :], H[h][:, 0, C + DS * b:C + DS * b + DS], start=False, stop=b == DB - 1)
                    pe_s.done("y", mm)

                    act_s.wait(pe, "y", j)
                    vec_s.wait(pe, "s1", j)
                    for n in range(NT):
                        mm = nc.tensor.matmul(accA[:, n, 0:TT], ones2, kkn[:, cols(n)], start=True, stop=True)
                    pe_o.done("mean", mm)
                    act_o.wait(pe, "sq", j)
                    for n in range(NT):
                        mm = nc.tensor.matmul(accA[:, n, 0:TT], ones2, rinv[:, cols(n)], start=True, stop=True)
                    pe_o.done("var", mm)
                    pe.wait_ge(gw_in, 16 * j + 16)
                    for n in range(NT):
                        mm = nc.tensor.matmul(accB[:, n, 0:TT], gate_w[:, :], low[:, 1, cols(n)], start=True, stop=True)
                    pe_o.done("gate", mm)

                for _ in ahead_of(0):
                    pass
                with pe.Fori(0, PAIRS - 1) as j:
                    pair(j, True)
                pair(PAIRS - 1, False)




def split_high(nc, raw, parts, s):
    return nc.scalar.activation(parts[0][:, s, :], raw[:, s, :], ACT.Copy)


def split_low(nc, raw, parts, s):
    return nc.gpsimd.tensor_tensor(parts[1][:, s, :], raw[:, s, :], parts[0][:, s, :].bitcast(F32), ALU.subtract)


def gated_stage(nc, top, name, w_src, width, tiles, psum, x, out, add, low=None):
    nb = len(tiles)
    with ExitStack() as ctx:
        sb = lambda n, *s: ctx.enter_context(nc.sbuf_tensor(f"{name}_{n}", [P, *s], F32))
        w = sb("w", 2, width)
        gate, prod = sb("gate", 2, T), sb("prod", 2, T)
        total = sb("total", T) if low is not None else None
        acc = [psum[:, 0:3, :], psum[:, 3:6, :]]
        w_in = [top.enter_context(nc.semaphore(f"{name}_w_in{s}")) for s in range(2)]
        pe_s = Steps(top.enter_context(nc.semaphore(f"{name}_pe")), [f"{m}{i}" for i in range(nb) for m in ("gate", "branch")], ahead=2)
        act_s = Steps(top.enter_context(nc.semaphore(f"{name}_act")), [f"gate{i}" for i in range(nb)] + (["high"] if low is not None else []), ahead=2)
        vec_s = Steps(top.enter_context(nc.semaphore(f"{name}_vec")), [f"mul{i}" for i in range(nb)] + [f"add{i}" for i in range(nb - 1 + add)] + (["low"] if low is not None else []), ahead=2)

        def turns(eng, turn):
            with eng.Fori(0, KT // 2) as i:
                for s in range(2):
                    turn(2 * i + s, s, i)

        with nc.Block() as block:
            @block.sync
            def _(sp):
                def turn(t, s, i):
                    pe_s.wait(sp, f"branch{nb - 1}", t - 2)
                    sp.dma_start(w[:, s, :], w_src[bass.ds(t, 1), :, :].rearrange("o p c -> p (o c)")).then_inc(w_in[s], 16)
                turns(sp, turn)

            @block.tensor
            def _(pe):
                pe_s.begin(pe)

                def turn(t, s, i):
                    pe.wait_ge(w_in[s], 16 * i + 16)
                    at = 0
                    for b, (gk, gx, bk, bx) in enumerate(tiles):
                        for m, kt, src in (("gate", gk, gx), ("branch", bk, bx)):
                            if m == "gate":
                                act_s.wait(pe, f"gate{(b - 1) % nb}", t if b else t - 1)
                            else:
                                vec_s.wait(pe, f"mul{(b - 1) % nb}", t if b else t - 1)
                            wt = w[:, s, at:at + kt * P].rearrange("p (k c) -> p k c", k=kt)
                            at += kt * P
                            pe_s.done(f"{m}{b}", product(nc, acc[m == "branch"], wt, src, kt))
                turns(pe, turn)

            @block.scalar
            def _(act):
                act_s.begin(act)

                def turn(t, s, i):
                    for b in range(nb):
                        pe_s.wait(act, f"gate{b}", t)
                        vec_s.wait(act, f"mul{b}", t - 1 if nb == 2 else t - 2)
                        act_s.done(f"gate{b}", nc.scalar.activation(thirds(gate[:, b if nb == 2 else s, :]), acc[0][:, :, 0:TT], ACT.Sigmoid))
                    if low is not None:
                        vec_s.wait(act, "add0", t)
                        act_s.done("high", nc.scalar.activation(out[:, bass.ds(t, 1), :].rearrange("p o c -> p (o c)"), total[:, :], ACT.Copy))
                turns(act, turn)

            @block.vector
            def _(vec):
                vec_s.begin(vec)

                def turn(t, s, i):
                    for b in range(nb):
                        act_s.wait(vec, f"gate{b}", t)
                        pe_s.wait(vec, f"branch{b}", t)
                        vec_s.wait(vec, vec_s.names[-1], t - 1)
                        vec_s.done(f"mul{b}", nc.vector.tensor_tensor(thirds(prod[:, b, :]), thirds(gate[:, b if nb == 2 else s, :]), acc[1][:, :, 0:TT], ALU.mult))
                    row = total[:, :] if low is not None else (x if add else out)[:, bass.ds(t, 1), :].rearrange("p o c -> p (o c)")
                    vec_s.wait(vec, f"mul{nb - 1}", t)
                    if add:
                        vec_s.done("add0", nc.vector.tensor_tensor(row, row, prod[:, 0, :], ALU.add))
                    else:
                        vec_s.done("add0", nc.vector.tensor_tensor(row, prod[:, 0, :], prod[:, 1, :], ALU.add))
                    if low is not None:
                        act_s.wait(vec, "high", t)
                        high = out[:, bass.ds(t, 1), :].rearrange("p o c -> p (o c)")
                        vec_s.done("low", nc.vector.tensor_tensor(low[:, bass.ds(t, 1), :].rearrange("p o c -> p (o c)"), row, high.bitcast(F32), ALU.subtract))
                turns(vec, turn)


def residual_projection(nc, top, name, w_src, psum, src, x):
    with ExitStack() as ctx:
        raw = ctx.enter_context(nc.sbuf_tensor(f"{name}_raw", [P, 2, KT * P], F32))
        parts = [ctx.enter_context(nc.sbuf_tensor(f"{name}_{n}", [P, 2, KT * P], F32R)) for n in ("high", "low")]
        acc = [psum[:, 0:3, :], psum[:, 3:6, :]]
        w_in = [top.enter_context(nc.semaphore(f"{name}_w_in{s}")) for s in range(2)]
        pe_s = Steps(top.enter_context(nc.semaphore(f"{name}_pe")), ["full"], ahead=2)
        act_s = Steps(top.enter_context(nc.semaphore(f"{name}_act")), ["high"], ahead=2)
        pool_s = Steps(top.enter_context(nc.semaphore(f"{name}_pool")), ["low"], ahead=2)
        vec_s = Steps(top.enter_context(nc.semaphore(f"{name}_vec")), ["add"], ahead=2)
        with nc.Block() as block:
            @block.sync
            def _(sp):
                with sp.Fori(0, KT // 2) as i:
                    for s in range(2):
                        pool_s.wait(sp, "low", 2 * i + s - 2)
                        sp.dma_start(raw[:, s, :], w_src[bass.ds(2 * i + s, 1), :, :].rearrange("o p c -> p (o c)")).then_inc(w_in[s], 16)

            @block.scalar
            def _(act):
                act_s.begin(act)
                with act.Fori(0, KT // 2) as i:
                    for s in range(2):
                        act.wait_ge(w_in[s], 16 * i + 16)
                        pe_s.wait(act, "full", 2 * i + s - 2)
                        act_s.done("high", split_high(nc, raw, parts, s))

            @block.gpsimd
            def _(pool):
                pool_s.begin(pool)
                with pool.Fori(0, KT // 2) as i:
                    for s in range(2):
                        act_s.wait(pool, "high", 2 * i + s)
                        pool_s.done("low", split_low(nc, raw, parts, s))

            @block.tensor
            def _(pe):
                pe_s.begin(pe)
                with pe.Fori(0, KT // 2) as i:
                    for s in range(2):
                        pool_s.wait(pe, "low", 2 * i + s)
                        vec_s.wait(pe, "add", 2 * i + s - 2)
                        pe_s.done("full", split_product(nc, acc[s], [m[:, s, :].rearrange("p (k c) -> p k c", k=KT) for m in parts], src, KT))

            @block.vector
            def _(vec):
                vec_s.begin(vec)
                with vec.Fori(0, KT // 2) as i:
                    for s in range(2):
                        t = 2 * i + s
                        pe_s.wait(vec, "full", t)
                        row = x[:, bass.ds(t, 1), :].rearrange("p o (n c) -> p (o n) c", n=NT)
                        vec_s.done("add", nc.vector.tensor_tensor(row, row, acc[s][:, :, 0:TT], ALU.add))


def mlp(nc, top, w_src, psum, h, ff, x):
    with ExitStack() as ctx:
        raw = ctx.enter_context(nc.sbuf_tensor("ff_raw", [P, 2, KT * P], F32))
        parts = [ctx.enter_context(nc.sbuf_tensor(f"ff_w_{n}", [P, 2, KT * P], F32R)) for n in ("high", "low")]
        up = ctx.enter_context(nc.sbuf_tensor("ff_up", [P, 2, T], F32))
        acc = [psum[:, 0:3, :], psum[:, 3:6, :]]
        w_in = [top.enter_context(nc.semaphore(f"ff_w_in{s}")) for s in range(2)]
        ups, downs, chunks = range(FFT), range(KT), range(2 * FFT)
        pe_s = Steps(top.enter_context(nc.semaphore("ff_pe")), [f"up{c}" for c in ups] + [f"down{m}" for m in downs])
        high_s = Steps(top.enter_context(nc.semaphore("ff_w_high_done")), [f"high{c}" for c in chunks])
        pool_s = Steps(top.enter_context(nc.semaphore("ff_w_low_done")), [f"low{c}" for c in chunks])
        act_s = Steps(top.enter_context(nc.semaphore("ff_act")), [f"{n}{c}" for c in ups for n in ("relu", "square", "high")])
        vec_s = Steps(top.enter_context(nc.semaphore("ff_vec")), [f"low{c}" for c in ups] + [f"add{m}" for m in downs])
        used = lambda c: f"up{c}" if c < FFT else f"down{2 * (c - FFT) + 1}"

        def chunk(c, q):
            return (c, q) if c >= 0 else (2 * FFT + c, q - 1)

        with nc.Block() as block:
            @block.sync
            def _(sp):
                with sp.Fori(0, FFQ) as q:
                    for c in chunks:
                        before, turn = chunk(c - 2, q)
                        pool_s.wait(sp, f"low{before}", turn)
                        sp.dma_start(raw[:, c % 2, :], w_src[bass.ds(2 * FFT * q + c, 1), :, :].rearrange("o p c -> p (o c)")).then_inc(w_in[c % 2], 16)

            @block.gpsimd
            def _(pool):
                pool_s.begin(pool)
                with pool.Fori(0, FFQ) as q:
                    for c in chunks:
                        high_s.wait(pool, f"high{c}", q)
                        pool_s.done(f"low{c}", split_low(nc, raw, parts, c % 2))

            @block.tensor
            def _(pe):
                pe_s.begin(pe)
                with pe.Fori(0, FFQ) as q:
                    for c in ups:
                        pool_s.wait(pe, f"low{c}", q)
                        if c < 2:
                            vec_s.wait(pe, f"add{KT - 2 + c}", q - 1)
                        else:
                            act_s.wait(pe, f"relu{c - 2}", q)
                        w = [m[:, c % 2, :].rearrange("p (k c) -> p k c", k=KT) for m in parts]
                        pe_s.done(f"up{c}", split_product(nc, acc[c % 2], w, h, KT))
                    for m in downs:
                        c = FFT + m // 2
                        if m == 0:
                            vec_s.wait(pe, f"low{FFT - 1}", q)
                        if m % 2 == 0:
                            pool_s.wait(pe, f"low{c}", q)
                        if m >= 2:
                            vec_s.wait(pe, f"add{m - 2}", q)
                        else:
                            act_s.wait(pe, f"relu{FFT - 2 + m}", q)
                        w = [p[:, c % 2, :].rearrange("p (o k c) -> p o k c", o=2, k=FFT)[:, m % 2] for p in parts]
                        pe_s.done(f"down{m}", split_product(nc, acc[m % 2], w, ff, FFT))

            @block.scalar
            def _(act):
                act_s.begin(act)
                high_s.begin(act)
                with act.Fori(0, FFQ) as q:
                    def weights(c):
                        before, turn = chunk(c - 2, q)
                        act.wait_ge(w_in[c % 2], 16 * FFT * q + (16 * (c // 2) + 16))
                        pe_s.wait(act, used(before), turn)
                        high_s.done(f"high{c}", split_high(nc, raw, parts, c % 2))

                    weights(0)
                    for c in ups:
                        weights(c + 1)
                        pe_s.wait(act, f"up{c}", q)
                        vec_s.wait(act, f"low{(c - 2) % FFT}", q if c >= 2 else q - 1)
                        act_s.done(f"relu{c}", nc.scalar.activation(thirds(up[:, c % 2, :]), acc[c % 2][:, :, 0:TT], ACT.Relu))
                        act_s.wait(act, f"relu{c}", q)
                        act_s.done(f"square{c}", nc.scalar.activation(up[:, c % 2, :], up[:, c % 2, :], ACT.Square))
                        act_s.wait(act, f"square{c}", q)
                        act_s.done(f"high{c}", nc.scalar.activation(ff[0][:, c, :], up[:, c % 2, :], ACT.Copy))
                    for c in range(FFT + 1, 2 * FFT):
                        weights(c)

            @block.vector
            def _(vec):
                vec_s.begin(vec)
                with vec.Fori(0, FFQ) as q:
                    for c in ups:
                        act_s.wait(vec, f"high{c}", q)
                        vec_s.done(f"low{c}", nc.vector.tensor_tensor(ff[1][:, c, :], up[:, c % 2, :], ff[0][:, c, :].bitcast(F32), ALU.subtract))
                    for m in downs:
                        pe_s.wait(vec, f"down{m}", q)
                        vec_s.done(f"add{m}", nc.vector.tensor_tensor(thirds(x[:, m, :]), thirds(x[:, m, :]), acc[m % 2][:, :, 0:TT], ALU.add))




def program(nc, ins, outs):
    with ExitStack() as ctx:
        sb = lambda n, s: ctx.enter_context(nc.sbuf_tensor(n, s, F32))
        front = ExitStack()
        sbf = lambda n, s: front.enter_context(nc.sbuf_tensor(n, s, F32))
        vec_sb = sb("vec_sb", [P, NVEC])
        cst_sb = sb("cst_sb", [P, NCST])
        mu1 = sb("mu1", [P, RT])
        ka1 = sb("ka1", [P, KT])
        mixer = sb("rwkv_out", [P, KT, T])

        hT = sbf("hT", [P, KT, T])
        attn = sbf("attn", [P, 2, T])
        psum = ctx.enter_context(nc.psum_tensor("psum", [P, 8, 512], F32))
        scratch = nc.dram_tensor("attention_rows", (SEQ, GROUPS * STG), F32, kind="Internal").ap()
        sem = lambda n: ctx.enter_context(nc.semaphore(n))
        cst = lambda n: cst_sb[:, CST[n][0]:CST[n][1]]
        gain = lambda n: vec_sb[:, VEC[n]:VEC[n] + KT]

        with nc.sbuf_tensor("x_in", [P, KT, T], F32) as x_in:
            load_all(nc, sem("loaded"), [(x_in[:, :, :], ins["xT"]), (vec_sb[:, :], ins["vecs"]), (cst_sb[:, :], ins["consts"])])
            rms_norm(nc, "mix", x_in, gain("norm_mix"), cst_sb, hT, psum, ctx)
        derived = sem("derived")
        with nc.Block() as block:
            @block.vector
            def _(vec):
                nc.vector.tensor_scalar(mu1[:, :], vec_sb[:, VEC["shift_mu"]:VEC["shift_mu"] + RT], -1.0, 1.0, ALU.mult, ALU.add).then_inc(derived, 1)
                nc.vector.tensor_scalar(ka1[:, :], vec_sb[:, VEC["k_a"]:VEC["k_a"] + KT], -1.0, 1.0, ALU.mult, ALU.add).then_inc(derived, 1)

        with ExitStack() as c1:
            sb1 = lambda n, s: c1.enter_context(nc.sbuf_tensor(n, s, F32))
            att_sb = sb1("att_sb", [P, NATT])
            att = lambda n: att_sb[:, ATT[n][0]:ATT[n][1]]
            vnew = sb1("vnew", [NS, GROUPS, AW])
            scores = sb1("sample_scores", [P, GROUPS, SK])
            V = [sb1(f"sample_v{g}", [P, DB, 1 if g == 0 else DS, AW]) for g in range(GROUPS - 1)]
            flat = mixer[:, :, :].rearrange("p k t -> p (k t)")
            V.append(flat[:, 0:DB * DS * AW].rearrange("p (b t c) -> p b t c", b=DB, t=DS))
            K = []
            for g in range(GROUPS):
                tt = 1 if g == 0 else DS
                K.append(flat[:, 0:2 * DB * tt * SK].rearrange("p (a b t k) -> p a b t k", a=2, b=DB, t=tt))
            wa_in, wb_in, k_in, v_in = sem("w_qk_in"), sem("w_kv_in"), sem("sample_k_in"), sem("sample_v_in")
            with ExitStack() as c2:
                sb2 = lambda n, s: c2.enter_context(nc.sbuf_tensor(n, s, F32))
                wa, wb = sb2("w_qk", [P, WQK]), sb2("w_kv", [P, WKV])
                qT, kT, vtok = sb2("qT", [P, 2, T]), sb2("kT", [P, 2, T]), sb2("vtok", [P, NB, AW])
                weights = lambda g: [(wa[:, :], ins["w_qk"][g], wa_in), (wb[:, :], ins["w_kv"][g], wb_in)]
                att_loaded = sem("att_loaded")
                start_loads(nc, weights(0) + [(att_sb[:, :], ins["att_consts"], att_loaded)])
                counts = prompt_counts(nc, ctx)
                for g in range(GROUPS):
                    ahead = [(K[g][:, hp, :, :, 0:NCACHE], ins[f"kc{g}"][:, hp, :, :, :], k_in) for hp in range(2)]
                    if g < GROUPS - 1:
                        ahead += weights(g + 1) + [(V[g][:, :, :, :], ins[f"vc{g}"], v_in)]
                    attention_projection(nc, ctx, g, hT, wa, wb, wa_in, wb_in, att_loaded, psum, qT, kT, vtok, vnew, outs["k_all"][g], outs["v_all"][g])
                    attention_prompt(nc, ctx, g, counts, psum, qT, kT, vtok, att, cst("ident"), scratch, ahead)
                    sample_scores(nc, ctx, g, psum, qT, kT, att, K[g], k_in, scores)
            combine_groups(nc, ctx, psum, cst("ident"), scratch, attn, [(V[2], ins["vc2"], v_in)])
            sample_attention(nc, ctx, psum, att, cst("ident"), scores, vnew, V, v_in, attn)
            load_all(nc, sem("vnew_stored"), [(outs["v_new"], vnew[:, :, :])])
        with ExitStack() as c2:
            low = c2.enter_context(nc.sbuf_tensor("low", [P, 2, T], F32))
            shift_sb = c2.enter_context(nc.sbuf_tensor("shift_sb", [P, RT, 1 + DB], F32))
            shift0 = c2.enter_context(nc.sbuf_tensor("shift0", [P, RT, DB], F32))
            load_all(nc, sem("shift_loaded"), [(shift0[:, :, :], ins["shift0"])])
            rwkv_lora_inputs(nc, ctx, hT, ins["w_lora"], shift0, vec_sb, mu1, cst, psum, low, shift_sb)
            rwkv_pairs(nc, ctx, hT, ins["w_pair"], shift0, ins["s0T"], vec_sb, mu1, ka1, cst, psum, low, shift_sb, mixer, outs["wkv_p"], outs["wkv_s"])
            load_all(nc, sem("shift_stored"), [(outs["shift"], shift_sb[:, :, :])])

        r2 = lambda c, n, kt: [c.enter_context(nc.sbuf_tensor(f"{n}_{part}", [P, kt, T], F32R)) for part in ("high", "low")]
        with ExitStack() as c3:
            mixed = r2(c3, "mixed", KT)
            gated_stage(nc, ctx, "merge", ins["w_mix"], WMIX, [(KT, hT, KT, mixer), (KT, hT, 2, attn)], psum, None, mixed[0], False, low=mixed[1])
            x = mixer
            load_all(nc, sem("x_again"), [(x[:, :, :], ins["xT"])])
            residual_projection(nc, ctx, "proj", ins["w_out"], psum, mixed, x)
        front.close()
        h = r2(ctx, "h", KT)
        rms_norm(nc, "mlp", x, gain("norm_mlp"), cst_sb, h[0], psum, ctx, low=h[1])
        with ExitStack() as c4:
            mlp(nc, ctx, ins["w_ff"], psum, h, r2(c4, "ff", FFT), x)
        with nc.sbuf_tensor("y", [P, KT, T], F32) as y:
            rms_norm(nc, "ple", x, gain("norm_ple"), cst_sb, y, psum, ctx)
            with nc.sbuf_tensor("pT", [P, 2, T], F32) as pT:
                load_all(nc, sem("p_loaded"), [(pT[:, :, :], ins["pT"])])
                gated_stage(nc, ctx, "ple", ins["w_ple"], WPLE, [(KT, y, 2, pT)], psum, x, None, True)
            rms_norm(nc, "final", x, gain("norm_final"), cst_sb, y, psum, ctx, store=outs["yT"])




def _constants(np):
    def two(m):
        return np.concatenate([m, m], 0)

    i, k = np.arange(P), np.arange(C)
    s, t = k[:, None], k[None, :]
    out = {
        "ident": np.eye(P),
        "ident2": two(np.eye(C)),
        "ones": np.ones((P, P)),
        "ones2": (i[:, None] // HD == i[None, :] // HD),
        "gram": two(np.concatenate([s < t, s <= t], 1)),
    }
    same = (s // DS == t // DS) & (s < NS) & (t < NS)
    out["gram_s"] = two(np.concatenate([same & (s < t), same & (s <= t)], 1))
    out["level"] = two(np.concatenate([(s // n % 2 == 1) & (t // n == s // n - 1) for n in (1 << np.arange(LEVELS))], 1))
    out["level0_t"] = two((s % 2 == 0) & (t == s + 1))
    out["eps"], out["lnx_eps"] = np.full((P, 1), EPS), np.full((P, 1), LNX_EPS)
    at = np.arange(T)
    out["reset"] = np.broadcast_to(np.where(at < SEQ, at % C != 0, (at - SEQ) % DS != 0), (P, T))
    q, key = i[:, None], np.arange(2 * BL)[None, :]
    dist = q + BL - key
    out["band"] = np.where((dist >= 0) & (dist <= BL), 0.0, NEG)
    kk = i[None, :]
    out["pairs"] = np.where((q % 2 == kk % 2) & (kk <= q), 0.0, NEG)
    hp, tok, c = np.arange(2)[:, None, None], np.arange(NS)[None, :, None], np.arange(32)[None, None, :]
    want = 16 * (tok // DS % 2) + 4 * (tok % DS) + 2 * hp
    out["place"] = np.stack([(c == want + h) for h in range(2)]).repeat(HD, 0).reshape(P, -1)
    row_t = (i // HPG % DS)[:, None]
    key = np.arange(SK)[None, :]
    new = key - NCACHE
    fresh = [np.where(np.where(new >= 0, new <= row_t, key >= row_t), 0.0, NEG)]
    fresh += [np.where((new < 0) | (new == row_t), 0.0, NEG)] * 2
    out["fresh"] = np.concatenate(fresh, 1)
    out["own8"] = i[:, None] // (HPG * DS) == np.arange(DB)[None, :]
    tk = np.concatenate([k, k])
    out["tok8"] = (tk[:, None] < NS) & (tk[:, None] // DS == np.arange(DB)[None, :])
    return [np.concatenate([np.asarray(out[n], np.float32) for n in names], 1) for names in (CST, ATT)]


def _tiles(np, w, cols):
    kk, m = w.shape
    return np.ascontiguousarray(w.reshape(kk // P, P, m // cols, cols).transpose(2, 1, 0, 3).reshape(m // cols, P, -1))


def _layout(np, a):
    a = {k: np.asarray(v) for k, v in a.items()}
    x = np.concatenate([a["x_prompt"][0], a["x_sample"].reshape(NS, D)], 0)
    p = np.concatenate([a["p_prompt"][0, 0], a["p_sample"][0].reshape(NS, -1)], 0)
    feat = lambda v: v.reshape(-1, P).T
    fm = lambda m: np.ascontiguousarray(m.T.reshape(-1, P, m.shape[0]).transpose(1, 0, 2))
    w_in = a["w_in"][0]
    rw = 3 * D + 256
    q0, k0, v0, g0 = rw, rw + 3 * AW, rw + 6 * AW, rw + 9 * AW
    heads = lambda c: [w_in[:, c + AW * g:c + AW * (g + 1)] for g in range(GROUPS)]
    d = {"xT": fm(x), "pT": fm(p)}
    d["vecs"] = np.concatenate([feat(a[n].reshape(-1)) for n in VEC], 1)
    d["consts"], d["att_consts"] = _constants(np)
    d["shift0"] = np.ascontiguousarray(a["state_shift"][0].T.reshape(RT, P, DB).transpose(1, 0, 2))
    d["w_lora"] = _tiles(np, w_in[:, 3 * D:rw], 256)[0].reshape(P, KT, 256)
    lora = np.concatenate([a["decay_w2"][0], a["aaa_a2"][0]], 0)
    rkv = w_in[:, :3 * D].reshape(KT, P, 3, PAIRS, P).transpose(3, 1, 0, 2, 4).reshape(PAIRS, P, -1)
    d["w_pair"] = np.concatenate([rkv, _tiles(np, lora, P), _tiles(np, a["gate_g2"][0], P)], 2)
    d["s0T"] = np.ascontiguousarray(a["state_wkv"][0].reshape(DB, PAIRS, 2, HD, HD).transpose(1, 2, 4, 0, 3).reshape(PAIRS, P, DB, HD))
    wq, wk, wv = heads(q0), heads(k0), heads(v0)
    d["w_qk"] = np.stack([_tiles(np, np.concatenate([wq[g], wk[g][:, :P]], 1), 3 * P)[0] for g in range(GROUPS)])
    d["w_kv"] = np.stack([np.concatenate([_tiles(np, wk[g][:, P:], P)[0], _tiles(np, wv[g], AW)[0]], 1) for g in range(GROUPS)])
    for g in range(GROUPS):
        cache = a[f"cache_kv_g{g}"][0]
        rows = cache.reshape(DB, NCACHE, DIL[g], 2, HPG, HD)[:, :, :DS]
        d[f"kc{g}"] = np.ascontiguousarray(rows[:, :, :, 0].reshape(DB, NCACHE, -1, 2, P).transpose(4, 3, 0, 2, 1))
        d[f"vc{g}"] = np.ascontiguousarray(rows[:, :, :, 1].reshape(DB, NCACHE, -1, AW).transpose(1, 0, 2, 3))
    g = _tiles(np, w_in[:, g0:], P)
    br = _tiles(np, a["w_branch_rwkv"][0], P)
    ba = _tiles(np, a["w_branch_attn"][0], P)
    d["w_mix"] = np.concatenate([g[:KT], br, g[KT:], ba], 2)
    d["w_out"] = _tiles(np, a["w_out"][0], P)
    w1 = _tiles(np, a["w_ff1"][0], P).reshape(FFQ, FFT, P, -1)
    w2 = np.stack([_tiles(np, w, P) for w in a["w_ff2"][0].reshape(FFQ, FFT * P, D)])
    w2 = w2.reshape(FFQ, FFT, 2, P, -1).transpose(0, 1, 3, 2, 4).reshape(FFQ, FFT, P, -1)
    d["w_ff"] = np.concatenate([w1, w2], 1).reshape(FFQ * 2 * FFT, P, -1)
    d["w_ple"] = np.concatenate([_tiles(np, a["w_ple_gate"][0], P), _tiles(np, a["w_ple"][0], P)], 2)
    return d


_OUT = {"yT": (P, KT, T), "k_all": (GROUPS, P, 2, T), "v_all": (GROUPS, P, NB, AW), "v_new": (NS, GROUPS, AW),
        "wkv_p": (PAIRS, P, HD), "wkv_s": (PAIRS, P, DB, HD), "shift": (P, RT, 1 + DB)}


def _results(np, r):
    y = r["yT"].transpose(2, 1, 0).reshape(T, D)
    kv_p, kv_s = [], []
    for g, keep in enumerate((128, 512, SEQ)):
        k = r["k_all"][g].transpose(2, 1, 0).reshape(T, HPG, HD)
        v = r["v_all"][g].transpose(1, 0, 2)
        if g == 1:
            v = v.reshape(STEP[1], SEQ // STEP[1], AW).transpose(1, 0, 2)
        elif g == 2:
            v = v.transpose(1, 0, 2)
        v = v.reshape(SEQ, HPG, HD)
        kv_p.append(np.stack([k[SEQ - keep:SEQ], v[SEQ - keep:]], 1)[None, None])
        vs = r["v_new"][:, g].reshape(DB, DS, HPG, HD)
        kv_s.append(np.stack([k[SEQ:].reshape(DB, DS, HPG, HD), vs], 2)[None])
    state = lambda w: w.reshape(PAIRS, 2, HD, -1, HD).transpose(3, 0, 1, 4, 2).reshape(-1, 2 * PAIRS, HD, HD)
    sh = r["shift"].transpose(2, 1, 0).reshape(1 + DB, RT * P)
    out = (y[None, :SEQ], y[SEQ:].reshape(DB, DS, D), *kv_p, state(r["wkv_p"][:, :, None, :])[None], sh[None, 0:1],
           *kv_s, state(r["wkv_s"])[None], sh[None, 1:])
    return tuple(np.ascontiguousarray(o) for o in out)


def kernel(**inputs):
    import numpy as np
    import concourse.bacc as bacc
    from concourse.bass_utils import run_bass_kernel_spmd

    nc = bacc.Bacc("TRN2", target_bir_lowering=False, num_devices=1)
    arrays = {f"in_{k}": np.ascontiguousarray(v) for k, v in _layout(np, inputs).items()}
    ins = {k[3:]: nc.dram_tensor(k, v.shape, F32, kind="ExternalInput").ap() for k, v in arrays.items()}
    outs = {k: nc.dram_tensor(f"out_{k}", s, F32, kind="ExternalOutput").ap() for k, s in _OUT.items()}
    program(nc, ins, outs)
    r = run_bass_kernel_spmd(nc, [arrays], core_ids=[0])
    got = r.results[0]
    return _results(np, {k: got[f"out_{k}"] for k in _OUT})
```

```python
import concourse.bass as bass
from concourse import mybir
from contextlib import ExitStack

F32 = mybir.dt.float32
F32R = mybir.dt.float32r
ACT = mybir.ActivationFunctionType
ALU = mybir.AluOpType
AXX = mybir.AxisListType.X

P = 128
D = 1024
KT = D // P
SEQ = 1024
DB, DS = 8, 4
NS = DB * DS
T = SEQ + NS
NT = 3
TT = T // NT
HD = 64
PAIRS = 8
RT = 26
GROUPS, HPG = 3, 4
DIL = (1, 4, 16)
STEP = (1, 4, 8)
AW = HPG * HD
BL = 128
NB = SEQ // BL
C = 64
QC = 4
QUADS = SEQ // (C * QC)
QT = QC * C
TQ = T // QUADS
FILL = {"G0": 2, "G1": 2, "G": 2, "inverse": 0, "rhs": (3, 1, 1, 1), "u": (1, 1, 2, 2)}
GRAM_AT = (2, 2, 2, 2, 0, 0, 0, 0)
LEVELS = 6
SLEVELS = 2
FFQ = 8
FFT = 4 * KT // FFQ
EPS, LNX_EPS = 1e-6, 64e-5
DECAY = 0.6065306597126334
NEG = -1e30
NCACHE = 128
SK = NCACHE + DS
STG = AW + 2 * HPG

VEC = {}
_at = 0
for _n, _w in (("norm_mix", KT), ("norm_mlp", KT), ("norm_ple", KT), ("norm_final", KT), ("shift_mu", RT),
               ("decay_w0", KT), ("aaa_a0", KT), ("k_k", KT), ("k_a", KT), ("r_k", KT), ("lnx_w", KT), ("lnx_b", KT)):
    VEC[_n] = _at
    _at += _w
NVEC = _at

def _columns(widths):
    out, at = {}, 0
    for n, w in widths:
        out[n] = (at, at + w)
        at += w
    return out, at


CST, NCST = _columns([("ident", P), ("ident2", HD), ("ones", P), ("ones2", P), ("gram", P), ("gram_s", P), ("level", LEVELS * HD),
                      ("reset", T), ("tok8", DB), ("level0_t", HD), ("eps", 1), ("lnx_eps", 1)])
ATT, NATT = _columns([("band", 2 * BL), ("pairs", BL), ("place", 2 * NS * 32), ("fresh", GROUPS * SK), ("own8", DB)])
WPAIR = 3 * KT * P + 2 * P
WMIX = (3 * KT + 2) * P
WQK, WKV = 3 * KT * P, KT * P + KT * AW
WPLE = (KT + 2) * P


class Steps:

    def __init__(self, sem, names, ahead=1):
        self.sem, self.names, self.at, self.ahead, self.first = sem, list(names), 0, ahead, 0
        assert len(set(self.names)) == len(self.names)

    def begin(self, eng):
        eng.sem_inc(self.sem, self.ahead * len(self.names))

    def done(self, name, ins):
        assert self.names[self.at % len(self.names)] == name, (name, self.names[self.at % len(self.names)])
        self.at += 1
        ins.then_inc(self.sem, 1)

    def wait(self, eng, name, turn):
        eng.wait_ge(self.sem, turn * len(self.names) + ((self.first + self.ahead) * len(self.names) + self.names.index(name) + 1))


def thirds(tile):
    return tile.rearrange("p (n c) -> p n c", n=NT)


def product(nc, acc, w, x, kt, width=None):
    for k in range(kt):
        for n in range(NT):
            last = nc.tensor.matmul(acc[:, n, 0:TT], w[:, k, :], x[:, k, n * TT:(n + 1) * TT], start=k == 0, stop=k == kt - 1)
    return last


def load_all(nc, sem, pairs):
    with nc.Block() as block:
        @block.sync
        def _(sp):
            for n, (dst, src) in enumerate(pairs):
                sp.dma_start(dst, src).then_inc(sem, 16)
            sp.wait_ge(sem, 16 * len(pairs))


def split_product(nc, acc, w, x, kt, ready=lambda k: None):
    (w_hi, w_lo), (x_hi, x_lo) = w, x
    for k in range(kt):
        ready(k)
        for a, b in ((w_hi, x_hi), (w_hi, x_lo), (w_lo, x_hi)):
            for n in range(NT):
                last = nc.tensor.matmul(acc[:, n, 0:TT], a[:, k, :], b[:, k, n * TT:(n + 1) * TT], start=k == 0 and b is x_hi and a is w_hi, stop=k == kt - 1 and a is w_lo)
    return last


def start_loads(nc, loads):
    with nc.Block() as block:
        @block.sync
        def _(sp):
            for dst, src, sem in loads:
                sp.dma_start(dst, src).then_inc(sem, 16)


class RmsNorm:

    def __init__(self, nc, name, x, gain, cst, out, psum, ctx, top, low=None):
        sb = lambda n, *s: ctx.enter_context(nc.sbuf_tensor(f"{name}_{n}", [P, *s], F32))
        sem = lambda n: top.enter_context(nc.semaphore(f"{name}_{n}"))
        self.nc, self.x, self.gain, self.cst, self.out, self.low, self.psum = nc, x, gain, cst, out, low, psum
        self.sq, self.rinv = sb("sq", 2, T), sb("rinv", T)
        self.squared, self.summed, self.root, self.normed = (sem(n) for n in ("squared", "summed", "root", "normed"))
        if low is not None:
            self.full = sb("full", 2, T)
            self.high_done, self.low_done = sem("high_done"), sem("low_done")

    def ready(self, eng, k):
        eng.wait_ge(self.normed if self.low is None else self.low_done, k + 1)

    def scalar(self, act, arrive=None):
        nc, rinv, eps = self.nc, self.rinv, self.cst[:, CST["eps"][0]:CST["eps"][1]]
        for k in range(KT):
            if arrive is not None and k % (KT // 2) == 0:
                act.wait_ge(arrive[0][k // (KT // 2)], 16)
            if k >= 2:
                act.wait_ge(self.summed, k - 1)
            nc.scalar.activation(self.sq[:, k % 2, :], self.x[:, k, :], ACT.Square).then_inc(self.squared, 1)
        act.wait_ge(self.summed, KT)
        if arrive is not None:
            act.wait_ge(arrive[1], 32)
        nc.scalar.activation(thirds(rinv[:, :]), self.psum[:, 0:NT, 0:TT], ACT.Ln, scale=1.0 / D, bias=eps).then_inc(self.root, 1)
        act.wait_ge(self.root, 1)
        nc.scalar.activation(rinv[:, :], rinv[:, :], ACT.Exp, scale=-0.5).then_inc(self.root, 1)

    def tensor(self, pe):
        ones = self.cst[:, CST["ones"][0]:CST["ones"][1]]
        for k in range(KT):
            pe.wait_ge(self.squared, k + 1)
            for n in range(NT):
                last = self.nc.tensor.matmul(self.psum[:, n, 0:TT], ones, self.sq[:, k % 2, n * TT:(n + 1) * TT], start=k == 0, stop=k == KT - 1)
            last.then_inc(self.summed, 1)

    def scalar_high(self, act):
        for k in range(KT):
            act.wait_ge(self.normed, k + 1)
            self.nc.scalar.activation(self.out[:, k, :], self.full[:, k % 2, :], ACT.Copy).then_inc(self.high_done, 1)

    def vector(self, vec):
        nc, x, gain, rinv, out, low = self.nc, self.x, self.gain, self.rinv, self.out, self.low
        vec.wait_ge(self.root, 2)
        for k in range(KT):
            if low is None:
                nc.vector.scalar_tensor_tensor(out[:, k, :], x[:, k, :], gain[:, k:k + 1], rinv[:, :], ALU.mult, ALU.mult).then_inc(self.normed, 1)
                continue
            if k >= 2:
                vec.wait_ge(self.low_done, k - 1)
            nc.vector.scalar_tensor_tensor(self.full[:, k % 2, :], x[:, k, :], gain[:, k:k + 1], rinv[:, :], ALU.mult, ALU.mult).then_inc(self.normed, 1)
            for m in ([k - 1] if k else []) + ([k] if k == KT - 1 else []):
                vec.wait_ge(self.high_done, m + 1)
                nc.vector.tensor_tensor(low[:, m, :], self.full[:, m % 2, :], out[:, m, :].bitcast(F32), ALU.subtract).then_inc(self.low_done, 1)


def rms_norm(nc, name, x, gain, cst, out, psum, top, store=None, arrive=None):
    with ExitStack() as ctx:
        norm = RmsNorm(nc, name, x, gain, cst, out, psum, ctx, top)
        stored = top.enter_context(nc.semaphore(f"{name}_stored"))
        with nc.Block() as block:
            @block.scalar
            def _(act):
                norm.scalar(act, arrive)

            @block.tensor
            def _(pe):
                if arrive is not None:
                    pe.wait_ge(arrive[1], 32)
                norm.tensor(pe)

            @block.vector
            def _(vec):
                if arrive is not None:
                    vec.wait_ge(arrive[1], 32)
                norm.vector(vec)

            if store is not None:
                @block.sync
                def _(sp):
                    for k in range(KT):
                        norm.ready(sp, k)
                        sp.dma_start(store[:, k, :], out[:, k, :]).then_inc(stored, 16)
                    sp.wait_ge(stored, 16 * KT)




def dilated(tile, g, first, n, blocks=None):
    if g == 0:
        return tile[:, bass.ds(first * BL, n)]
    rows = tile.rearrange("p (i r) -> p r i", r=STEP[g])
    lo = blocks * BL if g == 1 else 0
    return rows[:, bass.ds(first, 1), lo:lo + n].rearrange("p a b -> p (a b)")


def attention_projection(nc, top, g, hT, wa, wb, wa_in, wb_in, tables_in, psum, qT, kT, vtok, vnew, k_out, v_out, prefetch):
    with ExitStack() as ctx:
        sem = lambda n: top.enter_context(nc.semaphore(f"{n}{g}"))
        full, evac, v_full, v_evac, stored = (sem(n) for n in ("qk_full", "qk_evac", "v_full", "v_evac", "kv_stored"))
        with nc.Block() as block:
            @block.sync
            def _(sp):
                for dst, src, loaded in prefetch:
                    sp.dma_start(dst, src).then_inc(loaded, 16)
                sp.wait_ge(tables_in, 16)
                sp.wait_ge(evac, 4)
                sp.dma_start(k_out, kT[:, :, :]).then_inc(stored, 16)
                sp.wait_ge(v_evac, NB + 1)
                sp.dma_start(v_out, vtok[:, :, :]).then_inc(stored, 16)
                sp.wait_ge(stored, 32)

            @block.tensor
            def _(pe):
                wk = wa[:, :].rearrange("p (k c) -> p k c", k=KT)
                wk1 = wb[:, 0:KT * P].rearrange("p (k c) -> p k c", k=KT)
                wv = wb[:, KT * P:].rearrange("p (k c) -> p k c", k=KT)
                pe.wait_ge(wa_in, 16 * g + 16)
                for i in range(4):
                    if i >= 2:
                        pe.wait_ge(evac, i - 1)
                    if i == 3:
                        pe.wait_ge(wb_in, 16 * g + 16)
                    w = wk[:, :, i * P:(i + 1) * P] if i < 3 else wk1
                    product(nc, psum[:, 3 * (i % 2):3 * (i % 2) + 3, :], w, hT, KT).then_inc(full, 1)
                for b in range(NB + 1):
                    if b >= 2:
                        pe.wait_ge(v_evac, b - 1)
                    for k in range(KT):
                        if b == NB:
                            rows, toks = NS, hT[:, k, SEQ:T]
                        else:
                            rows = BL
                            toks = dilated(hT[:, k, 0:SEQ], g, (b, b // 2, b)[g], BL, b % 2)
                        last = nc.tensor.matmul(psum[0:rows, 6 + b % 2, 0:AW], toks, wv[:, k, :], start=k == 0, stop=k == KT - 1)
                    last.then_inc(v_full, 1)

            @block.scalar
            def _(act):
                for i in range(4):
                    act.wait_ge(full, i + 1)
                    dst = (qT if i < 2 else kT)[:, i % 2, :]
                    nc.scalar.activation(thirds(dst), psum[:, 3 * (i % 2):3 * (i % 2) + 3, 0:TT], ACT.Copy, scale=HD ** -0.5 if i < 2 else 1.0).then_inc(evac, 1)

            @block.vector
            def _(vec):
                for b in range(NB + 1):
                    vec.wait_ge(v_full, b + 1)
                    dst, rows = (vnew[:, g, :], NS) if b == NB else (vtok[:, b, :], BL)
                    nc.vector.tensor_copy(dst, psum[0:rows, 6 + b % 2, 0:AW]).then_inc(v_evac, 1)


def prompt_counts(nc, top):
    sem = lambda n: top.enter_context(nc.semaphore(f"att_{n}"))
    names = {"pool": ["q0", "q1"], "score": ["scores"], "pe": ["pt", "pv"], "vec": ["mask", "max"], "out": ["o"], "act": ["e0", "e1", "e2", "e3", "pt"]}
    return [Steps(sem(n), names[n], ahead=2) for n in names], sem("zero"), [sem(f"stored{s}") for s in range(2)]


def attention_prompt(nc, top, g, counts, psum, qT, kT, vtok, att, ident, scratch, prefetch):
    with ExitStack() as ctx:
        sb = lambda n, *s: ctx.enter_context(nc.sbuf_tensor(f"{n}{g}", [P, *s], F32))
        qz, stage = sb("qz", 2, 2, 2, BL), sb("stage", 2, STG)
        sc, ex, pt = sb("sc", HPG, 2 * BL), sb("ex", HPG, 2 * BL), sb("pt", HPG, 2, BL)
        S = [psum[:, n:n + 2, :].rearrange("p n (h k) -> p (n h) k", h=2) for n in (0, 2)]
        PT = psum[:, 4:6, :].rearrange("p n (h b k) -> p (n h) b k", h=2, b=2)
        O = psum[:, 6, 0:AW]
        (pool_s, score_s, pe_s, vec_s, out_s, act_s), zero, stored = counts
        for each in counts[0]:
            each.first = g * NB

        def turns(eng, unit):
            def run(t, half_t, parity):
                first = half_t if g == 1 else t
                both = {0: not (isinstance(t, int) and t == 0), 1: parity == 1, 2: False}[g]
                unit(t, first, both, parity, half_t)

            if g == 0:
                run(0, 0, 0)
                with eng.Fori(0, NB // 2 - 1) as i:
                    run(2 * i + 1, i, 1)
                    run(2 * i + 2, i + 1, 0)
                run(NB - 1, NB // 2 - 1, 1)
            else:
                with eng.Fori(0, NB // 2) as i:
                    run(2 * i, i, 0)
                    run(2 * i + 1, i, 1)

        def turns_ahead(eng, first_part, rest):
            def run(part, t, half_t, parity):
                both = {0: not (isinstance(t, int) and t == 0), 1: parity == 1, 2: False}[g]
                part(t, half_t if g == 1 else t, both, parity, half_t)

            run(first_part, 0, 0, 0)
            if g == 0:
                run(first_part, 1, 0, 1)
                run(rest, 0, 0, 0)
                with eng.Fori(0, NB // 2 - 1) as i:
                    run(first_part, 2 * i + 2, i + 1, 0)
                    run(rest, 2 * i + 1, i, 1)
                    run(first_part, 2 * i + 3, i + 1, 1)
                    run(rest, 2 * i + 2, i + 1, 0)
            else:
                with eng.Fori(0, NB // 2 - 1) as i:
                    run(first_part, 2 * i + 1, i, 1)
                    run(rest, 2 * i, i, 0)
                    run(first_part, 2 * i + 2, i + 1, 0)
                    run(rest, 2 * i + 1, i, 1)
                run(first_part, NB - 1, NB // 2 - 1, 1)
                run(rest, NB - 2, NB // 2 - 1, 0)
            run(rest, NB - 1, NB // 2 - 1, 1)

        with nc.Block() as block:
            @block.gpsimd
            def _(pool):
                if g == 0:
                    pool_s.begin(pool)
                pool.wait_ge(zero, g + 1)

                def unit(t, f, both, s, k):
                    score_s.wait(pool, "scores", t - 2)
                    for h in range(2):
                        rows = slice(h * HD, (h + 1) * HD)
                        src = qT[rows, :, 0:SEQ]
                        if g == 0:
                            src = src[:, :, bass.ds(f * BL, BL)]
                            dst = qz[rows, s, :, h, :]
                        elif g == 1:
                            src = src.rearrange("p a (i r) -> p a r i", r=STEP[1])[:, :, bass.ds(f, 1), (BL if both else 0):(2 * BL if both else BL)].rearrange("p a o i -> p a (o i)")
                            dst = qz[rows, s, :, h, :]
                        else:
                            src = src.rearrange("p a (i r) -> p a r i", r=STEP[2])[:, :, bass.ds(f, 1), :].rearrange("p a o i -> p a (o i)")
                            dst = qz[rows, s, :, h, :]
                        pool_s.done(f"q{h}", nc.gpsimd.tensor_copy(dst, src))
                turns(pool, unit)

            @block.tensor
            def _(pe):
                if g == 0:
                    pe_s.begin(pe)
                if g == 0:
                    score_s.begin(pe)

                def scores(t, f, both, s, k):
                    nk = 2 * BL if both else BL
                    pool_s.wait(pe, "q1", t)
                    vec_s.wait(pe, "mask", t - 2)
                    for h in range(HPG):
                        if g == 0:
                            keys = dilated(kT[:, h // 2, 0:SEQ], 0, f - 1 if both else f, nk)
                        elif g == 1:
                            keys = dilated(kT[:, h // 2, 0:SEQ], 1, f, nk, 0)
                        else:
                            keys = dilated(kT[:, h // 2, 0:SEQ], 2, f, nk)
                        last = nc.tensor.matmul(S[s][:, h, 0:nk], qz[:, s, h // 2, h % 2, :], keys, start=True, stop=True)
                    score_s.done("scores", last)

                def rest(t, f, both, s, k):
                    nk = 2 * BL if both else BL
                    act_s.wait(pe, "e3", t)
                    act_s.wait(pe, "pt", t - 1)
                    for h in range(HPG):
                        for b in range(nk // BL):
                            last = nc.tensor.transpose(PT[:, h, b, :], ex[:, h, b * BL:(b + 1) * BL], ident)
                    pe_s.done("pt", last)
                    act_s.wait(pe, "pt", t)
                    out_s.wait(pe, "o", t - 1)
                    for h in range(HPG):
                        for b in range(nk // BL):
                            blk = (t - 1 + b) if both else t
                            v = vtok[:, bass.ds(blk, 1), h * HD:(h + 1) * HD].rearrange("p o c -> p (o c)")
                            last = nc.tensor.matmul(O[:, h * HD:(h + 1) * HD], pt[:, h, b, :], v, start=b == 0, stop=b == nk // BL - 1)
                    pe_s.done("pv", last)
                turns_ahead(pe, scores, rest)

            @block.vector
            def _(vec):
                if g == 0:
                    vec_s.begin(vec)
                if g == 0:
                    out_s.begin(vec)
                nc.vector.memset(qz[:, :, :, :, :], 0.0).then_inc(zero, 1)

                def maxima(t, f, both, s, k):
                    nk = 2 * BL if both else BL
                    m = att("pairs") if g == 2 else att("band")[:, 2 * BL - nk:]
                    score_s.wait(vec, "scores", t)
                    act_s.wait(vec, "e3", t - 1)
                    vec_s.done("mask", nc.vector.tensor_tensor(sc[:, :, 0:nk], S[s][:, :, 0:nk], m[:, None, :].to_broadcast([P, HPG, nk]), ALU.add))
                    vec_s.wait(vec, "mask", t)
                    vec.wait_ge(stored[s], (k + g * (NB // 2)) * 16)
                    vec_s.done("max", nc.vector.tensor_reduce(stage[:, s, AW:AW + HPG], sc[:, :, 0:nk], AXX, ALU.max, negate=True))

                def values(t, f, both, s, k):
                    pe_s.wait(vec, "pv", t)
                    out_s.done("o", nc.vector.tensor_copy(stage[:, s, 0:AW], O))
                turns_ahead(vec, maxima, values)

            @block.scalar
            def _(act):
                if g == 0:
                    act_s.begin(act)
                for dst, src, loaded in prefetch:
                    act.dma_start(dst, src).then_inc(loaded, 16)

                def unit(t, f, both, s, k):
                    nk = 2 * BL if both else BL
                    vec_s.wait(act, "max", t)
                    pe_s.wait(act, "pt", t - 1)
                    for h in range(HPG):
                        act_s.done(f"e{h}", nc.scalar.activation(ex[:, h, 0:nk], sc[:, h, 0:nk], ACT.Exp, bias=stage[:, s, AW + h:AW + h + 1], accum_out=stage[:, s, AW + HPG + h:AW + HPG + h + 1]))
                    pe_s.wait(act, "pt", t)
                    act_s.done("pt", nc.scalar.activation(pt[:, :, 0:nk // BL, :], PT[:, :, 0:nk // BL, :], ACT.Copy))
                turns(act, unit)

            @block.sync
            def _(sp):
                rows = scratch.rearrange("(i r) c -> r i c", r=STEP[g])

                def unit(t, f, both, s, k):
                    out_s.wait(sp, "o", t)
                    act_s.wait(sp, "e3", t)
                    if g == 0:
                        dst = scratch[bass.ds(f * BL, BL), g * STG:(g + 1) * STG]
                    elif g == 1:
                        dst = rows[bass.ds(f, 1), (BL if both else 0):(2 * BL if both else BL), g * STG:(g + 1) * STG].rearrange("o i c -> (o i) c")
                    else:
                        dst = rows[bass.ds(f, 1), :, g * STG:(g + 1) * STG].rearrange("o i c -> (o i) c")
                    sp.dma_start(dst, stage[:, s, :]).then_inc(stored[s], 16)
                turns(sp, unit)
                for s in range(2):
                    sp.wait_ge(stored[s], 16 * (NB // 2) * (g + 1))


def sample_scores(nc, top, g, psum, qT, kT, att, K, k_in, scores):
    tt = 1 if g == 0 else DS
    with ExitStack() as ctx:
        Q = ctx.enter_context(nc.sbuf_tensor(f"sq{g}", [P, 2, NS, 32], F32))
        sem = lambda n: top.enter_context(nc.semaphore(f"samp_{n}{g}"))
        k_new, q_up, full, done = (sem(n) for n in ("k_new", "q_up", "full", "done"))
        with nc.Block() as block:
            @block.gpsimd
            def _(pool):
                for hp in range(2):
                    src = kT[:, hp, SEQ:T].rearrange("p (b t) -> p b t", b=DB)[:, :, None, :].to_broadcast([P, DB, tt, DS])
                    nc.gpsimd.tensor_copy(K[:, hp, :, :, NCACHE:SK], src).then_inc(k_new, 1)

            @block.vector
            def _(vec):
                place = att("place").rearrange("p (a t c) -> p a t c", a=2, t=NS)
                for hp in range(2):
                    nc.vector.tensor_tensor(Q[:, hp, :, :], qT[:, hp, SEQ:T][:, :, None].to_broadcast([P, NS, 32]), place[:, hp, :, :], ALU.mult).then_inc(q_up, 1)
                vec.wait_ge(full, 1)
                nc.vector.tensor_tensor(scores[:, g, :], psum[:, 0, 0:SK], att("fresh")[:, g * SK:(g + 1) * SK], ALU.add).then_inc(done, 1)

            @block.tensor
            def _(pe):
                pe.wait_ge(k_in, 32 * g + 32)
                pe.wait_ge(k_new, 2)
                pe.wait_ge(q_up, 2)
                for b in range(DB):
                    for t in range(DS):
                        for hp in range(2):
                            last = nc.tensor.matmul(psum[32 * (b // 2):32 * (b // 2) + 32, 0, 0:SK], Q[:, hp, DS * b + t, :], K[:, hp, b, t % tt, :],
                                                    start=b % 2 == 0 and t == 0 and hp == 0, stop=b % 2 == 1 and t == DS - 1 and hp == 1)
                last.then_inc(full, 1)


def sample_attention(nc, top, ctx, psum, att, ident, scores, vnew, V, v_in, v2_in, attn):
    sb = lambda n, s: ctx.enter_context(nc.sbuf_tensor(n, s, F32))
    stat = sb("sa_stat", [P, 4])
    pn = sb("sa_new", [P, GROUPS, DB, DS])
    pct = sb("sa_pct", [P, GROUPS, P])
    pnt = sb("sa_pnt", [NS, GROUPS, P])
    sem = lambda n: top.enter_context(nc.semaphore(f"sa_{n}"))
    chain, exped, turned, copied, summed, placed = (sem(n) for n in ("chain", "exped", "turned", "copied", "summed", "placed"))
    flat = scores[:, :, :].rearrange("p g k -> p (g k)")
    def vector(vec):
        nc.vector.tensor_reduce(stat[:, 0:1], flat, AXX, ALU.max, negate=True).then_inc(chain, 1)
        vec.wait_ge(exped, 1)
        nc.vector.reciprocal(stat[:, 2:3], stat[:, 1:2]).then_inc(chain, 1)
        vec.wait_ge(chain, 2)
        nc.vector.tensor_scalar(flat, flat, stat[:, 2:3], None, ALU.mult).then_inc(chain, 1)
        vec.wait_ge(chain, 3)
        for g in range(GROUPS):
            nc.vector.tensor_tensor(pn[:, g, :, :], scores[:, g, NCACHE:SK][:, None, :].to_broadcast([P, DB, DS]), att("own8")[:, :, None].to_broadcast([P, DB, DS]), ALU.mult).then_inc(chain, 1)
        vec.wait_ge(turned, 1)
        nc.vector.tensor_copy(pct[:, :, :], psum[:, 0, 0:GROUPS * P].rearrange("p (g r) -> p g r", g=GROUPS)).then_inc(copied, 1)
        nc.vector.tensor_copy(pnt[:, :, :], psum[0:NS, 1, 0:GROUPS * P].rearrange("p (g r) -> p g r", g=GROUPS)).then_inc(copied, 1)

    def scalar(act):
        act.wait_ge(chain, 1)
        nc.scalar.activation(flat, flat, ACT.Exp, bias=stat[:, 0:1], accum_out=stat[:, 1:2]).then_inc(exped, 1)

    def placing(act):
        act.wait_ge(summed, 1)
        for hp in range(2):
            for h in range(2):
                rows = slice(h * HD, (h + 1) * HD)
                src = psum[rows, 2 + hp, 0:P].rearrange("p (n h) -> p h n", h=HPG)[:, 2 * hp + h, :]
                nc.scalar.activation(attn[rows, hp, SEQ:T], src, ACT.Copy).then_inc(placed, 1)

    def tensor(pe):
        pe.wait_ge(chain, 6)
        for g in range(GROUPS):
            nc.tensor.transpose(psum[:, 0, g * P:(g + 1) * P], scores[:, g, 0:NCACHE], ident)
            last = nc.tensor.transpose(psum[0:NS, 1, g * P:(g + 1) * P], pn[:, g, :, :], ident)
        last.then_inc(turned, 1)
        pe.wait_ge(copied, 2)
        pe.wait_ge(v_in, 32)
        for hp in range(2):
            for g in range(GROUPS):
                nc.tensor.matmul(psum[:, 2 + hp, 0:P], vnew[:, g, hp * P:(hp + 1) * P], pnt[:, g, :], start=g == 0, stop=False)
            for b in range(DB):
                rows = psum[:, 2 + hp, 16 * b:16 * b + 16].rearrange("p (t h) -> p t h", h=HPG)[:, :, 2 * hp:2 * hp + 2]
                probs = pct[:, 0, 16 * b:16 * b + 16].rearrange("p (t h) -> p t h", h=HPG)[:, :, 2 * hp:2 * hp + 2]
                nc.tensor.matmul(rows, V[0][:, b, 0, hp * P:(hp + 1) * P], probs, start=False, stop=False)
        single(pe, 1)

    def single(pe, g):
        for hp in range(2):
            for b in range(DB):
                for t in range(DS):
                    r0 = HPG * (DS * b + t) + 2 * hp
                    last = nc.tensor.matmul(psum[:, 2 + hp, r0:r0 + 2], V[g][:, b, t, hp * P:(hp + 1) * P], pct[:, g, r0:r0 + 2],
                                            start=False, stop=b == DB - 1 and g == 2 and t == DS - 1)
        return last

    def last_group(pe):
        pe.wait_ge(v2_in, 16)
        single(pe, 2).then_inc(summed, 1)

    return vector, scalar, placing, tensor, last_group


def attention_ends(nc, top, psum, ident, scratch, attn, prefetch, samples):
    with ExitStack() as ctx:
        sb = lambda n, *s: ctx.enter_context(nc.sbuf_tensor(n, [P, NB, *s], F32))
        rows = sb("cg_rows", GROUPS, STG)
        w, wd, nmin, den = sb("cg_w", GROUPS, HPG), sb("cg_wd", GROUPS, HPG), sb("cg_min", HPG), sb("cg_den", HPG)
        sem = lambda n: top.enter_context(nc.semaphore(f"cg_{n}"))
        loaded, chain, exped, summed, turned, placed = (sem(n) for n in ("loaded", "chain", "exped", "summed", "turned", "placed"))
        sample_vector, sample_scalar, sample_placing, sample_tensor, sample_last = samples(ctx)
        with nc.Block() as block:
            @block.sync
            def _(sp):
                sp.dma_start(rows[:, :, :, :].rearrange("p n g c -> p n (g c)"), scratch.rearrange("(n p) c -> p n c", p=P)).then_inc(loaded, 16)
                for dst, src, sem_in in prefetch:
                    sp.dma_start(dst, src).then_inc(sem_in, 16)

            @block.vector
            def _(vec):
                sample_vector(vec)
                nm, dn = rows[:, :, :, AW:AW + HPG], rows[:, :, :, AW + HPG:STG]
                vec.wait_ge(loaded, 16)
                nc.vector.tensor_tensor(nmin[:, :, :], nm[:, :, 0, :], nm[:, :, 1, :], ALU.min).then_inc(chain, 1)
                vec.wait_ge(chain, 1)
                nc.vector.tensor_tensor(nmin[:, :, :], nmin[:, :, :], nm[:, :, 2, :], ALU.min).then_inc(chain, 1)
                vec.wait_ge(chain, 2)
                nc.vector.tensor_tensor(w[:, :, :, :], nmin[:, :, None, :].to_broadcast([P, NB, GROUPS, HPG]), nm, ALU.subtract).then_inc(chain, 1)
                vec.wait_ge(exped, 1)
                nc.vector.tensor_tensor(wd[:, :, :, :], w[:, :, :, :], dn, ALU.mult).then_inc(chain, 1)
                vec.wait_ge(chain, 4)
                nc.vector.tensor_reduce(den[:, :, :], wd[:, :, :, :].rearrange("p n g h -> p n h g"), AXX, ALU.add).then_inc(chain, 1)
                vec.wait_ge(chain, 5)
                nc.vector.reciprocal(den[:, :, :], den[:, :, :]).then_inc(chain, 1)
                vec.wait_ge(chain, 6)
                nc.vector.tensor_tensor(w[:, :, :, :], w[:, :, :, :], den[:, :, None, :].to_broadcast([P, NB, GROUPS, HPG]), ALU.mult).then_inc(chain, 1)
                vec.wait_ge(chain, 7)
                for n in range(NB):
                    vals = rows[:, n, :, 0:AW].rearrange("p g (h e) -> p g h e", h=HPG)
                    nc.vector.tensor_tensor(vals, vals, w[:, n, :, :][:, :, :, None].to_broadcast([P, GROUPS, HPG, HD]), ALU.mult).then_inc(chain, 1)
                    vec.wait_ge(chain, 8 + 2 * n)
                    nc.vector.tensor_tensor(rows[:, n, 0, 0:AW], rows[:, n, 0, 0:AW], rows[:, n, 1, 0:AW], ALU.add).then_inc(chain, 1)
                    vec.wait_ge(chain, 9 + 2 * n)
                    nc.vector.tensor_tensor(rows[:, n, 0, 0:AW], rows[:, n, 0, 0:AW], rows[:, n, 2, 0:AW], ALU.add).then_inc(summed, 1)

            @block.scalar
            def _(act):
                sample_scalar(act)
                act.wait_ge(chain, 3)
                nc.scalar.activation(w[:, :, :, :], w[:, :, :, :], ACT.Exp).then_inc(exped, 1)
                for n in range(NB):
                    act.wait_ge(turned, n + 1)
                    nc.scalar.activation(attn[:, :, n * BL:(n + 1) * BL], psum[:, 4 + n % 2, 0:2 * BL].rearrange("p (a t) -> p a t", a=2), ACT.Copy).then_inc(placed, 1)
                sample_placing(act)

            @block.tensor
            def _(pe):
                sample_tensor(pe)
                for n in range(NB):
                    pe.wait_ge(summed, n + 1)
                    if n >= 2:
                        pe.wait_ge(placed, n - 1)
                    for hp in range(2):
                        last = nc.tensor.transpose(psum[:, 4 + n % 2, hp * BL:(hp + 1) * BL], rows[:, n, 0, hp * P:(hp + 1) * P], ident)
                    last.then_inc(turned, 1)
                sample_last(pe)




def rwkv_lora_inputs(nc, top, hT, w_lora, shift0, vec_sb, mu1, cst, psum, low, shift_sb):
    with ExitStack() as ctx:
        sb = lambda n, s: ctx.enter_context(nc.sbuf_tensor(n, s, F32))
        w = sb("lora_w", [P, KT, 2 * P])
        raw = sb("lora_raw", [P, 2, 1 + T])
        part = sb("lora_part", [P, 2, T])
        sem = lambda n: top.enter_context(nc.semaphore(n))
        loaded, full, evac, lerp, kept, zero, done = (sem(f"lora_{n}") for n in ("loaded", "full", "evac", "lerp", "kept", "zero", "done"))
        with nc.Block() as block:
            @block.sync
            def _(sp):
                sp.dma_start(w[:, :, :], w_lora).then_inc(loaded, 16)

            @block.tensor
            def _(pe):
                pe.wait_ge(loaded, 16)
                for i in range(2):
                    product(nc, psum[:, 3 * i:3 * i + 3, :], w[:, :, i * P:(i + 1) * P], hT, KT).then_inc(full, 1)

            @block.scalar
            def _(act):
                for i in range(2):
                    acc = psum[:, 3 * i:3 * i + 3, 0:TT]
                    act.wait_ge(full, i + 1)
                    nc.scalar.activation(thirds(raw[:, i, 1:1 + T]), acc, ACT.Copy).then_inc(evac, 1)
                    nc.scalar.activation(thirds(part[:, i, :]), acc, ACT.Copy, scale=mu1[:, 24 + i:25 + i]).then_inc(evac, 1)
                act.wait_ge(lerp, 2)
                nc.scalar.activation(low[0:HD, 0, :], low[0:HD, 0, :], ACT.Tanh).then_inc(done, 1)
                act.wait_ge(lerp, 4)
                nc.scalar.activation(low[:, 1, :], low[:, 1, :], ACT.Sigmoid).then_inc(done, 1)

            @block.gpsimd
            def _(pool):
                for i in range(2):
                    pool.wait_ge(evac, 2 * i + 1)
                    nc.gpsimd.tensor_copy(shift_sb[:, 24 + i, 0:1], raw[:, i, SEQ:SEQ + 1]).then_inc(kept, 1)
                    nc.gpsimd.tensor_copy(shift_sb[:, 24 + i, 1:9], raw[:, i, SEQ + DS:1 + T:DS]).then_inc(kept, 1)

            @block.vector
            def _(vec):
                nc.vector.memset(raw[:, :, 0:1], 0.0).then_inc(zero, 1)
                vec.wait_ge(zero, 1)
                for i in range(2):
                    mu = vec_sb[:, VEC["shift_mu"] + 24 + i:VEC["shift_mu"] + 25 + i]
                    vec.wait_ge(evac, 2 * i + 2)
                    nc.vector.scalar_tensor_tensor(low[:, i, :], raw[:, i, 0:T], mu, part[:, i, :], ALU.mult, ALU.add).then_inc(lerp, 1)
                    vec.wait_ge(lerp, 2 * i + 1)
                    nc.vector.scalar_tensor_tensor(low[:, i, SEQ:T:DS], shift0[:, 24 + i, :], mu, part[:, i, SEQ:T:DS], ALU.mult, ALU.add).then_inc(lerp, 1)


def rwkv_pairs(nc, top, hT, w_pair, shift0, s0T, vec_sb, mu1, ka1, cst, psum, low, shift_sb, out, wkv_p, wkv_s):
    with ExitStack() as ctx:
        sb = lambda n, *s: ctx.enter_context(nc.sbuf_tensor(n, [P, *s], F32))
        w3, lora_w, gate_w = sb("rkv_w", KT, 3 * P), sb("lora2_w", P), sb("gate_w", P)
        raws = [sb(f"raw_{z}", 1 + T) for z in "rkv"]
        bonus, rinv, norm, centred, bias = sb("bonus", T), sb("rinv", T), sb("norm", T), sb("centred", T), sb("bias", 2)
        zr, zk, zv, sg, cs, pp, pr, av, kkn = (sb(n, T) for n in ("zr", "zk", "zv", "sg", "cs", "pp", "pr", "av", "kkn"))
        mixed = (zr, zk, zv)
        H0, second = [sb("H0", QC, P), sb("H1", QC, P)], centred[:, 0:2 * QC * P].rearrange("p (h c t) -> p h c t", h=2, c=QC)
        H = [[m[:, :, :] for m in H0], [second[:, h, :, :] for h in range(2)]]
        BK = sb("BK", QC, 3, C)
        KB = sb("KB", QC, 2, C)
        LT = sb("LT", QC, P)
        RB = sb("RB", QC, 2, C)
        Gs, Gd, X, XT, XTd = sb("Gs", QC, C), sb("Gd", QC, P), sb("X", QC, C), sb("XT", QC, C), sb("XTd", QC, P)
        SU = sb("SU", QC, 2, 2, C)
        SV, UV = SU[:, :, 0, :, :], SU[:, :, 1, :, :]
        rhs, PC = sb("rhs", QC, C), sb("PC", 2, QC)
        Vs, SP = rhs, Gs[:, 0, :]
        SVs, UVx, Rx = sb("SVs", 2, DB, HD), sb("UVx", 2, DB, HD), sb("Rx", DB, HD)
        ident, ident2 = cst("ident"), cst("ident2")
        ones2, gram, gram_s, reset = cst("ones2"), cst("gram"), cst("gram_s"), cst("reset")
        level = cst("level").rearrange("p (l c) -> p l c", l=LEVELS)
        tok8 = cst("tok8")
        half = (slice(0, HD), slice(HD, P))
        accA, accB = psum[:, 0:3, :], psum[:, 3:6, :]
        bank = lambda i: psum[:, i, :]
        G = [bank(0).rearrange("p (c t) -> p c t", c=QC), bank(1).rearrange("p (c t) -> p c t", c=QC)]
        TK = bank(2).rearrange("p (c h t) -> p c h t", c=QC, h=2)
        VT = bank(3)[:, QT:2 * QT].rearrange("p (c t) -> p c t", c=QC)
        Y = bank(3)[:, 0:QT].rearrange("p (c t) -> p c t", c=QC)
        inv = [m.rearrange("p (c t) -> p c t", c=QC) for m in (bank(4)[:, 0:QT], bank(4)[:, QT:2 * QT], bank(5)[:, 0:QT])]
        side = lambda i: bank(6 + i % 2)[:, 0:TT]
        ahead = [bank(6)[:, 0:TQ], bank(7)[:, 0:TQ], bank(6)[:, 0:TQ]]
        RH, UU, SS = inv

        def steps(name, names, ahead=1):
            return Steps(top.enter_context(nc.semaphore(name)), names, ahead)

        zero = top.enter_context(nc.semaphore("rwkv_zero"))
        w3_in, lw_in, gw_in = (top.enter_context(nc.semaphore(n)) for n in ("rkv_w_in", "lora2_w_in", "gate_w_in"))
        s0_in = top.enter_context(nc.semaphore("s0_in"))
        sp_out, ss_out = (top.enter_context(nc.semaphore(f"wkv_{n}_out")) for n in ("prompt", "sample"))
        pe_n = steps("pe_next", ["r", "k", "v"])
        act_n = steps("act_next", ["r", "k", "v"])
        tri = lambda n: [f"{n}{i}" for i in range(NT)]
        pe_p = steps("pe_pair", [*tri("decay"), *tri("aaa"), *tri("ksum")])
        act_p = steps("act_pair", ["bias_w", "bias_a", "part_k", "part_r", *tri("sig_w"), "part_v", *tri("sig_a"), "ksq", "t1", "ln", "rn", "pp", "pr", "pi"])
        vec_p = steps("vec_pair", ["lerp_k", "cum", "before", *tri("nmax"), "lerp_r", "lerp_v", "s_zero0", "s_zero1", "kkn", "bb", "kmod"])
        pool_p = steps("pool_pair", [f"{m}_{z}" for z in "krv" for m in ("keep", "keep8", "first")])
        inv_pe = lambda levels: ["G0", "tk"] + [m if m == "vt" else f"{m}{i}" for i in range(1, levels) for m in (("G", "vt", "W", "WT") if i == 1 else ("G", "W", "WT")) if not (m == "W" and i == levels - 1)]
        inv_vec = lambda levels: ["g0", "x0", "xa0", "xa1", "xt0"] + [f"{m}{i}" for i in range(1, levels) for m in ("g", "x", "xt") if not (m == "x" and i == levels - 1)]
        inv_act = lambda levels, v: ["xd0_0", "xd1_0", "kb"] + [f"{m}_{i}" for i in range(1, 2) for m in ("gd0", "gd1", "xd0", "xd1")] + v + [f"{m}_{i}" for i in range(2, levels) for m in ("gd0", "gd1", "xd0", "xd1")]
        pe_g = steps("pe_gram", ["gram0", "gram1"])
        vec_h = steps("vec_first", ["r0", "r1", "a0", "a1", "pc", "l0", "l1", "m0", "m1"])
        pe_q = steps("pe_quad", [*inv_pe(LEVELS), *[f"{m}{c}" for c in range(QC) for m in ("rhs", "u", "s", "y")]])
        vec_q = steps("vec_quad", ["rb0", "rb1",
                                   *inv_vec(LEVELS),
                                   *[f"{m}{c}" for c in range(QC) for m in ("rhs", "u0", "s0", "s1")]], ahead=2)
        act_q = steps("act_quad", ["vs", *inv_act(LEVELS, ["v0", "v1"]),
                                   *[f"{m}{c}" for c in range(QC) for m in ("sp0", "sp1", "u1_")], "y"], ahead=2)
        pool_q = steps("pool_quad", ["b", "k"])
        pe_s = steps("pe_samp", ["gram0", "gram1", *inv_pe(SLEVELS), "rhs", "u", "s", "y"])
        vec_s = steps("vec_samp", ["r0", "r1", "a0", "a1", "l0", "l1", "m0", "m1", "rb0", "rb1",
                                   *inv_vec(SLEVELS),
                                   "sel", "rhs", "u0", "ux0", "ux1", "s0", "s1", "dec"])
        act_s = steps("act_samp", ["vs", *inv_act(SLEVELS, ["sv0", "sv1", "v0", "v1"]),
                                   "u1", "y"])
        pool_s = steps("pool_samp", ["b", "k"])
        pe_o = steps("pe_post", [*tri("bonus"), "mean", "var", "gate"])
        vec_o = steps("vec_post", ["rkk", *tri("bon"), "yc", "yn", "yb", "out"])
        act_o = steps("act_post", ["sq", "ln", "rs"])
        all_steps = {"pe": [pe_n, pe_g, pe_p, pe_q, pe_s, pe_o], "act": [act_n, act_p, act_q, act_s, act_o], "vec": [vec_p, vec_h, vec_q, vec_s, vec_o], "pool": [pool_p, pool_q, pool_s]}

        def col(name, j):
            return vec_sb[:, bass.ds(VEC[name] + j, 1)]

        def quad_cols(tile, q):
            return tile[:, bass.ds(q * QT, QT)].rearrange("p (c t) -> p c t", c=QC)

        def cols(n):
            return slice(n * TT, (n + 1) * TT)

        with nc.Block() as block:
            @block.sync
            def _(sp):
                def rkv(j):
                    sp.dma_start(w3[:, :, :].rearrange("p k c -> p (k c)"), w_pair[bass.ds(j, 1), :, 0:3 * KT * P].rearrange("o p c -> p (o c)")).then_inc(w3_in, 16)

                def lora(j):
                    sp.dma_start(lora_w[:, :], w_pair[bass.ds(j, 1), :, 3 * KT * P:3 * KT * P + P].rearrange("o p c -> p (o c)")).then_inc(lw_in, 16)

                def pair(j):
                    pe_o.wait(sp, "gate", j - 1)
                    sp.dma_start(gate_w[:, :], w_pair[bass.ds(j, 1), :, 3 * KT * P + P:WPAIR].rearrange("o p c -> p (o c)")).then_inc(gw_in, 16)
                    vec_s.wait(sp, "s1", j - 1)
                    pe_s.wait(sp, "y", j - 1)
                    for h in range(2):
                        sp.dma_start(SVs[half[h], h, :, :], s0T[bass.ds(j, 1), half[h], :, :].rearrange("o p b v -> p (o b) v")).then_inc(s0_in, 16)
                    if not isinstance(j, int) or j < PAIRS - 1:
                        pe_p.wait(sp, "aaa2", j)
                        lora(j + 1)
                    if not isinstance(j, int):
                        pe_n.wait(sp, "v", (j + 1) * QUADS + (QUADS - 1))
                        rkv(j + 2)
                    vec_q.wait(sp, f"s1{QC - 1}", j * QUADS + (QUADS - 1))
                    for h in range(2):
                        sp.dma_start(wkv_p[bass.ds(j, 1), half[h], :].rearrange("o p v -> p (o v)"), SV[half[h], 0, h, :]).then_inc(sp_out, 16)
                    vec_s.wait(sp, "dec", j)
                    sp.dma_start(wkv_s[bass.ds(j, 1), :, :, :].rearrange("o p b v -> p (o b) v"), Rx[:, :, :]).then_inc(ss_out, 16)

                rkv(0)
                lora(0)
                pe_n.wait(sp, "v", QUADS - 1)
                rkv(1)
                with sp.Fori(0, PAIRS - 2) as j:
                    pair(j)
                for j in (PAIRS - 2, PAIRS - 1):
                    pair(j)
                sp.wait_ge(sp_out, 32 * PAIRS)
                sp.wait_ge(ss_out, 16 * PAIRS)

            @block.gpsimd
            def _(pool):
                for s in all_steps["pool"]:
                    s.begin(pool)

                def ahead_of(j):
                    for n, z in ((1, "k"), (0, "r"), (2, "v")):
                        raw = raws[n]
                        act_n.wait(pool, "v", j * QUADS + (QUADS - 1))
                        pool_p.done(f"keep_{z}", nc.gpsimd.tensor_copy(shift_sb[:, bass.ds(j + n * KT, 1), 0:1].rearrange("p a b -> p (a b)"), raw[:, SEQ:SEQ + 1]))
                        pool_p.done(f"keep8_{z}", nc.gpsimd.tensor_copy(shift_sb[:, bass.ds(j + n * KT, 1), 1:9].rearrange("p a b -> p (a b)"), raw[:, SEQ + DS:1 + T:DS]))
                        act_p.wait(pool, f"part_{z}", j)
                        pool_p.wait(pool, f"keep8_{z}", j)
                        pool_p.done(f"first_{z}", nc.gpsimd.tensor_copy(raw[:, SEQ:T:DS], shift0[:, bass.ds(j + n * KT, 1), :].rearrange("p a b -> p (a b)")))

                def pair(j, more):
                    with pool.Fori(0, QUADS) as q:
                        n = j * QUADS + q
                        act_p.wait(pool, "pi", j)
                        vec_p.wait(pool, "kmod", j)
                        pe_q.wait(pool, "tk", n - 1)
                        pe_s.wait(pool, "tk", j - 1)
                        pool_q.done("b", nc.gpsimd.tensor_tensor(BK[:, :, 0:3:2, :], quad_cols(av, q)[:, :, None, :].to_broadcast([P, QC, 2, C]), quad_cols(cs, q)[:, :, None, :].to_broadcast([P, QC, 2, C]), ALU.mult))
                        pool_q.done("k", nc.gpsimd.tensor_tensor(BK[:, :, 1, :], quad_cols(zk, q), quad_cols(cs, q), ALU.mult))
                    tail = slice(SEQ, T)
                    pe_q.wait(pool, "tk", j * QUADS + (QUADS - 1))
                    pool_s.done("b", nc.gpsimd.tensor_tensor(BK[:, 0, 0:3:2, 0:NS], av[:, None, tail].to_broadcast([P, 2, NS]), cs[:, None, tail].to_broadcast([P, 2, NS]), ALU.mult))
                    pool_s.done("k", nc.gpsimd.tensor_tensor(BK[:, 0, 1, 0:NS], zk[:, tail], cs[:, tail], ALU.mult))

                    if more:
                        ahead_of(j + 1)

                ahead_of(0)
                with pool.Fori(0, PAIRS - 1) as j:
                    pair(j, True)
                pair(PAIRS - 1, False)

            @block.scalar
            def _(act):
                for s in all_steps["act"]:
                    s.begin(act)
                def evacuate(i, m, q):
                    pe_n.wait(act, "rkv"[i], m)
                    act_n.done("rkv"[i], nc.scalar.activation(raws[i][:, bass.ds(q * TQ + 1, TQ)], ahead[i], ACT.Copy))

                with act.Fori(0, QUADS) as q:
                    for i in range(3):
                        evacuate(i, q, q)

                def ahead_of(j):
                    def part(n, z):
                        act_p.done(f"part_{z}", nc.scalar.activation(mixed[n][:, :], raws[n][:, 1:1 + T], ACT.Copy, scale=mu1[:, bass.ds(j + n * KT, 1)]))

                    act_n.wait(act, "v", j * QUADS + (QUADS - 1))
                    pool_s.wait(act, "k", j - 1)
                    vec_s.wait(act, "a1", j - 1)
                    act_p.wait(act, "sig_a2", j - 1)
                    act_p.done("bias_w", nc.scalar.activation(bias[:, 0:1], col("decay_w0", j), ACT.Copy))
                    act_p.done("bias_a", nc.scalar.activation(bias[:, 1:2], col("aaa_a0", j), ACT.Copy))
                    part(1, "k")
                    part(0, "r")
                    act_p.wait(act, "bias_a", j)
                    pe_o.wait(act, "bonus2", j - 1)
                    for n in range(NT):
                        pe_p.wait(act, f"decay{n}", j)
                        act_p.done(f"sig_w{n}", nc.scalar.activation(sg[:, cols(n)], side(1 + n), ACT.Sigmoid, bias=bias[:, 0:1]))
                    yield
                    vec_o.wait(act, "bon2", j - 1)
                    part(2, "v")
                    for n in range(NT):
                        pe_p.wait(act, f"aaa{n}", j)
                        act_p.done(f"sig_a{n}", nc.scalar.activation(av[:, cols(n)], side(n), ACT.Sigmoid, bias=bias[:, 1:2]))
                    vec_p.wait(act, "lerp_k", j)
                    vec_p.wait(act, "kkn", j - 1)
                    act_p.done("ksq", nc.scalar.activation(norm[:, :], zk[:, :], ACT.Square, scale=col("k_k", j)))
                    yield
                    vec_p.wait(act, "before", j)
                    act_p.wait(act, "sig_a2", j)
                    act_p.done("t1", nc.scalar.activation(sg[:, :], av[:, :], ACT.Identity, scale=col("k_a", j), bias=ka1[:, bass.ds(j, 1)]))
                    vec_p.wait(act, "nmax2", j)
                    act_p.done("ln", nc.scalar.activation(norm[:, :], norm[:, :], ACT.Ln))
                    act_p.wait(act, "ln", j)
                    act_p.done("rn", nc.scalar.activation(norm[:, :], norm[:, :], ACT.Exp, scale=-0.5))
                    act_p.done("pp", nc.scalar.activation(pp[:, :], pp[:, :], ACT.Exp, scale=-DECAY))
                    yield
                    vec_s.wait(act, "dec", j - 1)
                    act_p.done("pr", nc.scalar.activation(pr[:, :], cs[:, :], ACT.Exp, scale=-DECAY))
                    act_p.wait(act, "pr", j)
                    act_p.done("pi", nc.scalar.activation(cs[:, :], cs[:, :], ACT.Exp, scale=DECAY))
                    yield

                def pair(j, more):
                    piece = ahead_of(j + 1) if more else iter(())

                    def keys(st, pe_t, n, c):
                        pe_t.wait(act, "tk", n)
                        st.done("kb", nc.scalar.activation(KB[:, c, :, :], TK[:, c, :, :], ACT.Copy))

                    def values(st, pe_t, n, c, samples):
                        pe_t.wait(act, "vt", n)
                        if samples:
                            for h in range(2):
                                o = half[1 - h]
                                st.done(f"sv{h}", nc.scalar.activation(SVs[o, h, :, :], VT[o, 0, :][:, None, :].to_broadcast([HD, DB, HD]), ACT.Copy))
                            for h in range(2):
                                st.done(f"v{h}", nc.scalar.activation(UV[half[1 - h], 0, h, :], VT[half[1 - h], 0, :], ACT.Copy))
                        else:
                            for h in range(2):
                                o = half[1 - h]
                                st.done(f"v{h}", nc.scalar.activation(SU[o, :, :, h, :], VT[o, :, None, :].to_broadcast([HD, QC, 2, HD]), ACT.Copy))

                    def diagonals(st, pe_t, vec_t, n, c, levels, samples, fill=lambda: None):
                        for i in range(levels):
                            if i:
                                vec_t.wait(act, f"g{i}", n)
                                for h in range(2):
                                    st.done(f"gd{h}_{i}", nc.scalar.activation(Gd[half[h], c, h * C:(h + 1) * C], Gs[half[h], c, :], ACT.Copy))
                            vec_t.wait(act, f"xt{i}", n)
                            for h in range(2):
                                st.done(f"xd{h}_{i}", nc.scalar.activation(XTd[half[h], c, h * C:(h + 1) * C], XT[half[h], c, :], ACT.Copy))
                            if i == 0:
                                keys(st, pe_t, n, c)
                                fill()
                            if i == 1:
                                values(st, pe_t, n, c, samples)

                    with act.Fori(0, QUADS // 2) as i:
                        for s in range(2):
                            q = 2 * i + s
                            n = j * QUADS + q
                            vec_p.wait(act, "lerp_v", j)
                            pe_q.wait(act, f"y{QC - 1}", n - 1)
                            pe_s.wait(act, "y", j - 1)
                            act_q.done("vs", nc.scalar.activation(Vs[:, :, :], quad_cols(zv, q), ACT.Copy))
                            pe_q.wait(act, f"y{QC - 1}", n - 1)
                            pe_s.wait(act, "y", j - 1)
                            diagonals(act_q, pe_q, vec_q, n, slice(0, QC), LEVELS, False)
                            if more:
                                evacuate(0, (j + 1) * QUADS + q, q)
                            for c in range(QC):
                                if c:
                                    vec_q.wait(act, f"s1{c - 1}", n)
                                else:
                                    vec_q.wait(act, f"s1{QC - 1}", n - 1)
                                    vec_p.wait(act, "s_zero1", j)
                                    vec_h.wait(act, "pc", n)
                                for h in range(2):
                                    act_q.done(f"sp{h}{c}", nc.scalar.activation(SP[half[h], :], SV[half[h], c, h, :], ACT.Copy, scale=PC[half[h], s, c:c + 1]))
                                pe_q.wait(act, f"u{c}", n)
                                act_q.done(f"u1_{c}", nc.scalar.activation(UV[HD:P, c, 1, :], UU[HD:P, c, :], ACT.Copy))
                                if more and c == 1:
                                    evacuate(1, (j + 1) * QUADS + q, q)
                            pe_q.wait(act, f"y{QC - 1}", n)
                            act_q.done("y", nc.scalar.activation(quad_cols(kkn, q), Y[:, :, :], ACT.Copy))
                            if more:
                                evacuate(2, (j + 1) * QUADS + q, q)
                    nq = j * QUADS + (QUADS - 1)
                    pe_q.wait(act, f"y{QC - 1}", nq)
                    act_s.done("vs", nc.scalar.activation(Vs[:, 0, 0:NS], zv[:, SEQ:T], ACT.Copy))
                    pe_q.wait(act, f"y{QC - 1}", nq)
                    next(piece, None)
                    diagonals(act_s, pe_s, vec_s, j, 0, SLEVELS, True, lambda: next(piece, None))
                    next(piece, None)
                    pe_s.wait(act, "u", j)
                    act_s.done("u1", nc.scalar.activation(UV[HD:P, 0, 1, :], UU[HD:P, 0, :], ACT.Copy))
                    pe_s.wait(act, "y", j)
                    act_s.done("y", nc.scalar.activation(kkn[:, SEQ:T], Y[:, 0, 0:NS], ACT.Copy))
                    next(piece, None)
                    vec_o.wait(act, "yc", j)
                    act_o.done("sq", nc.scalar.activation(rinv[:, :], centred[:, :], ACT.Square))
                    pe_o.wait(act, "var", j)
                    act_o.done("ln", nc.scalar.activation(thirds(rinv[:, :]), accA[:, :, 0:TT], ACT.Ln, scale=1.0 / HD, bias=cst("lnx_eps")))
                    act_o.wait(act, "ln", j)
                    act_o.done("rs", nc.scalar.activation(rinv[:, :], rinv[:, :], ACT.Exp, scale=-0.5))

                for _ in ahead_of(0):
                    pass
                with act.Fori(0, PAIRS - 1) as j:
                    pair(j, True)
                pair(PAIRS - 1, False)

            @block.vector
            def _(vec):
                for s in all_steps["vec"]:
                    s.begin(vec)
                for z in (RB[HD:P, :, 0, :], RB[0:HD, :, 1, :], LT[:, :, :], Gd[:, :, :], XTd[:, :, :], *[raw[:, 0:1] for raw in raws]):
                    nc.vector.memset(z, 0.0).then_inc(zero, 1)
                vec.wait_ge(zero, 8)

                def mask_lower(st, gram_t, n, c, m, bc):
                    for h in range(2):
                        gram_t.wait(vec, f"gram{h}", n)
                        st.done(f"l{h}", nc.vector.tensor_tensor(LT[half[h], c, h * C:(h + 1) * C], G[h][half[h], c, 0:C], bc(m[half[h], 0:C]), ALU.mult))

                def mask_mixed(st, Hs, c, m, bc):
                    for h in range(2):
                        o = half[1 - h]
                        st.done(f"m{h}", nc.vector.tensor_tensor(Hs[h][o, c, :], G[h][o, c, :], bc(m[o, :]), ALU.mult))

                def mask_rb(st, c, m, bc):
                    for h in range(2):
                        st.done(f"rb{h}", nc.vector.tensor_tensor(RB[half[h], c, h, :], G[h][half[h], c, C:P], bc(m[half[h], C:P]), ALU.mult))

                def doubling(st, pe_t, act_t, n, c, levels, bc, fill=lambda: None):
                    pe_t.wait(vec, "G0", n)
                    st.done("g0", nc.vector.tensor_tensor(Gs[:, c, :], inv[0][:, c, :], bc(level[:, 0, :]), ALU.mult))
                    st.wait(vec, "g0", n)
                    st.done("x0", nc.vector.tensor_tensor(X[:, c, :], Gs[:, c, :], bc(ident2), ALU.add))
                    for h in range(2):
                        st.done(f"xa{h}", nc.vector.tensor_tensor(XT[half[h], c, :], G[h][half[h], c, 0:C], bc(cst("level0_t")[half[h], :]), ALU.mult))
                    st.wait(vec, "xa1", n)
                    st.done("xt0", nc.vector.tensor_tensor(XT[:, c, :], XT[:, c, :], bc(ident2), ALU.add))
                    fill()
                    for i in range(1, levels):
                        pe_t.wait(vec, f"G{i}", n)
                        st.done(f"g{i}", nc.vector.tensor_tensor(Gs[:, c, :], inv[0][:, c, :], bc(level[:, i, :]), ALU.mult))
                        if i < levels - 1:
                            pe_t.wait(vec, f"W{i}", n)
                            st.done(f"x{i}", nc.vector.tensor_tensor(X[:, c, :], inv[1][:, c, :], X[:, c, :], ALU.add))
                        pe_t.wait(vec, f"WT{i}", n)
                        st.done(f"xt{i}", nc.vector.tensor_tensor(XT[:, c, :], inv[2][:, c, :], XT[:, c, :], ALU.add))
                        if i < levels - 1:
                            fill()

                def ahead_of(j):
                    def lerp(n, z):
                        act_p.wait(vec, f"part_{z}", j)
                        pool_p.wait(vec, f"first_{z}", j)
                        mu = vec_sb[:, bass.ds(VEC["shift_mu"] + j + n * KT, 1)]
                        vec_p.done(f"lerp_{z}", nc.vector.scalar_tensor_tensor(mixed[n][:, :], raws[n][:, 0:T], mu, mixed[n][:, :], ALU.mult, ALU.add))

                    lerp(1, "k")
                    yield
                    act_p.wait(vec, "sig_w2", j)
                    pool_s.wait(vec, "k", j - 1)
                    vec_p.done("cum", nc.vector.tensor_tensor_scan(cs[:, :], reset, sg[:, :], 0.0, ALU.mult, ALU.add))
                    vec_p.wait(vec, "cum", j)
                    vec_p.done("before", nc.vector.tensor_tensor(pp[:, :], cs[:, :], sg[:, :], ALU.subtract))
                    for n in range(NT):
                        pe_p.wait(vec, f"ksum{n}", j)
                        vec_p.done(f"nmax{n}", nc.vector.tensor_scalar(norm[:, cols(n)], side(1 + n), 1e-24, None, ALU.max))
                    yield
                    lerp(0, "r")
                    yield
                    lerp(2, "v")
                    vec.wait_ge(sp_out, 32 * j)
                    pe_q.wait(vec, f"y{QC - 1}", j * QUADS - 1)
                    for h in range(2):
                        vec_p.done(f"s_zero{h}", nc.vector.memset(SV[half[h], 0, h, :], 0.0))
                    yield
                    vec_o.wait(vec, "yc", j - 1)
                    act_p.wait(vec, "rn", j)
                    vec_p.done("kkn", nc.vector.scalar_tensor_tensor(kkn[:, :], zk[:, :], col("k_k", j), norm[:, :], ALU.mult, ALU.mult))
                    act_p.wait(vec, "t1", j)
                    vec_p.wait(vec, "kkn", j)
                    vec_p.done("bb", nc.vector.tensor_tensor(av[:, :], kkn[:, :], av[:, :], ALU.mult))
                    vec_p.done("kmod", nc.vector.tensor_tensor(zk[:, :], zk[:, :], sg[:, :], ALU.mult))
                    yield

                def pair(j, more):
                    piece = ahead_of(j + 1) if more else iter(())
                    over = lambda m: m[:, None, :].to_broadcast([m.shape[0], QC, m.shape[1]])
                    every = slice(0, QC)

                    def operands(q):
                        n, s = j * QUADS + q, q % 2
                        for h in range(2):
                            vec_h.done(f"r{h}", nc.vector.tensor_tensor(H[s][h][half[h], :, C:P], quad_cols(zr[half[h], :], q), quad_cols(pr[half[h], :], q), ALU.mult))
                            yield
                        for h in range(2):
                            vec_h.done(f"a{h}", nc.vector.scalar_tensor_tensor(H[s][h][half[h], :, 0:C], quad_cols(kkn[half[h], :], q), -1.0, quad_cols(pp[half[h], :], q), ALU.mult, ALU.mult))
                            yield
                        act_q.wait(vec, f"sp1{QC - 1}", n - 2)
                        vec_q.wait(vec, f"s1{QC - 1}", n - 2)
                        vec_h.done("pc", nc.vector.tensor_copy(PC[:, s, :], quad_cols(pr, q)[:, :, C - 1]))
                        yield

                    act_p.wait(vec, "pi", j)
                    pe_s.wait(vec, "y", j - 1)
                    vec_o.wait(vec, "yn", j - 1)
                    vec_s.wait(vec, "xt1", j - 1)
                    for _ in operands(0):
                        pass
                    mask_lower(vec_h, pe_g, j * QUADS, every, gram, over)
                    mask_mixed(vec_h, H[0], every, gram, over)
                    for q in range(QUADS):
                        n = j * QUADS + q
                        last = q == QUADS - 1
                        ahead_quad = iter(()) if last else operands(q + 1)
                        pe_q.wait(vec, f"y{QC - 1}", n - 1)
                        vec_q.wait(vec, f"s1{QC - 1}", n - 1)
                        mask_rb(vec_q, every, gram, over)

                        def two():
                            next(ahead_quad, None)
                            next(ahead_quad, None)

                        doubling(vec_q, pe_q, act_q, n, every, LEVELS, over, two)
                        for _ in ahead_quad:
                            pass
                        for c in range(QC):
                            pe_q.wait(vec, f"rhs{c}", n)
                            vec_q.done(f"rhs{c}", nc.vector.tensor_copy(rhs[:, c, :], RH[:, c, :]))
                            pe_q.wait(vec, f"u{c}", n)
                            vec_q.done(f"u0{c}", nc.vector.tensor_copy(UV[0:HD, c, 0, :], UU[0:HD, c, :]))
                            pe_q.wait(vec, f"s{c}", n)
                            act_q.wait(vec, f"sp1{c}", n)
                            for h in range(2):
                                vec_q.done(f"s{h}{c}", nc.vector.scalar_tensor_tensor(SV[half[h], (c + 1) % QC, h, :], SS[half[h], c, :], PC[half[h], q % 2, c:c + 1], SP[half[h], :], ALU.mult, ALU.add))
                            if not last and c == 1:
                                mask_lower(vec_h, pe_g, n + 1, every, gram, over)
                            if not last and c == 2:
                                mask_mixed(vec_h, H[(q + 1) % 2], every, gram, over)

                    vec_p.wait(vec, "kmod", j)
                    vec_o.done("rkk", nc.vector.scalar_tensor_tensor(sg[:, :], zr[:, :], col("r_k", j), zk[:, :], ALU.mult, ALU.mult))
                    tail = slice(SEQ, T)
                    pe_q.wait(vec, f"y{QC - 1}", j * QUADS + (QUADS - 1))
                    for h in range(2):
                        vec_s.done(f"r{h}", nc.vector.tensor_tensor(H[0][h][half[h], 0, C:C + NS], zr[half[h], tail], pr[half[h], tail], ALU.mult))
                    for h in range(2):
                        vec_s.done(f"a{h}", nc.vector.scalar_tensor_tensor(H[0][h][half[h], 0, 0:NS], kkn[half[h], tail], -1.0, pp[half[h], tail], ALU.mult, ALU.mult))
                    one = lambda m: m
                    for n in range(NT):
                        pe_o.wait(vec, f"bonus{n}", j)
                        vec_o.done(f"bon{n}", nc.vector.tensor_tensor(bonus[:, cols(n)], side(n), zv[:, cols(n)], ALU.mult))
                    mask_lower(vec_s, pe_s, j, 0, gram_s, one)
                    mask_mixed(vec_s, H[0], 0, gram_s, one)
                    mask_rb(vec_s, 0, gram_s, one)
                    doubling(vec_s, pe_s, act_s, j, 0, SLEVELS, one, lambda: next(piece, None))
                    next(piece, None)
                    pe_s.wait(vec, "rhs", j)
                    vec.wait_ge(ss_out, 16 * j)
                    big = psum[:, 0, :].rearrange("p (b v) -> p b v", b=DB)
                    vec_s.done("sel", nc.vector.tensor_tensor(Rx[:, :, :], big, tok8[:, :, None].to_broadcast([P, DB, HD]), ALU.mult))
                    vec_s.wait(vec, "sel", j)
                    vec_s.done("rhs", nc.vector.tensor_reduce(rhs[:, 0, :], Rx[:, :, :].rearrange("p b v -> p v b"), AXX, ALU.add))
                    next(piece, None)
                    pe_s.wait(vec, "u", j)
                    vec_s.done("u0", nc.vector.tensor_copy(UV[0:HD, 0, 0, :], UU[0:HD, 0, :]))
                    vec_s.wait(vec, "u0", j)
                    act_s.wait(vec, "u1", j)
                    for h in range(2):
                        vec_s.done(f"ux{h}", nc.vector.tensor_tensor(UVx[:, h, :, :], UV[:, 0, h, :][:, None, :].to_broadcast([P, DB, HD]), tok8[:, :, None].to_broadcast([P, DB, HD]), ALU.mult))
                    pe_s.wait(vec, "s", j)
                    big1 = psum[:, 1, :].rearrange("p (b v) -> p b v", b=DB)
                    for h in range(2):
                        vec_s.done(f"s{h}", nc.vector.tensor_tensor(Rx[half[h], :, :], big1[half[h], :, :], SVs[half[h], h, :, :], ALU.add))
                    vec_s.wait(vec, "s1", j)
                    vec_s.done("dec", nc.vector.tensor_tensor(Rx[:, :, :], Rx[:, :, :], pr[:, SEQ + DS - 1:T:DS][:, :, None].to_broadcast([P, DB, HD]), ALU.mult))

                    next(piece, None)
                    pe_o.wait(vec, "mean", j)
                    vec_o.done("yc", nc.vector.scalar_tensor_tensor(thirds(centred[:, :]), accA[:, :, 0:TT], -1.0 / HD, thirds(kkn[:, :]), ALU.mult, ALU.add))
                    next(piece, None)
                    act_o.wait(vec, "rs", j)
                    vec_o.done("yn", nc.vector.scalar_tensor_tensor(rinv[:, :], centred[:, :], col("lnx_w", j), rinv[:, :], ALU.mult, ALU.mult))
                    vec_o.wait(vec, "yn", j)
                    vec_o.done("yb", nc.vector.scalar_tensor_tensor(bonus[:, :], rinv[:, :], col("lnx_b", j), bonus[:, :], ALU.add, ALU.add))
                    vec_o.wait(vec, "yb", j)
                    pe_o.wait(vec, "gate", j)
                    vec_o.done("out", nc.vector.tensor_tensor(out[:, bass.ds(j, 1), :].rearrange("p o (n c) -> p (o n) c", n=NT), accB[:, :, 0:TT], thirds(bonus[:, :]), ALU.mult))

                for _ in ahead_of(0):
                    pass
                with vec.Fori(0, PAIRS - 1) as j:
                    pair(j, True)
                pair(PAIRS - 1, False)

            @block.tensor
            def _(pe):
                for s in all_steps["pe"]:
                    s.begin(pe)
                pe.wait_ge(zero, 8)

                def next_pair(m, q):
                    for z in range(3):
                        act_n.wait(pe, "vkr"[z], m - 1 if z < 2 else m)
                        for k in range(KT):
                            mm = nc.tensor.matmul(ahead[z], w3[:, k, z * P:(z + 1) * P], hT[:, k, bass.ds(q * TQ, TQ)], start=k == 0, stop=k == KT - 1)
                            if k == KT - 1:
                                pe_n.done("rkv"[z], mm)
                            yield

                def grams(st, n, chunks, Hs, vec_t, pool_t):
                    vec_t.wait(pe, "a1", n)
                    pool_t.wait(pe, "k", n)
                    for h in range(2):
                        for c in chunks:
                            last = nc.tensor.matmul(G[h][:, c, :], BK[half[h], c, h:h + 2, :], Hs[h][half[h], c, :], start=True, stop=True)
                            if c == chunks[-1]:
                                st.done(f"gram{h}", last)
                            yield

                def token_major(st, n, chunks, act_t):
                    for c in chunks:
                        for h in range(2):
                            last = nc.tensor.matmul(TK[:, c, h, :], BK[:, c, h:h + 2, :], ident[:, half[h]], start=True, stop=True)
                    st.done("tk", last)
                    yield
                    act_t.wait(pe, "vs", n)
                    for c in chunks:
                        for h in range(2):
                            last = nc.tensor.matmul(VT[half[1 - h], c, :], Vs[:, c, :], ident[:, half[h]], start=True, stop=True)
                    st.done("vt", last)
                    yield

                def inverse(st, n, chunks, vec_t, act_t, levels, fill, lower, after_first=lambda: None):
                    lower.wait(pe, "l1", n)
                    turned = token_major(st, n, chunks, act_t)
                    for i in range(levels):
                        if i:
                            vec_t.wait(pe, f"x{i - 1}", n)
                        for c in chunks:
                            last = nc.tensor.matmul(inv[0][:, c, :], LT[:, c, :], X[:, c, :] if i else ident2, start=True, stop=True)
                        st.done(f"G{i}", last)
                        if i < 2:
                            next(turned)
                        if i == 0:
                            after_first()
                            fill(FILL["G0"])
                            continue
                        fill(FILL["G1"] if i == 1 else FILL["G"])
                        vec_t.wait(pe, f"g{i}", n)
                        act_t.wait(pe, f"xd1_{i - 1}", n)
                        if i < levels - 1:
                            for c in chunks:
                                last = nc.tensor.matmul(inv[1][:, c, :], XTd[:, c, :], Gs[:, c, :], start=True, stop=True)
                            st.done(f"W{i}", last)
                        act_t.wait(pe, f"gd1_{i}", n)
                        for c in chunks:
                            last = nc.tensor.matmul(inv[2][:, c, :], Gd[:, c, :], XT[:, c, :], start=True, stop=True)
                        st.done(f"WT{i}", last)

                pe.wait_ge(w3_in, 16)
                with pe.Fori(0, QUADS) as q:
                    for _ in next_pair(q, q):
                        pass

                def ahead_of(j):
                    pe.wait_ge(lw_in, 16 * j + 16)
                    for n in range(NT):
                        if n < 2:
                            vec_o.wait(pe, f"bon{1 + n}", j - 1)
                            act_n.wait(pe, "v", j * QUADS + (QUADS - 1))
                        else:
                            act_p.wait(pe, "sig_w0", j)
                        pe_p.done(f"decay{n}", nc.tensor.matmul(side(1 + n), lora_w[half[0], :], low[half[0], 0, cols(n)], start=True, stop=True))
                    yield
                    for n, last in enumerate(("sig_w1", "sig_w2", "sig_a0")):
                        act_p.wait(pe, last, j)
                        pe_p.done(f"aaa{n}", nc.tensor.matmul(side(n), lora_w[half[1], :], low[half[1], 0, cols(n)], start=True, stop=True))
                    yield
                    act_p.wait(pe, "ksq", j)
                    for n, (t, last) in enumerate(((act_p, "sig_a1"), (act_p, "sig_a2"), (vec_p, "nmax0"))):
                        t.wait(pe, last, j)
                        pe_p.done(f"ksum{n}", nc.tensor.matmul(side(1 + n), ones2, norm[:, cols(n)], start=True, stop=True))
                    yield

                def pair(j, more):
                    piece = ahead_of(j + 1) if more else iter(())
                    if more:
                        pe.wait_ge(w3_in, 16 * j + 32)
                    vec_p.wait(pe, "nmax2", j)
                    vec_o.wait(pe, "out", j - 1)
                    for _ in grams(pe_g, j * QUADS, range(QC), H[0], vec_h, pool_q):
                        pass
                    for q in range(QUADS):
                        n, Hs = j * QUADS + q, H[q % 2]
                        product_ahead = next_pair((j + 1) * QUADS + q, q) if more else iter(())
                        next_grams = grams(pe_g, n + 1, range(QC), H[(q + 1) % 2], vec_h, pool_q) if q < QUADS - 1 else iter(())

                        def fill(count):
                            for _ in range(count):
                                next(product_ahead, None)

                        inverse(pe_q, n, range(QC), vec_q, act_q, LEVELS, fill, vec_h)
                        fill(FILL["inverse"])
                        act_q.wait(pe, "v1", n)
                        vec_h.wait(pe, "m1", n)
                        act_q.wait(pe, "y", n - 1)
                        for c in range(QC):
                            if c:
                                vec_q.wait(pe, f"s1{c - 1}", n)
                            elif q:
                                vec_q.wait(pe, f"s1{QC - 1}", n - 1)
                            else:
                                vec_p.wait(pe, "s_zero1", j)
                            for h in range(2):
                                mm = nc.tensor.matmul(RH[half[h], c, :], Hs[h][:, c, 0:C], SV[:, c, h, :], start=True, stop=True)
                            pe_q.done(f"rhs{c}", mm)
                            for _ in range(GRAM_AT[2 * c]):
                                next(next_grams, None)
                            fill(FILL["rhs"][c])
                            if c == 0:
                                act_q.wait(pe, f"xd1_{LEVELS - 1}", n)
                            vec_q.wait(pe, f"rhs{c}", n)
                            pe_q.done(f"u{c}", nc.tensor.matmul(UU[:, c, :], XTd[:, c, :], rhs[:, c, :], start=True, stop=True))
                            for _ in range(GRAM_AT[2 * c + 1]):
                                next(next_grams, None)
                            fill(FILL["u"][c])
                            vec_q.wait(pe, f"u0{c}", n)
                            act_q.wait(pe, f"u1_{c}", n)
                            for h in range(2):
                                mm = nc.tensor.matmul(SS[half[h], c, :], KB[:, c, h, :], UV[:, c, h, :], start=True, stop=True)
                            pe_q.done(f"s{c}", mm)
                            for h in range(2):
                                nc.tensor.matmul(Y[half[h], c, :], SV[:, c, h, :], Hs[h][:, c, C:P], start=True, stop=False)
                                mm = nc.tensor.matmul(Y[half[h], c, :], UV[:, c, h, :], RB[:, c, h, :], start=False, stop=True)
                            pe_q.done(f"y{c}", mm)
                        fill(3 * KT)
                    nq = j * QUADS + (QUADS - 1)
                    act_q.wait(pe, "y", nq)
                    vec_q.wait(pe, f"s1{QC - 1}", nq)
                    nothing = lambda count: None
                    vec_o.wait(pe, "rkk", j)
                    if more:
                        act_n.wait(pe, "v", (j + 1) * QUADS + (QUADS - 1))
                    else:
                        vec_p.wait(pe, "nmax2", j)
                    for n in range(NT):
                        if n == 2:
                            vec_o.wait(pe, "bon0", j)
                        pe_o.done(f"bonus{n}", nc.tensor.matmul(side(n), ones2, sg[:, cols(n)], start=True, stop=True))
                    for _ in grams(pe_s, j, range(1), H[0], vec_s, pool_s):
                        pass
                    next(piece, None)
                    inverse(pe_s, j, range(1), vec_s, act_s, SLEVELS, nothing, vec_s, lambda: next(piece, None))
                    act_s.wait(pe, "v1", j)
                    vec_s.wait(pe, "rb1", j)
                    act_s.wait(pe, f"xd1_{SLEVELS - 1}", j)
                    pe.wait_ge(s0_in, 32 * j + 32)
                    next(piece, None)
                    for h in range(2):
                        mm = nc.tensor.matmul(psum[half[h], 0, :], H[0][h][:, 0, 0:C], SVs[:, h, :, :], start=True, stop=True)
                    pe_s.done("rhs", mm)
                    vec_s.wait(pe, "rhs", j)
                    pe_s.done("u", nc.tensor.matmul(UU[:, 0, :], XTd[:, 0, :], rhs[:, 0, :], start=True, stop=True))
                    vec_s.wait(pe, "ux1", j)
                    for h in range(2):
                        mm = nc.tensor.matmul(psum[half[h], 1, :], KB[:, 0, h, :], UVx[:, h, :, :], start=True, stop=True)
                    pe_s.done("s", mm)
                    for h in range(2):
                        nc.tensor.matmul(Y[half[h], 0, 0:NS], UV[:, 0, h, :], RB[:, 0, h, 0:NS], start=True, stop=False)
                        for b in range(DB):
                            mm = nc.tensor.matmul(Y[half[h], 0, DS * b:DS * b + DS], SVs[:, h, b, :], H[0][h][:, 0, C + DS * b:C + DS * b + DS], start=False, stop=b == DB - 1)
                    pe_s.done("y", mm)

                    act_s.wait(pe, "y", j)
                    vec_s.wait(pe, "s1", j)
                    for n in range(NT):
                        mm = nc.tensor.matmul(accA[:, n, 0:TT], ones2, kkn[:, cols(n)], start=True, stop=True)
                    pe_o.done("mean", mm)
                    act_o.wait(pe, "sq", j)
                    for n in range(NT):
                        mm = nc.tensor.matmul(accA[:, n, 0:TT], ones2, rinv[:, cols(n)], start=True, stop=True)
                    pe_o.done("var", mm)
                    pe.wait_ge(gw_in, 16 * j + 16)
                    for n in range(NT):
                        mm = nc.tensor.matmul(accB[:, n, 0:TT], gate_w[:, :], low[:, 1, cols(n)], start=True, stop=True)
                    pe_o.done("gate", mm)

                for _ in ahead_of(0):
                    pass
                with pe.Fori(0, PAIRS - 1) as j:
                    pair(j, True)
                pair(PAIRS - 1, False)




def split_high(nc, raw, parts, s):
    return nc.scalar.activation(parts[0][:, s, :], raw[:, s, 0:KT * P], ACT.Copy)


def split_low(nc, raw, parts, s):
    return nc.gpsimd.tensor_tensor(parts[1][:, s, :], raw[:, s, 0:KT * P], parts[0][:, s, :].bitcast(F32), ALU.subtract)


def gated_stage(nc, top, name, w_src, width, tiles, psum, x, out, add, low=None, norm=None):
    nb = len(tiles)
    with ExitStack() as ctx:
        sb = lambda n, *s: ctx.enter_context(nc.sbuf_tensor(f"{name}_{n}", [P, *s], F32))
        w = sb("w", 2, width)
        if norm is not None:
            parts = [ctx.enter_context(nc.sbuf_tensor(f"{name}_w_{n}", [P, 2, KT * P], F32R)) for n in ("high", "low")]
            split_s = Steps(top.enter_context(nc.semaphore(f"{name}_high")), ["high"], ahead=2)
            pool_s = Steps(top.enter_context(nc.semaphore(f"{name}_low")), ["low"], ahead=2)
        gate, prod = sb("gate", 2, T), sb("prod", 2, T)
        total = sb("total", T) if low is not None else None
        acc = [psum[:, 0:3, :], psum[:, 3:6, :]]
        w_in = [top.enter_context(nc.semaphore(f"{name}_w_in{s}")) for s in range(2)]
        pe_s = Steps(top.enter_context(nc.semaphore(f"{name}_pe")), [f"{m}{i}" for i in range(nb) for m in ("gate", "branch")], ahead=2)
        act_s = Steps(top.enter_context(nc.semaphore(f"{name}_act")), [f"gate{i}" for i in range(nb)] + (["high"] if low is not None else []), ahead=2)
        vec_s = Steps(top.enter_context(nc.semaphore(f"{name}_vec")), [f"mul{i}" for i in range(nb)] + [f"add{i}" for i in range(nb - 1 + add)] + (["low"] if low is not None else []), ahead=2)

        def turns(eng, turn):
            with eng.Fori(0, KT // 2) as i:
                for s in range(2):
                    turn(2 * i + s, s, i)

        with nc.Block() as block:
            @block.sync
            def _(sp):
                def turn(t, s, i):
                    pe_s.wait(sp, f"branch{nb - 1}", t - 2)
                    sp.dma_start(w[:, s, :], w_src[bass.ds(t, 1), :, :].rearrange("o p c -> p (o c)")).then_inc(w_in[s], 16)
                turns(sp, turn)

            @block.tensor
            def _(pe):
                pe_s.begin(pe)
                if norm is not None:
                    norm.tensor(pe)

                def turn(t, s, i):
                    if norm is not None:
                        pool_s.wait(pe, "low", t)
                    pe.wait_ge(w_in[s], 16 * i + 16)
                    at = 0
                    for b, (gk, gx, bk, bx) in enumerate(tiles):
                        for m, kt, src in (("gate", gk, gx), ("branch", bk, bx)):
                            if m == "gate":
                                act_s.wait(pe, f"gate{(b - 1) % nb}", t if b else t - 1)
                            else:
                                vec_s.wait(pe, f"mul{(b - 1) % nb}", t if b else t - 1)
                            wt = w[:, s, at:at + kt * P].rearrange("p (k c) -> p k c", k=kt)
                            at += kt * P
                            if norm is not None and m == "gate":
                                w2 = [p[:, s, :].rearrange("p (k c) -> p k c", k=KT) for p in parts]
                                pe_s.done(f"{m}{b}", split_product(nc, acc[0], w2, src, kt, lambda k: norm.ready(pe, k)))
                                continue
                            pe_s.done(f"{m}{b}", product(nc, acc[m == "branch"], wt, src, kt))
                turns(pe, turn)

            @block.scalar
            def _(act):
                act_s.begin(act)
                if norm is not None:
                    split_s.begin(act)
                    norm.scalar(act)

                def weights(t, s, i):
                    act.wait_ge(w_in[s], 16 * i + 16)
                    pe_s.wait(act, "gate0", t - 2)
                    split_s.done("high", split_high(nc, w, parts, s))

                def turn(t, s, i):
                    if norm is not None and s == 0:
                        weights(t, 0, i)
                        if isinstance(t, int):
                            norm.scalar_high(act)
                        weights(t + 1, 1, i)
                    for b in range(nb):
                        pe_s.wait(act, f"gate{b}", t)
                        vec_s.wait(act, f"mul{b}", t - 1 if nb == 2 else t - 2)
                        act_s.done(f"gate{b}", nc.scalar.activation(thirds(gate[:, b if nb == 2 else s, :]), acc[0][:, :, 0:TT], ACT.Sigmoid))
                    if low is not None:
                        vec_s.wait(act, "add0", t)
                        act_s.done("high", nc.scalar.activation(out[:, bass.ds(t, 1), :].rearrange("p o c -> p (o c)"), total[:, :], ACT.Copy))
                if norm is None:
                    turns(act, turn)
                else:
                    turn(0, 0, 0)
                    turn(1, 1, 0)
                    with act.Fori(1, KT // 2) as i:
                        for s in range(2):
                            turn(2 * i + s, s, i)

            if norm is not None:
                @block.gpsimd
                def _(pool):
                    pool_s.begin(pool)

                    def turn(t, s, i):
                        split_s.wait(pool, "high", t)
                        pool_s.done("low", split_low(nc, w, parts, s))
                    turns(pool, turn)

            @block.vector
            def _(vec):
                vec_s.begin(vec)
                if norm is not None:
                    norm.vector(vec)

                def turn(t, s, i):
                    for b in range(nb):
                        act_s.wait(vec, f"gate{b}", t)
                        pe_s.wait(vec, f"branch{b}", t)
                        vec_s.wait(vec, vec_s.names[-1], t - 1)
                        vec_s.done(f"mul{b}", nc.vector.tensor_tensor(thirds(prod[:, b, :]), thirds(gate[:, b if nb == 2 else s, :]), acc[1][:, :, 0:TT], ALU.mult))
                    row = total[:, :] if low is not None else (x if add else out)[:, bass.ds(t, 1), :].rearrange("p o c -> p (o c)")
                    vec_s.wait(vec, f"mul{nb - 1}", t)
                    if add:
                        vec_s.done("add0", nc.vector.tensor_tensor(row, row, prod[:, 0, :], ALU.add))
                    else:
                        vec_s.done("add0", nc.vector.tensor_tensor(row, prod[:, 0, :], prod[:, 1, :], ALU.add))
                    if low is not None:
                        act_s.wait(vec, "high", t)
                        high = out[:, bass.ds(t, 1), :].rearrange("p o c -> p (o c)")
                        vec_s.done("low", nc.vector.tensor_tensor(low[:, bass.ds(t, 1), :].rearrange("p o c -> p (o c)"), row, high.bitcast(F32), ALU.subtract))
                turns(vec, turn)


def residual_projection(nc, top, name, w_src, psum, src, x, x_src):
    with ExitStack() as ctx:
        raw = ctx.enter_context(nc.sbuf_tensor(f"{name}_raw", [P, 2, KT * P], F32))
        parts = [ctx.enter_context(nc.sbuf_tensor(f"{name}_{n}", [P, 2, KT * P], F32R)) for n in ("high", "low")]
        acc = [psum[:, 0:3, :], psum[:, 3:6, :]]
        w_in = [top.enter_context(nc.semaphore(f"{name}_w_in{s}")) for s in range(2)]
        pe_s = Steps(top.enter_context(nc.semaphore(f"{name}_pe")), ["full"], ahead=2)
        act_s = Steps(top.enter_context(nc.semaphore(f"{name}_act")), ["high"], ahead=2)
        pool_s = Steps(top.enter_context(nc.semaphore(f"{name}_pool")), ["low"], ahead=2)
        vec_s = Steps(top.enter_context(nc.semaphore(f"{name}_vec")), ["add"], ahead=2)
        x_in = top.enter_context(nc.semaphore(f"{name}_x_in"))
        with nc.Block() as block:
            @block.sync
            def _(sp):
                with sp.Fori(0, KT // 2) as i:
                    for s in range(2):
                        pool_s.wait(sp, "low", 2 * i + s - 2)
                        sp.dma_start(raw[:, s, :], w_src[bass.ds(2 * i + s, 1), :, :].rearrange("o p c -> p (o c)")).then_inc(w_in[s], 16)

            @block.scalar
            def _(act):
                act_s.begin(act)
                act.wait_ge(w_in[0], 16)
                act.dma_start(x[:, :, :], x_src).then_inc(x_in, 16)
                with act.Fori(0, KT // 2) as i:
                    for s in range(2):
                        act.wait_ge(w_in[s], 16 * i + 16)
                        pe_s.wait(act, "full", 2 * i + s - 2)
                        act_s.done("high", split_high(nc, raw, parts, s))

            @block.gpsimd
            def _(pool):
                pool_s.begin(pool)
                with pool.Fori(0, KT // 2) as i:
                    for s in range(2):
                        act_s.wait(pool, "high", 2 * i + s)
                        pool_s.done("low", split_low(nc, raw, parts, s))

            @block.tensor
            def _(pe):
                pe_s.begin(pe)
                with pe.Fori(0, KT // 2) as i:
                    for s in range(2):
                        pool_s.wait(pe, "low", 2 * i + s)
                        vec_s.wait(pe, "add", 2 * i + s - 2)
                        pe_s.done("full", split_product(nc, acc[s], [m[:, s, :].rearrange("p (k c) -> p k c", k=KT) for m in parts], src, KT))

            @block.vector
            def _(vec):
                vec_s.begin(vec)
                vec.wait_ge(x_in, 16)
                with vec.Fori(0, KT // 2) as i:
                    for s in range(2):
                        t = 2 * i + s
                        pe_s.wait(vec, "full", t)
                        row = x[:, bass.ds(t, 1), :].rearrange("p o (n c) -> p (o n) c", n=NT)
                        vec_s.done("add", nc.vector.tensor_tensor(row, row, acc[s][:, :, 0:TT], ALU.add))


def mlp(nc, top, w_src, psum, h, ff, x, norm):
    with ExitStack() as ctx:
        raw = ctx.enter_context(nc.sbuf_tensor("ff_raw", [P, 2, KT * P], F32))
        parts = [ctx.enter_context(nc.sbuf_tensor(f"ff_w_{n}", [P, 2, KT * P], F32R)) for n in ("high", "low")]
        up = ctx.enter_context(nc.sbuf_tensor("ff_up", [P, 2, T], F32))
        acc = [psum[:, 0:3, :], psum[:, 3:6, :]]
        w_in = [top.enter_context(nc.semaphore(f"ff_w_in{s}")) for s in range(2)]
        ups, downs, chunks = range(FFT), range(KT), range(2 * FFT)
        pe_s = Steps(top.enter_context(nc.semaphore("ff_pe")), [f"up{c}" for c in ups] + [f"down{m}" for m in downs])
        high_s = Steps(top.enter_context(nc.semaphore("ff_w_high_done")), [f"high{c}" for c in chunks])
        pool_s = Steps(top.enter_context(nc.semaphore("ff_w_low_done")), [f"low{c}" for c in chunks])
        act_s = Steps(top.enter_context(nc.semaphore("ff_act")), [f"{n}{c}" for c in ups for n in ("relu", "square", "high")])
        vec_s = Steps(top.enter_context(nc.semaphore("ff_vec")), [f"low{c}" for c in ups] + [f"add{m}" for m in downs])
        used = lambda c: f"up{c}" if c < FFT else f"down{2 * (c - FFT) + 1}"

        def chunk(c, q):
            return (c, q) if c >= 0 else (2 * FFT + c, q - 1)

        with nc.Block() as block:
            @block.sync
            def _(sp):
                with sp.Fori(0, FFQ) as q:
                    for c in chunks:
                        before, turn = chunk(c - 2, q)
                        pool_s.wait(sp, f"low{before}", turn)
                        sp.dma_start(raw[:, c % 2, :], w_src[bass.ds(2 * FFT * q + c, 1), :, :].rearrange("o p c -> p (o c)")).then_inc(w_in[c % 2], 16)

            @block.gpsimd
            def _(pool):
                pool_s.begin(pool)
                with pool.Fori(0, FFQ) as q:
                    for c in chunks:
                        high_s.wait(pool, f"high{c}", q)
                        pool_s.done(f"low{c}", split_low(nc, raw, parts, c % 2))

            @block.tensor
            def _(pe):
                pe_s.begin(pe)
                norm.tensor(pe)
                with pe.Fori(0, FFQ) as q:
                    for c in ups:
                        pool_s.wait(pe, f"low{c}", q)
                        if c < 2:
                            vec_s.wait(pe, f"add{KT - 2 + c}", q - 1)
                        else:
                            act_s.wait(pe, f"relu{c - 2}", q)
                        w = [m[:, c % 2, :].rearrange("p (k c) -> p k c", k=KT) for m in parts]
                        pe_s.done(f"up{c}", split_product(nc, acc[c % 2], w, h, KT, (lambda k: norm.ready(pe, k)) if c == 0 else (lambda k: None)))
                    for m in downs:
                        c = FFT + m // 2
                        if m == 0:
                            vec_s.wait(pe, f"low{FFT - 1}", q)
                        if m % 2 == 0:
                            pool_s.wait(pe, f"low{c}", q)
                        if m >= 2:
                            vec_s.wait(pe, f"add{m - 2}", q)
                        else:
                            act_s.wait(pe, f"relu{FFT - 2 + m}", q)
                        w = [p[:, c % 2, :].rearrange("p (o k c) -> p o k c", o=2, k=FFT)[:, m % 2] for p in parts]
                        pe_s.done(f"down{m}", split_product(nc, acc[m % 2], w, ff, FFT))

            @block.scalar
            def _(act):
                act_s.begin(act)
                high_s.begin(act)
                norm.scalar(act)

                def eighth(q, first):
                    def weights(c):
                        before, turn = chunk(c - 2, q)
                        act.wait_ge(w_in[c % 2], 16 * FFT * q + (16 * (c // 2) + 16))
                        pe_s.wait(act, used(before), turn)
                        high_s.done(f"high{c}", split_high(nc, raw, parts, c % 2))

                    weights(0)
                    if first:
                        norm.scalar_high(act)
                    for c in ups:
                        weights(c + 1)
                        pe_s.wait(act, f"up{c}", q)
                        vec_s.wait(act, f"low{(c - 2) % FFT}", q if c >= 2 else q - 1)
                        act_s.done(f"relu{c}", nc.scalar.activation(thirds(up[:, c % 2, :]), acc[c % 2][:, :, 0:TT], ACT.Relu))
                        act_s.wait(act, f"relu{c}", q)
                        act_s.done(f"square{c}", nc.scalar.activation(up[:, c % 2, :], up[:, c % 2, :], ACT.Square))
                        act_s.wait(act, f"square{c}", q)
                        act_s.done(f"high{c}", nc.scalar.activation(ff[0][:, c, :], up[:, c % 2, :], ACT.Copy))
                    for c in range(FFT + 1, 2 * FFT):
                        weights(c)

                eighth(0, True)
                with act.Fori(1, FFQ) as q:
                    eighth(q, False)

            @block.vector
            def _(vec):
                vec_s.begin(vec)
                norm.vector(vec)
                with vec.Fori(0, FFQ) as q:
                    for c in ups:
                        act_s.wait(vec, f"high{c}", q)
                        vec_s.done(f"low{c}", nc.vector.tensor_tensor(ff[1][:, c, :], up[:, c % 2, :], ff[0][:, c, :].bitcast(F32), ALU.subtract))
                    for m in downs:
                        pe_s.wait(vec, f"down{m}", q)
                        vec_s.done(f"add{m}", nc.vector.tensor_tensor(thirds(x[:, m, :]), thirds(x[:, m, :]), acc[m % 2][:, :, 0:TT], ALU.add))




def program(nc, ins, outs):
    with ExitStack() as ctx:
        sb = lambda n, s: ctx.enter_context(nc.sbuf_tensor(n, s, F32))
        front = ExitStack()
        sbf = lambda n, s: front.enter_context(nc.sbuf_tensor(n, s, F32))
        vec_sb = sb("vec_sb", [P, NVEC])
        cst_sb = sb("cst_sb", [P, NCST])
        mu1 = sb("mu1", [P, RT])
        ka1 = sb("ka1", [P, KT])
        mixer = sb("rwkv_out", [P, KT, T])

        hT = sbf("hT", [P, KT, T])
        attn = sbf("attn", [P, 2, T])
        psum = ctx.enter_context(nc.psum_tensor("psum", [P, 8, 512], F32))
        scratch = nc.dram_tensor("attention_rows", (SEQ, GROUPS * STG), F32, kind="Internal").ap()
        sem = lambda n: ctx.enter_context(nc.semaphore(n))
        cst = lambda n: cst_sb[:, CST[n][0]:CST[n][1]]
        gain = lambda n: vec_sb[:, VEC[n]:VEC[n] + KT]

        with nc.sbuf_tensor("x_in", [P, KT, T], F32) as x_in:
            tables_in, halves = sem("tables_in"), [sem(f"x_in{i}") for i in range(2)]
            start_loads(nc, [(x_in[:, 0:KT // 2, :], ins["xT"][:, 0:KT // 2, :], halves[0]), (vec_sb[:, :], ins["vecs"], tables_in),
                             (cst_sb[:, :], ins["consts"], tables_in), (x_in[:, KT // 2:KT, :], ins["xT"][:, KT // 2:KT, :], halves[1])])
            rms_norm(nc, "mix", x_in, gain("norm_mix"), cst_sb, hT, psum, ctx, arrive=(halves, tables_in))
        derived = sem("derived")
        with nc.Block() as block:
            @block.vector
            def _(vec):
                nc.vector.tensor_scalar(mu1[:, :], vec_sb[:, VEC["shift_mu"]:VEC["shift_mu"] + RT], -1.0, 1.0, ALU.mult, ALU.add).then_inc(derived, 1)
                nc.vector.tensor_scalar(ka1[:, :], vec_sb[:, VEC["k_a"]:VEC["k_a"] + KT], -1.0, 1.0, ALU.mult, ALU.add).then_inc(derived, 1)

        with ExitStack() as c1:
            sb1 = lambda n, s: c1.enter_context(nc.sbuf_tensor(n, s, F32))
            att_sb = sb1("att_sb", [P, NATT])
            att = lambda n: att_sb[:, ATT[n][0]:ATT[n][1]]
            vnew = sb1("vnew", [NS, GROUPS, AW])
            scores = sb1("sample_scores", [P, GROUPS, SK])
            V = [sb1(f"sample_v{g}", [P, DB, 1 if g == 0 else DS, AW]) for g in range(GROUPS - 1)]
            flat = mixer[:, :, :].rearrange("p k t -> p (k t)")
            V.append(flat[:, 0:DB * DS * AW].rearrange("p (b t c) -> p b t c", b=DB, t=DS))
            K = []
            for g in range(GROUPS):
                tt = 1 if g == 0 else DS
                K.append(flat[:, 0:2 * DB * tt * SK].rearrange("p (a b t k) -> p a b t k", a=2, b=DB, t=tt))
            wa_in, wb_in, k_in, v_in = sem("w_qk_in"), sem("w_kv_in"), sem("sample_k_in"), sem("sample_v_in")
            with ExitStack() as c2:
                sb2 = lambda n, s: c2.enter_context(nc.sbuf_tensor(n, s, F32))
                wa, wb = sb2("w_qk", [P, WQK]), sb2("w_kv", [P, WKV])
                qT, kT, vtok = sb2("qT", [P, 2, T]), sb2("kT", [P, 2, T]), sb2("vtok", [P, NB, AW])
                weights = lambda g: [(wa[:, :], ins["w_qk"][g], wa_in), (wb[:, :], ins["w_kv"][g], wb_in)]
                att_loaded = sem("att_loaded")
                start_loads(nc, weights(0) + [(att_sb[:, :], ins["att_consts"], att_loaded)])
                counts = prompt_counts(nc, ctx)
                for g in range(GROUPS):
                    ahead = [(K[g][:, hp, :, :, 0:NCACHE], ins[f"kc{g}"][:, hp, :, :, :], k_in) for hp in range(2)]
                    if g < GROUPS - 1:
                        ahead += weights(g + 1)
                    values = [(V[g][:, :, :, :], ins[f"vc{g}"], v_in)] if g < GROUPS - 1 else []
                    attention_projection(nc, ctx, g, hT, wa, wb, wa_in, wb_in, att_loaded, psum, qT, kT, vtok, vnew, outs["k_all"][g], outs["v_all"][g], values)
                    attention_prompt(nc, ctx, g, counts, psum, qT, kT, vtok, att, cst("ident"), scratch, ahead)
                    sample_scores(nc, ctx, g, psum, qT, kT, att, K[g], k_in, scores)
            v2_in = sem("sample_v2_in")
            attention_ends(nc, ctx, psum, cst("ident"), scratch, attn, [(V[2], ins["vc2"], v2_in)],
                           lambda c: sample_attention(nc, ctx, c, psum, att, cst("ident"), scores, vnew, V, v_in, v2_in, attn))
            load_all(nc, sem("vnew_stored"), [(outs["v_new"], vnew[:, :, :])])
        with ExitStack() as c2:
            low = c2.enter_context(nc.sbuf_tensor("low", [P, 2, T], F32))
            shift_sb = c2.enter_context(nc.sbuf_tensor("shift_sb", [P, RT, 1 + DB], F32))
            shift0 = c2.enter_context(nc.sbuf_tensor("shift0", [P, RT, DB], F32))
            load_all(nc, sem("shift_loaded"), [(shift0[:, :, :], ins["shift0"])])
            rwkv_lora_inputs(nc, ctx, hT, ins["w_lora"], shift0, vec_sb, mu1, cst, psum, low, shift_sb)
            rwkv_pairs(nc, ctx, hT, ins["w_pair"], shift0, ins["s0T"], vec_sb, mu1, ka1, cst, psum, low, shift_sb, mixer, outs["wkv_p"], outs["wkv_s"])
            load_all(nc, sem("shift_stored"), [(outs["shift"], shift_sb[:, :, :])])

        r2 = lambda c, n, kt: [c.enter_context(nc.sbuf_tensor(f"{n}_{part}", [P, kt, T], F32R)) for part in ("high", "low")]
        with ExitStack() as c3:
            mixed = r2(c3, "mixed", KT)
            gated_stage(nc, ctx, "merge", ins["w_mix"], WMIX, [(KT, hT, KT, mixer), (KT, hT, 2, attn)], psum, None, mixed[0], False, low=mixed[1])
            x = mixer
            residual_projection(nc, ctx, "proj", ins["w_out"], psum, mixed, x, ins["xT"])
        front.close()
        h = r2(ctx, "h", KT)
        norm = lambda c, n: RmsNorm(nc, n, x, gain(f"norm_{n}"), cst_sb, h[0], psum, c, ctx, low=h[1])
        with ExitStack() as c4:
            mlp(nc, ctx, ins["w_ff"], psum, h, r2(c4, "ff", FFT), x, norm(c4, "mlp"))
        with ExitStack() as c5:
            pT = c5.enter_context(nc.sbuf_tensor("pT", [P, 2, T], F32))
            load_all(nc, sem("p_loaded"), [(pT[:, :, :], ins["pT"])])
            gated_stage(nc, ctx, "ple", ins["w_ple"], WPLE, [(KT, h, 2, pT)], psum, x, None, True, norm=norm(c5, "ple"))
        with nc.sbuf_tensor("y", [P, KT, T], F32) as y:
            rms_norm(nc, "final", x, gain("norm_final"), cst_sb, y, psum, ctx, store=outs["yT"])




def _constants(np):
    def two(m):
        return np.concatenate([m, m], 0)

    i, k = np.arange(P), np.arange(C)
    s, t = k[:, None], k[None, :]
    out = {
        "ident": np.eye(P),
        "ident2": two(np.eye(C)),
        "ones": np.ones((P, P)),
        "ones2": (i[:, None] // HD == i[None, :] // HD),
        "gram": two(np.concatenate([s < t, s <= t], 1)),
    }
    same = (s // DS == t // DS) & (s < NS) & (t < NS)
    out["gram_s"] = two(np.concatenate([same & (s < t), same & (s <= t)], 1))
    out["level"] = two(np.concatenate([(s // n % 2 == 1) & (t // n == s // n - 1) for n in (1 << np.arange(LEVELS))], 1))
    out["level0_t"] = two((s % 2 == 0) & (t == s + 1))
    out["eps"], out["lnx_eps"] = np.full((P, 1), EPS), np.full((P, 1), LNX_EPS)
    at = np.arange(T)
    out["reset"] = np.broadcast_to(np.where(at < SEQ, at % C != 0, (at - SEQ) % DS != 0), (P, T))
    q, key = i[:, None], np.arange(2 * BL)[None, :]
    dist = q + BL - key
    out["band"] = np.where((dist >= 0) & (dist <= BL), 0.0, NEG)
    kk = i[None, :]
    out["pairs"] = np.where((q % 2 == kk % 2) & (kk <= q), 0.0, NEG)
    hp, tok, c = np.arange(2)[:, None, None], np.arange(NS)[None, :, None], np.arange(32)[None, None, :]
    want = 16 * (tok // DS % 2) + 4 * (tok % DS) + 2 * hp
    out["place"] = np.stack([(c == want + h) for h in range(2)]).repeat(HD, 0).reshape(P, -1)
    row_t = (i // HPG % DS)[:, None]
    key = np.arange(SK)[None, :]
    new = key - NCACHE
    fresh = [np.where(np.where(new >= 0, new <= row_t, key >= row_t), 0.0, NEG)]
    fresh += [np.where((new < 0) | (new == row_t), 0.0, NEG)] * 2
    out["fresh"] = np.concatenate(fresh, 1)
    out["own8"] = i[:, None] // (HPG * DS) == np.arange(DB)[None, :]
    tk = np.concatenate([k, k])
    out["tok8"] = (tk[:, None] < NS) & (tk[:, None] // DS == np.arange(DB)[None, :])
    return [np.concatenate([np.asarray(out[n], np.float32) for n in names], 1) for names in (CST, ATT)]


def _tiles(np, w, cols):
    kk, m = w.shape
    return np.ascontiguousarray(w.reshape(kk // P, P, m // cols, cols).transpose(2, 1, 0, 3).reshape(m // cols, P, -1))


def _layout(np, a):
    a = {k: np.asarray(v) for k, v in a.items()}
    x = np.concatenate([a["x_prompt"][0], a["x_sample"].reshape(NS, D)], 0)
    p = np.concatenate([a["p_prompt"][0, 0], a["p_sample"][0].reshape(NS, -1)], 0)
    feat = lambda v: v.reshape(-1, P).T
    fm = lambda m: np.ascontiguousarray(m.T.reshape(-1, P, m.shape[0]).transpose(1, 0, 2))
    w_in = a["w_in"][0]
    rw = 3 * D + 256
    q0, k0, v0, g0 = rw, rw + 3 * AW, rw + 6 * AW, rw + 9 * AW
    heads = lambda c: [w_in[:, c + AW * g:c + AW * (g + 1)] for g in range(GROUPS)]
    d = {"xT": fm(x), "pT": fm(p)}
    d["vecs"] = np.concatenate([feat(a[n].reshape(-1)) for n in VEC], 1)
    d["consts"], d["att_consts"] = _constants(np)
    d["shift0"] = np.ascontiguousarray(a["state_shift"][0].T.reshape(RT, P, DB).transpose(1, 0, 2))
    d["w_lora"] = _tiles(np, w_in[:, 3 * D:rw], 256)[0].reshape(P, KT, 256)
    lora = np.concatenate([a["decay_w2"][0], a["aaa_a2"][0]], 0)
    rkv = w_in[:, :3 * D].reshape(KT, P, 3, PAIRS, P).transpose(3, 1, 0, 2, 4).reshape(PAIRS, P, -1)
    d["w_pair"] = np.concatenate([rkv, _tiles(np, lora, P), _tiles(np, a["gate_g2"][0], P)], 2)
    d["s0T"] = np.ascontiguousarray(a["state_wkv"][0].reshape(DB, PAIRS, 2, HD, HD).transpose(1, 2, 4, 0, 3).reshape(PAIRS, P, DB, HD))
    wq, wk, wv = heads(q0), heads(k0), heads(v0)
    d["w_qk"] = np.stack([_tiles(np, np.concatenate([wq[g], wk[g][:, :P]], 1), 3 * P)[0] for g in range(GROUPS)])
    d["w_kv"] = np.stack([np.concatenate([_tiles(np, wk[g][:, P:], P)[0], _tiles(np, wv[g], AW)[0]], 1) for g in range(GROUPS)])
    for g in range(GROUPS):
        cache = a[f"cache_kv_g{g}"][0]
        rows = cache.reshape(DB, NCACHE, DIL[g], 2, HPG, HD)[:, :, :DS]
        d[f"kc{g}"] = np.ascontiguousarray(rows[:, :, :, 0].reshape(DB, NCACHE, -1, 2, P).transpose(4, 3, 0, 2, 1))
        d[f"vc{g}"] = np.ascontiguousarray(rows[:, :, :, 1].reshape(DB, NCACHE, -1, AW).transpose(1, 0, 2, 3))
    g = _tiles(np, w_in[:, g0:], P)
    br = _tiles(np, a["w_branch_rwkv"][0], P)
    ba = _tiles(np, a["w_branch_attn"][0], P)
    d["w_mix"] = np.concatenate([g[:KT], br, g[KT:], ba], 2)
    d["w_out"] = _tiles(np, a["w_out"][0], P)
    w1 = _tiles(np, a["w_ff1"][0], P).reshape(FFQ, FFT, P, -1)
    w2 = np.stack([_tiles(np, w, P) for w in a["w_ff2"][0].reshape(FFQ, FFT * P, D)])
    w2 = w2.reshape(FFQ, FFT, 2, P, -1).transpose(0, 1, 3, 2, 4).reshape(FFQ, FFT, P, -1)
    d["w_ff"] = np.concatenate([w1, w2], 1).reshape(FFQ * 2 * FFT, P, -1)
    d["w_ple"] = np.concatenate([_tiles(np, a["w_ple_gate"][0], P), _tiles(np, a["w_ple"][0], P)], 2)
    return d


_OUT = {"yT": (P, KT, T), "k_all": (GROUPS, P, 2, T), "v_all": (GROUPS, P, NB, AW), "v_new": (NS, GROUPS, AW),
        "wkv_p": (PAIRS, P, HD), "wkv_s": (PAIRS, P, DB, HD), "shift": (P, RT, 1 + DB)}


def _results(np, r):
    y = r["yT"].transpose(2, 1, 0).reshape(T, D)
    kv_p, kv_s = [], []
    for g, keep in enumerate((128, 512, SEQ)):
        k = r["k_all"][g].transpose(2, 1, 0).reshape(T, HPG, HD)
        v = r["v_all"][g].transpose(1, 0, 2)
        if g == 1:
            v = v.reshape(STEP[1], SEQ // STEP[1], AW).transpose(1, 0, 2)
        elif g == 2:
            v = v.transpose(1, 0, 2)
        v = v.reshape(SEQ, HPG, HD)
        kv_p.append(np.stack([k[SEQ - keep:SEQ], v[SEQ - keep:]], 1)[None, None])
        vs = r["v_new"][:, g].reshape(DB, DS, HPG, HD)
        kv_s.append(np.stack([k[SEQ:].reshape(DB, DS, HPG, HD), vs], 2)[None])
    state = lambda w: w.reshape(PAIRS, 2, HD, -1, HD).transpose(3, 0, 1, 4, 2).reshape(-1, 2 * PAIRS, HD, HD)
    sh = r["shift"].transpose(2, 1, 0).reshape(1 + DB, RT * P)
    out = (y[None, :SEQ], y[SEQ:].reshape(DB, DS, D), *kv_p, state(r["wkv_p"][:, :, None, :])[None], sh[None, 0:1],
           *kv_s, state(r["wkv_s"])[None], sh[None, 1:])
    return tuple(np.ascontiguousarray(o) for o in out)


def kernel(**inputs):
    import numpy as np
    import concourse.bacc as bacc
    from concourse.bass_utils import run_bass_kernel_spmd

    nc = bacc.Bacc("TRN2", target_bir_lowering=False, num_devices=1)
    arrays = {f"in_{k}": np.ascontiguousarray(v) for k, v in _layout(np, inputs).items()}
    ins = {k[3:]: nc.dram_tensor(k, v.shape, F32, kind="ExternalInput").ap() for k, v in arrays.items()}
    outs = {k: nc.dram_tensor(f"out_{k}", s, F32, kind="ExternalOutput").ap() for k, s in _OUT.items()}
    program(nc, ins, outs)
    r = run_bass_kernel_spmd(nc, [arrays], core_ids=[0])
    got = r.results[0]
    return _results(np, {k: got[f"out_{k}"] for k in _OUT})
```
